# Optimizing a Trainium2 kernel written in Bass

```python
import math
import jax, jax.numpy as jnp
from jax import lax
import numpy as np

D_MODEL = 1024
BATCH = 1
SEQ = 1024
DEPTH = 1

HEAD_DIM = 64
D_ATTN = D_MODEL // 2
D_RWKV = D_MODEL - D_ATTN
N_Q_HEADS = D_ATTN // HEAD_DIM
N_KV_HEADS = max(1, N_Q_HEADS // 4)
Q_PER_KV = N_Q_HEADS // N_KV_HEADS
D_KV = N_KV_HEADS * HEAD_DIM
WINDOW = 128
BLOCK = 128
N_BUCKETS = 32
MAX_DISTANCE = 128
N_RWKV_HEADS = D_RWKV // HEAD_DIM
LORA_DECAY = 64
LORA_ICLR = 64
LORA_GATE = 128
RWKV_COLS = 3 * D_RWKV + LORA_DECAY + LORA_ICLR + LORA_GATE
RWKV_SPLITS = (D_RWKV, 2 * D_RWKV, 3 * D_RWKV, 3 * D_RWKV + LORA_DECAY, 3 * D_RWKV + LORA_DECAY + LORA_ICLR)
D_IN = D_ATTN + 2 * D_KV + RWKV_COLS
D_FF = 4 * D_MODEL
CONV_WIDTH = 3
NORM_EPS = 1e-6
GN_EPS = 64e-5
NEG_INF = -1e30


def rms_norm(x, g):
    xf = x.astype(jnp.float32)
    y = xf * lax.rsqrt(jnp.mean(xf * xf, axis=-1, keepdims=True) + NORM_EPS) * g.astype(jnp.float32)
    return y.astype(x.dtype)

def t5_bucket(rel):
    n = jnp.maximum(rel, 0)
    max_exact = N_BUCKETS // 2
    large = max_exact + (jnp.log(jnp.maximum(n, 1).astype(jnp.float32) / max_exact)
                         / math.log(MAX_DISTANCE / max_exact) * (N_BUCKETS - max_exact)).astype(jnp.int32)
    large = jnp.minimum(large, N_BUCKETS - 1)
    return jnp.where(n < max_exact, n, large)

def sliding_window_sink_attention(q, k, v, rel_bias, sinks):
    B, S, _ = q.shape
    NB = S // BLOCK
    q = q.reshape(B, NB, BLOCK, N_KV_HEADS, Q_PER_KV, HEAD_DIM)

    def band(t):
        t = t.reshape(B, NB, BLOCK, N_KV_HEADS, HEAD_DIM)
        prev = jnp.concatenate([jnp.zeros_like(t[:, :1]), t[:, :-1]], axis=1)
        return jnp.concatenate([prev, t], axis=2)

    kb, vb = band(k), band(v)
    rel = (jnp.arange(BLOCK)[:, None] + BLOCK) - jnp.arange(2 * BLOCK)[None, :]
    in_window = (rel >= 0) & (rel < WINDOW)
    key_pos = (jnp.arange(NB)[:, None] - 1) * BLOCK + jnp.arange(2 * BLOCK)[None, :]
    mask = in_window[None] & (key_pos >= 0)[:, None, :]
    bias = rel_bias.astype(jnp.float32)[t5_bucket(rel)]
    bias = bias.transpose(2, 0, 1).reshape(N_KV_HEADS, Q_PER_KV, BLOCK, 2 * BLOCK)
    scores = jnp.einsum('bnqhgd,bnkhd->bnhgqk', q, kb).astype(jnp.float32) * (HEAD_DIM ** -0.5) + bias
    scores = jnp.where(mask[None, :, None, None], scores, NEG_INF)
    sink = sinks.astype(jnp.float32).reshape(N_KV_HEADS, Q_PER_KV)[:, :, None, None]
    m = jnp.maximum(scores.max(axis=-1, keepdims=True), sink)
    p = jnp.exp(scores - m)
    probs = p / (p.sum(axis=-1, keepdims=True) + jnp.exp(sink - m))
    out = jnp.einsum('bnhgqk,bnkhd->bnqhgd', probs.astype(v.dtype), vb)
    return out.reshape(B, S, D_ATTN)

def rwkv7_time_mix(p, w0, w_decay_up, a0, w_iclr_up, w_gate_up, k_k, k_a, r_k, ln_x_g, ln_x_b):
    B, S, _ = p.shape
    H, N = N_RWKV_HEADS, HEAD_DIM
    p = p.astype(jnp.float32)
    r, k, v, zw, za, zg = jnp.split(p, RWKV_SPLITS, axis=-1)
    w_log = -jax.nn.softplus(-(w0 + jnp.tanh(zw) @ w_decay_up)) - 0.5
    decay = jnp.exp(-jnp.exp(w_log))
    a = jax.nn.sigmoid(a0 + za @ w_iclr_up)
    g = jax.nn.sigmoid(zg) @ w_gate_up
    kk = (k * k_k).reshape(B, S, H, N)
    kk = kk / jnp.maximum(jnp.sqrt(jnp.sum(kk * kk, axis=-1, keepdims=True)), 1e-12)
    k = k * (1.0 + (a - 1.0) * k_a)

    def heads(t):
        return t.reshape(B, S, H, N)

    def tmaj(t):
        return t.swapaxes(0, 1)

    rh, kh, vh = heads(r), heads(k), heads(v)

    def step(state, inp):
        r_t, w_t, k_t, v_t, kk_t, a_t = inp
        sa = jnp.einsum('bhvk,bhk->bhv', state, -kk_t)
        state = (state * w_t[:, :, None, :]
                 + sa[..., None] * (kk_t * a_t)[:, :, None, :]
                 + v_t[..., None] * k_t[:, :, None, :])
        return state, jnp.einsum('bhvk,bhk->bhv', state, r_t)

    state0 = jnp.zeros((B, H, N, N), jnp.float32)
    _, o = lax.scan(step, state0, (tmaj(rh), tmaj(heads(decay)), tmaj(kh), tmaj(vh), tmaj(kk), tmaj(heads(a))))
    o = o.swapaxes(0, 1)
    mu = jnp.mean(o, axis=-1, keepdims=True)
    var = jnp.mean(jnp.square(o - mu), axis=-1, keepdims=True)
    o = ((o - mu) * lax.rsqrt(var + GN_EPS)).reshape(B, S, D_RWKV) * ln_x_g + ln_x_b
    bonus = jnp.sum(rh * kh * r_k, axis=-1, keepdims=True) * vh
    o = o + bonus.reshape(B, S, D_RWKV)
    return o * g

def conv_gated_ffn(h, w_up, conv_w, conv_b, w_down):
    S = h.shape[1]
    u = h @ w_up
    u_pad = jnp.pad(u, ((0, 0), (CONV_WIDTH - 1, 0), (0, 0)))
    u = conv_b + sum(conv_w[j] * u_pad[:, j:j + S] for j in range(CONV_WIDTH))
    gate, val = jnp.split(u, 2, axis=-1)
    return (jax.nn.gelu(gate, approximate=True) * val) @ w_down

def first_inputs(seed: int = 0) -> dict:
    key = jax.random.key(seed)
    ks = jax.random.split(key, 24)
    L = DEPTH
    nrm = lambda k, shape, s: jax.random.normal(k, shape, jnp.float32) * s
    return {
        "x": jax.random.normal(ks[0], (BATCH, SEQ, D_MODEL), jnp.float32),
        "norm_mix_pre": 1.0 + nrm(ks[1], (L, D_MODEL), 0.02),
        "norm_mix_post": 1.0 + nrm(ks[2], (L, D_MODEL), 0.02),
        "norm_ffn_pre": 1.0 + nrm(ks[3], (L, D_MODEL), 0.02),
        "norm_ffn_post": 1.0 + nrm(ks[4], (L, D_MODEL), 0.02),
        "w_in": nrm(ks[5], (L, D_MODEL, D_IN), D_MODEL ** -0.5),
        "rel_bias": nrm(ks[6], (N_BUCKETS, N_Q_HEADS), 0.5),
        "sinks": nrm(ks[7], (L, N_Q_HEADS), 0.5),
        "rwkv_shift_mix": jax.random.uniform(ks[8], (L, RWKV_COLS), jnp.float32),
        "w0": jax.random.uniform(ks[9], (L, D_RWKV), jnp.float32, -5.0, 0.0),
        "w_decay_up": nrm(ks[10], (L, LORA_DECAY, D_RWKV), 0.5 * LORA_DECAY ** -0.5),
        "a0": nrm(ks[11], (L, D_RWKV), 0.1),
        "w_iclr_up": nrm(ks[12], (L, LORA_ICLR, D_RWKV), 0.5 * LORA_ICLR ** -0.5),
        "w_gate_up": nrm(ks[13], (L, LORA_GATE, D_RWKV), LORA_GATE ** -0.5),
        "k_k": 0.85 + nrm(ks[14], (L, D_RWKV), 0.05),
        "k_a": 1.0 + nrm(ks[15], (L, D_RWKV), 0.05),
        "r_k": nrm(ks[16], (L, N_RWKV_HEADS, HEAD_DIM), 0.1),
        "ln_x_g": 1.0 + nrm(ks[17], (L, D_RWKV), 0.02),
        "ln_x_b": nrm(ks[18], (L, D_RWKV), 0.02),
        "w_out": nrm(ks[19], (L, D_MODEL, D_MODEL), D_MODEL ** -0.5),
        "w_ffn_up": nrm(ks[20], (L, D_MODEL, 2 * D_FF), D_MODEL ** -0.5),
        "conv_w": nrm(ks[21], (L, CONV_WIDTH, 2 * D_FF), CONV_WIDTH ** -0.5),
        "conv_b": nrm(ks[22], (L, 2 * D_FF), 0.02),
        "w_ffn_down": nrm(ks[23], (L, D_FF, D_MODEL), D_FF ** -0.5),
    }

def first_block(x, norm_mix_pre, norm_mix_post, norm_ffn_pre, norm_ffn_post, w_in, rel_bias, sinks,
              rwkv_shift_mix, w0, w_decay_up, a0, w_iclr_up, w_gate_up, k_k, k_a, r_k, ln_x_g, ln_x_b,
              w_out, w_ffn_up, conv_w, conv_b, w_ffn_down):
    for l in range(DEPTH):
        h = rms_norm(x, norm_mix_pre[l])
        proj = h @ w_in[l]
        q, k, v, p = jnp.split(proj, (D_ATTN, D_ATTN + D_KV, D_ATTN + 2 * D_KV), axis=-1)
        attn = sliding_window_sink_attention(q, k, v, rel_bias, sinks[l])
        p_prev = jnp.concatenate([jnp.zeros_like(p[:, :1]), p[:, :-1]], axis=1)
        p = p + (p_prev - p) * rwkv_shift_mix[l]
        rw = rwkv7_time_mix(p, w0[l], w_decay_up[l], a0[l], w_iclr_up[l], w_gate_up[l],
                            k_k[l], k_a[l], r_k[l], ln_x_g[l], ln_x_b[l])
        mix = jnp.concatenate([attn, rw.astype(x.dtype)], axis=-1) @ w_out[l]
        x = x + rms_norm(mix, norm_mix_post[l])
        f = conv_gated_ffn(rms_norm(x, norm_ffn_pre[l]), w_ffn_up[l], conv_w[l], conv_b[l], w_ffn_down[l])
        x = x + rms_norm(f, norm_ffn_post[l])
    return x


CHUNK = 64
D_MIX = D_MODEL

GLA_W = D_MIX // 2
GLA_HEADS = 4
GLA_DV = GLA_W // GLA_HEADS
GLA_DK = GLA_DV // 2
GLA_QK_W = GLA_HEADS * GLA_DK
GLA_GATE_RANK = 16
GLA_GATE_TAU = 16.0

HGRN_W = D_MIX // 4
HGRN_HEADS = 4
HGRN_DV = HGRN_W // HGRN_HEADS
HGRN_DK = 64
HGRN_QK_W = HGRN_HEADS * HGRN_DK

SB_W = D_MIX - GLA_W - HGRN_W
SB_HEADS = 4
SB_DH = SB_W // SB_HEADS
SB_BLOCK = 128

IN_WIDTHS = (GLA_QK_W, GLA_QK_W, GLA_W, GLA_GATE_RANK, GLA_W,
             HGRN_QK_W, HGRN_QK_W, HGRN_W, HGRN_W,
             SB_W, SB_W, SB_W, SB_W)
D_IN_2 = sum(IN_WIDTHS)
EPS = 1e-6


def rms_norm_2(x):
    xf = x.astype(jnp.float32)
    y = xf * lax.rsqrt(jnp.mean(xf * xf, axis=-1, keepdims=True) + EPS)
    return y.astype(x.dtype)

def split_heads(a, n_heads):
    b, t, w = a.shape
    return a.reshape(b, t, n_heads, w // n_heads).transpose(0, 2, 1, 3)

def merge_heads(a):
    b, h, t, d = a.shape
    return a.transpose(0, 2, 1, 3).reshape(b, t, h * d)

def chunk_gated_linear_attn(q, k, v, g):
    bsz, nh, t, dk = q.shape
    dv = v.shape[-1]
    n_chunks = t // CHUNK

    def to_chunks(a):
        return a.reshape(bsz, nh, n_chunks, CHUNK, a.shape[-1]).transpose(2, 0, 1, 3, 4)

    causal = jnp.tril(jnp.ones((CHUNK, CHUNK), dtype=bool))[:, :, None]

    def step(state, inp):
        q_c, k_c, v_c, g_c = inp
        b_cum = jnp.cumsum(g_c, axis=2)
        diff = b_cum[:, :, :, None, :] - b_cum[:, :, None, :, :]
        decay = jnp.exp(jnp.where(causal, diff, -jnp.inf))
        scores = jnp.einsum('bhtd,bhsd,bhtsd->bhts', q_c, k_c, decay)
        o_c = (jnp.einsum('bhts,bhsv->bhtv', scores, v_c)
               + jnp.einsum('bhtd,bhdv->bhtv', q_c * jnp.exp(b_cum), state))
        b_last = b_cum[:, :, -1:, :]
        state = (jnp.exp(b_last[:, :, 0, :, None]) * state
                 + jnp.einsum('bhsd,bhsv->bhdv', k_c * jnp.exp(b_last - b_cum), v_c))
        return state, o_c

    s0 = jnp.zeros((bsz, nh, dk, dv), dtype=v.dtype)
    _, o = lax.scan(step, s0, (to_chunks(q), to_chunks(k), to_chunks(v), to_chunks(g)))
    return o.transpose(1, 2, 0, 3, 4).reshape(bsz, nh, t, dv)

def stick_breaking_attn(q, k, v):
    bsz, nh, t, dh = q.shape
    scale = dh ** -0.5
    outs = []
    for i in range(t // SB_BLOCK):
        n_keys = (i + 1) * SB_BLOCK
        q_blk = q[:, :, i * SB_BLOCK:n_keys]
        k_blk = k[:, :, :n_keys]
        v_blk = v[:, :, :n_keys]
        z = jnp.einsum('bhtd,bhsd->bhts', q_blk, k_blk).astype(jnp.float32) * scale
        t_pos = i * SB_BLOCK + jnp.arange(SB_BLOCK)[:, None]
        s_pos = jnp.arange(n_keys)[None, :]
        strict = s_pos < t_pos
        log_beta = jax.nn.log_sigmoid(z)
        log_1m_beta = jnp.where(strict, jax.nn.log_sigmoid(-z), 0.0)
        between = lax.cumsum(log_1m_beta, axis=3, reverse=True) - log_1m_beta
        weights = jnp.where(strict, jnp.exp(log_beta + between), 0.0)
        outs.append(jnp.einsum('bhts,bhsv->bhtv', weights.astype(v.dtype), v_blk))
    return jnp.concatenate(outs, axis=2)

def split_columns(p):
    idx = []
    acc = 0
    for w in IN_WIDTHS[:-1]:
        acc += w
        idx.append(acc)
    return jnp.split(p, idx, axis=-1)

def second_inputs(seed: int = 0) -> dict:
    key = jax.random.key(seed)
    ks = jax.random.split(key, 12)
    f32 = jnp.float32
    x = jax.random.normal(ks[0], (BATCH, SEQ, D_MODEL), f32)
    c = jax.random.normal(ks[1], (BATCH, D_MODEL), f32)
    w_ada = jax.random.normal(ks[2], (DEPTH, D_MODEL, 3 * D_MODEL), f32) * (0.5 * D_MODEL ** -0.5)
    b_ada = 0.02 * jax.random.normal(ks[3], (DEPTH, 3 * D_MODEL), f32)
    w_in = jax.random.normal(ks[4], (DEPTH, D_MODEL, D_IN_2), f32) * D_MODEL ** -0.5
    w_gla_gate2 = jax.random.normal(ks[5], (DEPTH, GLA_GATE_RANK, GLA_QK_W), f32) * GLA_GATE_RANK ** -0.5
    b_gla_gate = 0.1 * jax.random.normal(ks[6], (DEPTH, GLA_QK_W), f32)
    gla_norm_w = 1.0 + 0.1 * jax.random.normal(ks[7], (DEPTH, GLA_DV), f32)
    hgrn_lb_logits = jax.random.normal(ks[8], (DEPTH, HGRN_QK_W), f32)
    hgrn_norm_w = 1.0 + 0.1 * jax.random.normal(ks[9], (DEPTH, HGRN_DV), f32)
    w_out = jax.random.normal(ks[10], (DEPTH, D_MIX, D_MODEL), f32) * D_MIX ** -0.5
    final_norm_w = 1.0 + 0.1 * jax.random.normal(ks[11], (D_MODEL,), f32)
    return {'x': x, 'c': c, 'w_ada': w_ada, 'b_ada': b_ada, 'w_in': w_in,
            'w_gla_gate2': w_gla_gate2, 'b_gla_gate': b_gla_gate, 'gla_norm_w': gla_norm_w,
            'hgrn_lb_logits': hgrn_lb_logits, 'hgrn_norm_w': hgrn_norm_w,
            'w_out': w_out, 'final_norm_w': final_norm_w}

def second_block(x, c, w_ada, b_ada, w_in, w_gla_gate2, b_gla_gate, gla_norm_w,
              hgrn_lb_logits, hgrn_norm_w, w_out, final_norm_w):
    c_act = jax.nn.silu(c)
    probs = jax.nn.softmax(hgrn_lb_logits.astype(jnp.float32), axis=0)
    cum = jnp.cumsum(probs, axis=0)
    lower_bounds = (cum - cum[0:1]).astype(x.dtype)

    for l in range(DEPTH):
        ada = c_act @ w_ada[l] + b_ada[l]
        shift, scale, gate = jnp.split(ada, 3, axis=-1)
        h = rms_norm_2(x) * (1.0 + scale[:, None, :]) + shift[:, None, :]
        p = h @ w_in[l]
        (qa, ka, va, lra, ga,
         qb, fb, ib, gb,
         qc, kc, vc, gc) = split_columns(p)

        log_alpha = jax.nn.log_sigmoid(lra @ w_gla_gate2[l] + b_gla_gate[l]) / GLA_GATE_TAU
        o_a = chunk_gated_linear_attn(split_heads(qa, GLA_HEADS) * GLA_DK ** -0.5,
                                      split_heads(ka, GLA_HEADS),
                                      split_heads(va, GLA_HEADS),
                                      split_heads(log_alpha, GLA_HEADS))
        o_a = merge_heads(rms_norm_2(o_a) * gla_norm_w[l]) * jax.nn.silu(ga)

        lb = lower_bounds[l]
        log_f = jnp.logaddexp(jnp.log(lb), jnp.log1p(-lb) + jax.nn.log_sigmoid(fb))
        k_b = (1.0 - lb) * jax.nn.sigmoid(-fb)
        o_b = chunk_gated_linear_attn(split_heads(jax.nn.silu(qb), HGRN_HEADS),
                                      split_heads(k_b, HGRN_HEADS),
                                      split_heads(ib, HGRN_HEADS),
                                      split_heads(log_f, HGRN_HEADS))
        o_b = merge_heads(rms_norm_2(o_b) * hgrn_norm_w[l]) * jax.nn.silu(gb)

        o_c = stick_breaking_attn(split_heads(qc, SB_HEADS),
                                  split_heads(kc, SB_HEADS),
                                  split_heads(vc, SB_HEADS))
        o_c = merge_heads(o_c) * jax.nn.silu(gc)

        y = jnp.concatenate([o_a, o_b, o_c], axis=-1) @ w_out[l]
        x = x + gate[:, None, :] * y

    return rms_norm_2(x) * final_norm_w


def setup_inputs(seed=0):
    out = dict(first_inputs(seed))
    for name, value in second_inputs(seed + 1).items():
        if name != "x":
            out[name + "_2"] = value
    return out


def reference(
    x, norm_mix_pre, norm_mix_post, norm_ffn_pre, norm_ffn_post, w_in, rel_bias, sinks,
    rwkv_shift_mix, w0, w_decay_up, a0, w_iclr_up, w_gate_up, k_k, k_a, r_k, ln_x_g, ln_x_b,
    w_out, w_ffn_up, conv_w, conv_b, w_ffn_down, c_2, w_ada_2, b_ada_2, w_in_2, w_gla_gate2_2,
    b_gla_gate_2, gla_norm_w_2, hgrn_lb_logits_2, hgrn_norm_w_2, w_out_2, final_norm_w_2,
):
    x = first_block(
        x, norm_mix_pre, norm_mix_post, norm_ffn_pre, norm_ffn_post, w_in, rel_bias, sinks,
        rwkv_shift_mix, w0, w_decay_up, a0, w_iclr_up, w_gate_up, k_k, k_a, r_k, ln_x_g, ln_x_b,
        w_out, w_ffn_up, conv_w, conv_b, w_ffn_down,
    )
    return second_block(
        x, c_2, w_ada_2, b_ada_2, w_in_2, w_gla_gate2_2, b_gla_gate_2, gla_norm_w_2,
        hgrn_lb_logits_2, hgrn_norm_w_2, w_out_2, final_norm_w_2,
    )


_drawn_inputs = setup_inputs


def setup_inputs(seed=0):
    import zlib

    import numpy as np

    out = dict(_drawn_inputs(seed))
    spreads = {}
    factors = {'norm_mix_post': 3.331,
     'norm_ffn_pre': 3.561,
     'norm_ffn_post': 43.399,
     'sinks': 26.303,
     'ln_x_g': 3.662,
     'ln_x_b': 3.699,
     'conv_b': 3.426,
     'b_ada_2': 5.946,
     'w_gla_gate2_2': 3.281,
     'b_gla_gate_2': 8.0,
     'gla_norm_w_2': 72.068,
     'hgrn_norm_w_2': 96.241}
    for name, (base, spread) in spreads.items():
        noise = np.random.default_rng([zlib.crc32(name.encode()), seed]).standard_normal(out[name].shape)
        drawn = base * np.exp(spread * noise) if base else spread * noise
        out[name] = __import__('jax').numpy.asarray(drawn.astype(out[name].dtype))
    for name, factor in factors.items():
        out[name] = (out[name] * factor).astype(out[name].dtype)
    return out
```

```python
from contextlib import ExitStack, contextmanager

import numpy as np

import concourse.bass as bass
from concourse import mybir

ACT = mybir.ActivationFunctionType
ALU = mybir.AluOpType
F32 = mybir.dt.float32
F32R = mybir.dt.float32r
U32 = mybir.dt.uint32
AX_X = mybir.AxisListType.X

P = 128
T = 1024
D = 1024
KT = D // P
NB = T // P
RC = 64
NEG = -1e30
EPS = 1e-6
GN_EPS = 64e-5
DECAY = float(np.exp(-0.5))
SCALE = 64 ** -0.5
N_BUCKETS, MAX_DISTANCE = 32, 128

G_IN, G_OUT, G_FFN = 0, 20, 28
FFN_GROUPS, GROUP = 4, 8
G_IN2 = G_FFN + FFN_GROUPS * 3 * GROUP
N_GATE2, N_CHAN2, N_TOK2 = 8, 13, 8
G_OUT2 = G_IN2 + N_GATE2 + N_CHAN2 + N_TOK2
N_TILES = G_OUT2 + 8

UNIT = 4096
BASE = 16640

PARAMS = [("g_mix_pre", 8), ("g_mix_post", 8), ("g_ffn_pre", 8), ("g_ffn_post", 8), ("shift_mix", 14),
          ("w0", 4), ("a0", 4), ("k_k", 4), ("k_a", 4), ("r_k", 4), ("ln_g", 4), ("ln_b", 4),
          ("conv_w", 3 * 64), ("conv_b", 64), ("b_ada", 24), ("c", 8), ("b_gla", 2), ("gla_w", 1),
          ("hgrn_w", 1), ("lb", 2), ("final_w", 8), ("sinks", 8),
          ("ident", 128), ("halves", 128), ("center", 128), ("mean_all", 1), ("mean2", 2), ("mean_half", 2),
          ("w_lora", 512), ("w_gate", 512), ("w_gla2", 256), ("onehot", 384), ("rel_bias", 8)]
COL = {}
for _n, _w in PARAMS:
    COL[_n] = (sum(w for _, w in COL.values()), _w)
N_COL = sum(w for _, w in COL.values())
N_RMASK = 2 * RC + RC + 6 * RC + RC


class InOrder:

    def __init__(self, eng):
        self.eng, self.busy = eng, False
        self.dma_start, self.snap, self.sem_inc = eng.dma_start, eng.snap, eng.sem_inc

    def settle(self):
        if self.busy:
            self.eng.drain()
            self.busy = False

    def wait_ge(self, sem, value):
        self.settle()
        self.eng.wait_ge(sem, value)

    def op(self, emit):
        def run(*args, **kw):
            self.settle()
            self.busy = True
            return emit(*args, **kw)
        return run

    @contextmanager
    def Fori(self, lo, hi):
        self.settle()
        with self.eng.Fori(lo, hi) as i:
            yield i
            self.settle()


def build(nc, dr, stop=99):
    with ExitStack() as ctx:
        sems = {}

        def S(name):
            if name not in sems:
                sems[name] = ctx.enter_context(nc.semaphore(name))
            return sems[name]

        def at(name, shape, unit, dt=F32, off=0):
            return nc.alloc_sbuf_tensor_at(name, shape, dt, offset=BASE + int(unit * UNIT) + off)

        w_raw = at("w_raw", [P, 2, KT, P], 0)
        w_hi = at("w_hi", [P, 2, KT, P], 2, F32R)
        w_lo = at("w_lo", [P, 2, KT, P], 4, F32R)
        x_hi = at("x_hi", [P, KT, T], 6, F32R)
        x_lo = at("x_lo", [P, KT, T], 14, F32R)
        f_hi = at("f_hi", [P, GROUP, T], 22, F32R)
        f_lo = at("f_lo", [P, GROUP, T], 30, F32R)
        cst = at("cst", [P, N_COL], 49)
        small = at("small", [P, 256], 49, off=-(-4 * N_COL // 32) * 32)
        assert 4 * (N_COL + 256) <= 229368 - BASE - 49 * UNIT

        def par(name, a=0, n=None, p0=0, p1=P):
            c, w = COL[name]
            return cst[p0:p1, c + a:c + a + (w - a if n is None else n)]


        class Places:

            def __init__(self, *runs):
                self.runs = [[BASE + a * UNIT, BASE + b * UNIT] for a, b in runs]

            def __call__(self, name, shape, dt=F32, size=4):
                need = -(-int(np.prod(shape[1:])) * size // 32) * 32
                run = next(r for r in self.runs if r[1] - r[0] >= need)
                run[0] += need
                return nc.alloc_sbuf_tensor_at(name, shape, dt, offset=run[0] - need)

        x_in = at("x_in", [P, KT, T], 22)
        sq_a = at("sq_a", [P, 2, T], 42)
        nrm_a = at("nrm_a", [P, 2, T], 44)
        sq_b = at("sq_b", [P, 2, T], 30)
        nrm_b = at("nrm_b", [P, 2, T], 32)
        proj = at("proj", [P, 20, T], 22)
        raw = at("raw", [P, 2, T], 42)
        dif = at("dif", [P, 2, T], 44)
        ADA_RING, ADA_N = 6, 3 * KT
        ada_w = at("ada_w", [P, ADA_RING, T], 33)
        ada_acc = at("ada_acc", [P, 3, T], 39)

        bias = at("bias", [P, 8, 256], 47)
        bias_row = at("bias_row", [P, 384], 46)
        pl = Places((6, 14))
        sc = pl("sc", [P, 2, 4, 256])
        pT = pl("pT", [P, 2, 2, 512])
        q_st = pl("q_st", [P, 2, 4, P])
        k_st = pl("k_st", [P, 2, 2 * P])
        v_st = pl("v_st", [P, 2, 2, P])

        kkn = at("kkn", [P, 4, T], 6)
        kka = at("kka", [P, 4, T], 10)
        cum = at("cum", [P, 4, T], 14)
        rk = at("rk", [P, 4, T], 18)
        smask = at("smask", [P, T], 46)
        ut = at("ut", [P, 2, T], 42)
        tt_ = at("tt_", [P, 2, T], 44)
        pl = Places((18, 22), (26, 28), (42, 49), (40, 41))
        lvl = pl("lvl", [P, 2, 5, 4, RC])
        rmask = pl("rmask", [P, N_RMASK])
        xx = pl("xx", [P, 2, 2, 4, RC])
        m1 = pl("m1", [P, 2, 4, 2 * RC])
        m2 = pl("m2", [P, 2, 4, 2 * RC])
        ar = pl("ar", [P, 2, 4, 2, RC])
        e_neg = pl("e_neg", [P, 2, 4, RC + 1])
        e_pos = pl("e_pos", [P, 2, 4, RC])
        b_ch = pl("b_ch", [P, 2, 4, RC])
        k_ch = pl("k_ch", [P, 2, 4, RC])
        v_ch = pl("v_ch", [P, 2, 4, RC])
        vk_tok = pl("vk_tok", [P, 2, 2, 4, RC])
        b_tok = pl("b_tok", [P, 2, 4, RC])
        y_sb = pl("y_sb", [P, 2, 4, RC])
        rhs = pl("rhs", [P, 4, RC])
        u_sb = pl("u_sb", [P, 4, RC])
        st = pl("st", [P, 2, 4, RC])
        o1 = proj[:, 6:10, :]
        rk2 = at("rk2", [P, 4, T], 18)
        oc = at("oc", [P, 2, T], 42)
        osq = at("osq", [P, 2, T], 44)

        y1 = at("y1", [P, KT, T], 22)
        x1 = at("x1", [P, KT, T], 30)
        f_acc = at("f_acc", [P, KT, T], 38)
        cg = at("cg", [P, T], 46)
        cv = at("cv", [P, T], 47)
        gv = at("gv", [P, T], 48)
        x2 = at("x2", [P, KT, T], 22)

        proj2 = at("proj2", [P, N_CHAN2, T], 22)
        v2 = at("v2", [P, 8, NB, P], 35)
        gate_st = at("gate_st", [P, 2, T], 43)
        c4 = at("c4", [P, 4, T], 6)
        smask2 = at("smask2", [P, T], 10)
        g4 = at("g4", [P, 2, T], 12)
        g5 = at("g5", [P, 2, T], 14)
        lbt = at("lbt", [P, 2, T], 16)
        pl = Places((10, 22), (43, 49))
        e7 = pl("e7", [P, 2, 7, 4, P])
        s_m = pl("s_m", [P, 2, 8, P])
        zz = pl("zz", [P, 2, 4, P])
        v_b = pl("v_b", [P, 2, 6, P])
        st2 = pl("st2", [P, 384])
        c_b = pl("c_b", [P, 2, 4, P])
        q_b = pl("q_b", [P, 2, 4, P])
        k_b = pl("k_b", [P, 2, 4, P])
        qe = pl("qe", [P, 2, 4, P])
        gmask = pl("gmask", [P, 8, P])
        kh = pl("kh", [P, 4, P])
        e_end = pl("e_end", [P, 4, P])
        pl = Places((10, 22), (43, 49))
        sbmask = pl("sbmask", [P, 3, P])
        ab = pl("ab", [P, 2, T])
        spl = pl("spl", [P, 2, T])
        wts = pl("wts", [P, 2, T])
        lacc = pl("lacc", [P, T])
        sq_h = at("sq_h", [P, 2, T], 43)
        hn_v = at("hn_v", [P, 96], 45)
        hn_r = at("hn_r", [P, 96], 45, off=512)
        gate_in = at("gate_in", [P, 2, T], 46)
        y2 = at("y2", [P, KT, T], 22)
        x3 = at("x3", [P, KT, T], 30)

        ps = ctx.enter_context(nc.psum_tensor("ps", [P, 8, 512], F32))

        def pair(b):
            return ps[:, b:b + 2, :].rearrange("p a b -> p (a b)")

        rs_bc = pair(5)

        sm = {}
        for name, w in (("var", 8), ("rstd", 8), ("silu_c", 8), ("ada", 24), ("omka", 4), ("kn", 64), ("kinv", 64),
                        ("mx", 8), ("nm", 8), ("es", 8), ("den", 8), ("rec", 8), ("lb_d", 2), ("lb_e", 2), ("lb", 2), ("omlb", 2), ("ecl", 8), ("one", 1), ("took", 1), ("took_v", 1)):
            at0 = sum(v.shape[-1] for v in sm.values())
            sm[name] = small[:, at0:at0 + w]

        x1_dram = nc.dram_tensor("x1_spill", (P, KT * T), F32).ap()
        x2_dram = nc.dram_tensor("x2_spill", (P, KT * T), F32).ap()
        bias_dram = nc.dram_tensor("bias_table", (8, P, 384), F32).ap()
        rk_dram = nc.dram_tensor("rk_spill", (P, 4 * T), F32).ap()
        gate_dram = nc.dram_tensor("gate_spill", (8, P, T), F32).ap()

        sq_of = {0: sq_a, 1: sq_a, 2: sq_a, 3: sq_b, 4: sq_b, 5: sq_a}

        mix_src = [proj[:, k, :] for k in range(4)] + [o1[:, k, :] for k in range(4)]
        o_a = [proj2[:, k, :] for k in range(6)] + [proj2[:, 9 + k, :] for k in range(2)]

        def blocks(x, w):
            return x.rearrange("p a (n w) -> p (a n) w", w=w)

        block = ctx.enter_context(nc.Block())

        @block.sync
        def _(sp):
            def load(g, u):
                return sp.dma_start(w_raw[:, u, :, :], g.rearrange("o p (k c) -> p (o k) c", c=P))

            for u in range(2):
                load(dr["wall"][u:u + 1], u).then_inc(S(f"w_in{u}"), 16)
            with sp.Fori(1, N_TILES // 2) as i:
                for u in range(2):
                    g = sp.snap(2 * i + u)
                    src = dr["wall"][bass.ds(g, 1)]
                    sp.wait_ge(S("w_split"), 2 * i + u - 1)
                    load(src, u).then_inc(S(f"w_in{u}"), 16)
            if N_TILES % 2:
                sp.wait_ge(S("w_split"), N_TILES - 2)
                load(dr["wall"][N_TILES - 1:N_TILES], 0).then_inc(S("w_in0"), 16)

        @block.gpsimd
        def _(pool):
            def split(g, u, turn, first=False):
                pool.wait_ge(S(f"w_in{u}"), turn * 16)
                if not first:
                    pool.wait_ge(S("gemm_mm"), g - 1)
                nc.gpsimd.tensor_tensor(w_hi[:, u, :, :], w_raw[:, u, :, :],
                                        sm["one"].unsqueeze(2).to_broadcast([P, KT, P]), ALU.mult).then_inc(S("w_hi_done"), 1)
                pool.wait_ge(S("w_hi_done"), g + 1)
                nc.gpsimd.tensor_tensor(w_lo[:, u, :, :], w_raw[:, u, :, :], w_hi[:, u, :, :].bitcast(F32),
                                        ALU.subtract).then_inc(S("w_split"), 1)

            nc.gpsimd.memset(sm["one"], 1.0).then_inc(S("one"), 1)
            pool.wait_ge(S("one"), 1)
            for u in range(2):
                split(u, u, 1, first=True)
            last = G_OUT2 + 1
            with pool.Fori(1, last // 2) as i:
                for u in range(2):
                    split(2 * i + u, u, i + 1)
            split(last, last % 2, last // 2 + 1)

            def exponents(b, s, first=False):
                pool.wait_ge(S("blk_stage"), b + 1)
                if not first:
                    pool.wait_ge(S("kh_done"), b)
                tt = nc.gpsimd.tensor_tensor
                tt(e_end[:, :, :], c_b[:, s, :, P - 1:P].to_broadcast([P, 4, P]), c_b[:, s, :, :], ALU.subtract)\
                    .then_inc(S("d_done"), 1)
                for l in range(7):
                    hw = 64 >> l
                    e, c_ = blocks(e7[:, s, l, :, :], 2 * hw), blocks(c_b[:, s, :, :], 2 * hw)
                    ref = c_[:, :, hw - 1:hw].to_broadcast([P, 4 * P // (2 * hw), hw])
                    tt(e[:, :, 0:hw], ref, c_[:, :, 0:hw], ALU.subtract).then_inc(S("d_done"), 1)
                    tt(e[:, :, hw:], c_[:, :, hw:], ref, ALU.subtract).then_inc(S("d_done"), 1)

            exponents(0, 0, first=True)
            exponents(1, 1)
            with pool.Fori(1, NB // 2) as i:
                for s in range(2):
                    exponents(2 * i + s, s)

            for g in range(last + 1, last + 2 + last % 2):
                split(g, g % 2, g // 2 + 1)
            with pool.Fori((last + 2 + last % 2) // 2, N_TILES // 2) as i:
                for u in range(2):
                    split(2 * i + u, u, i + 1)
            for g in range(N_TILES // 2 * 2, N_TILES):
                split(g, g % 2, g // 2 + 1)

        @block.tensor
        def _(pe):
            mm = nc.tensor.matmul

            def hold(sem, value):
                pe.wait_ge(S("cst_in"), 16)
                pe.wait_ge(sem, value)

            def gemm(g, u, hi, lo, by_token=False, first=False):
                pe.wait_ge(S("w_split"), g + 1)
                if not first:
                    pe.wait_ge(S("gemm_evac"), g - 1)
                if by_token:
                    for t in range(NB):
                        for k in range(KT):
                            blk = slice(t * P, (t + 1) * P)
                            out = ps[:, 2 * u + t // 4, (t % 4) * P:(t % 4 + 1) * P]
                            mm(out, hi[:, k, blk], w_hi[:, u, k, :], start=(k == 0), stop=False)
                            mm(out, hi[:, k, blk], w_lo[:, u, k, :], start=False, stop=False)
                            last = mm(out, lo[:, k, blk], w_hi[:, u, k, :], start=False, stop=(k == KT - 1))
                else:
                    for k in range(KT):
                        for w, x in ((w_hi, hi), (w_hi, lo), (w_lo, hi)):
                            for h in range(2):
                                last = mm(ps[:, 2 * u + h, :], w[:, u, k, :], x[:, k, h * 512:(h + 1) * 512],
                                          start=(k == 0 and w is w_hi and x is hi),
                                          stop=(k == KT - 1 and w is w_lo))
                last.then_inc(S("gemm_mm"), 1)

            def norm_sum(n):
                for k in range(KT):
                    pe.wait_ge(S("norm_sq"), 8 * n + k + 1)
                    for t in range(NB):
                        last = mm(ps[:, 4, t:t + 1], sq_of[n][:, k % 2, t * P:(t + 1) * P], par("mean_all"),
                                  start=(k == 0 and t == 0), stop=(k == KT - 1), skip_group_check=True)
                    last.then_inc(S("norm_mm"), 1)
                pe.wait_ge(S("rstd_tok"), n + 1)
                for t in range(NB):
                    last = mm(ps[:, 5 + t // 4, (t % 4) * P:(t % 4 + 1) * P], sm["rstd"][:, t:t + 1].to_broadcast([P, P]),
                              par("ident"), start=True, stop=True)
                last.then_inc(S("rs_bcast"), 1)

            pe.wait_ge(S("cst_in"), 16)
            pe.wait_ge(S("neg_row"), 1)
            mm(ps[0:8, 0, 0:384], par("rel_bias", p1=N_BUCKETS + 1), par("onehot", p1=N_BUCKETS + 1),
               start=True, stop=True).then_inc(S("bias_mm"), 1)
            norm_sum(0)

            pe.wait_ge(S("x_lo_done"), 8)
            pe.wait_ge(S("bias_cp"), 1)
            gemm(0, 0, x_hi, x_lo, first=True)
            gemm(1, 1, x_hi, x_lo, first=True)
            gemm(2, 0, x_hi, x_lo)
            gemm(3, 1, x_hi, x_lo)
            pe.wait_ge(S("one"), 1)
            pe.wait_ge(S("ada_acc"), ADA_N)
            for j in range(ADA_N):
                last = mm(ps[:, 7, j:j + 1], ada_acc[:, j // KT, (j % KT) * P:(j % KT + 1) * P], sm["one"],
                          start=True, stop=True)
            last.then_inc(S("ada_mm"), 1)
            gemm(4, 0, x_hi, x_lo)
            gemm(5, 1, x_hi, x_lo, by_token=True)
            with pe.Fori(3, 10) as i:
                for u in range(2):
                    gemm(2 * i + u, u, x_hi, x_lo)
            if stop <= 1:
                return

            pe.wait_ge(S("gemm_evac"), 20)

            def scores(b, s, first=False):
                kb0 = 1 if first else 0
                pe.wait_ge(S("att_stage"), b + 1)
                for g in range(2):
                    if not first:
                        pe.wait_ge(S("att_sc"), 2 * b + g - 1)
                    for m in range(4):
                        last = mm(ps[:, 2 * g + m // 2, (m % 2) * 256 + kb0 * P:(m % 2) * 256 + 256],
                                  q_st[64 * g:64 * g + 64, s, m, :], k_st[64 * g:64 * g + 64, s, kb0 * P:],
                                  start=True, stop=True)
                    last.then_inc(S("att_mm"), 1)

            def attend(b, s, first=False, second=False, last_one=False):
                kb0 = 1 if first else 0
                if not last_one:
                    scores(b + 1, 1 - s)
                for g in range(2):
                    pe.wait_ge(S("att_p"), 2 * b + g + 1)
                    if not (first and g == 0):
                        pe.wait_ge(S("attT_cp"), 2 * b + g)
                    for kb in range(kb0, 2):
                        for m in range(4):
                            last = nc.tensor.transpose(ps[:, 4 + kb, m * P:(m + 1) * P],
                                                       sc[:, g, m, kb * P:(kb + 1) * P], par("ident"))
                    last.then_inc(S("attT_mm"), 1)
                for g in range(2):
                    pe.wait_ge(S("attT_cp"), 2 * b + g + 1)
                    if first and g == 0:
                        pe.wait_ge(S("ada_done"), 1)
                    elif not (first or second) and g == 0:
                        pe.wait_ge(S("att_out"), 2 * b - 2)
                    for kb in range(kb0, 2):
                        last = mm(ps[64 * g:64 * g + 64, 6 + s, :], v_st[:, s, kb, 64 * g:64 * g + 64],
                                  pT[:, g, kb, :], start=(kb == kb0), stop=(kb == 1))
                    last.then_inc(S("av_mm"), 1)

            scores(0, 0, first=True)
            attend(0, 0, first=True)
            attend(1, 1, second=True)
            with pe.Fori(1, NB // 2 - 1) as i:
                for s in range(2):
                    attend(2 * i + s, s)
            attend(NB - 2, 0)
            attend(NB - 1, 1, last_one=True)
            if stop <= 2:
                return

            pe.wait_ge(S("lora_act"), 1)
            pe.wait_ge(S("att_out"), 16)
            for m in range(4):
                if m:
                    pe.wait_ge(S("lora_sig"), m)
                for h in range(2):
                    t = slice(h * 512, (h + 1) * 512)
                    mm(ps[:, h, :], par("w_lora", m * P, P, 0, 64), proj[0:64, 18, t], start=True, stop=True)
                    last = mm(ps[:, 2 + h, :], par("w_lora", m * P, P, 64, P), proj[64:P, 18, t], start=True, stop=True)
                last.then_inc(S("lora_mm"), 1)
                pe.wait_ge(S("kn_sq"), m + 1)
                for t in range(NB):
                    last = mm(ps[:, 4, (m * NB + t) * 2:(m * NB + t) * 2 + 2], tt_[:, m % 2, t * P:(t + 1) * P],
                              par("halves")[:, 0:P:64], start=True, stop=True)
                last.then_inc(S("kn_mm"), 1)

            def spread(src, m, b0):
                for t in range(NB):
                    for h in range(2):
                        c = (m * NB + t) * 2 + h
                        last = mm(ps[64 * h:64 * h + 64, b0 + t // 4, (t % 4) * P:(t % 4 + 1) * P],
                                  src[:, c:c + 1].to_broadcast([P, 64]), par("ident"), start=True, stop=True)
                return last

            pe.wait_ge(S("kinv"), 1)
            for m in range(4):
                if m >= 2:
                    pe.wait_ge(S("kkn_done"), m - 1)
                spread(sm["kinv"], m, 2 * (m % 2)).then_inc(S("kinv_bc"), 1)

            pe.wait_ge(S("kkn_done"), 4)
            H2 = [(m, slice(64 * h, 64 * h + 64)) for m in range(4) for h in range(2)]

            two = {n: pe.alloc_register(f"two{n}") for n in (1, 2, 3)}
            five = {n: pe.alloc_register(f"five{n}") for n in range(1, 6)}
            with pe.Fori(0, 8) as i:
                for n, r in two.items():
                    pe.reg_mov(r, 2 * i + n)
                for n, r in five.items():
                    pe.reg_mov(r, 5 * i + n)
                pe.nop()
                for s in range(2):
                    hold(S("ch_prep"), two[s + 1])
                    z = 4 * s
                    for m, q in H2:
                        mm(ps[q, z + 0, m * P:(m + 1) * P], b_ch[q, s, m, :], ar[q, s, m, :, :], start=True, stop=True)
                        mm(ps[q, z + 1, m * P:(m + 1) * P], k_ch[q, s, m, :], ar[q, s, m, :, :], start=True, stop=True)
                        mm(ps[q, z + 2, m * 64:m * 64 + 64], ar[q, s, m, 0, :], b_ch[q, s, m, :], start=True, stop=True)
                        mm(ps[q, z + 2, 256 + m * 64:256 + m * 64 + 64], b_ch[q, s, m, :], par("ident")[q, q],
                           start=True, stop=True)
                        mm(ps[q, z + 3, m * 64:m * 64 + 64], v_ch[q, s, m, :], par("ident")[q, q], start=True, stop=True)
                        last = mm(ps[q, z + 3, 256 + m * 64:256 + m * 64 + 64], k_ch[q, s, m, :], par("ident")[q, q],
                                  start=True, stop=True)
                    last.then_inc(S("ch_mm"), 1)
                for l in range(5):
                    for s in range(2):
                        if l == 0:
                            hold(S("ch_masked"), two[s + 1])
                        else:
                            hold(S(f"x_upd{s}"), five[l])
                        for m, q in H2:
                            last = mm(ps[q, 4 * s, m * 64:m * 64 + 64], lvl[q, s, l, m, :], xx[q, s, 0, m, :],
                                      start=True, stop=True)
                        last.then_inc(S(f"y_mm{s}"), 1)
                    for s in range(2):
                        hold(S(f"y_cp{s}"), five[l + 1])
                        for m, q in H2:
                            if l < 4:
                                mm(ps[q, 4 * s, m * 64:m * 64 + 64], xx[q, s, 1, m, :], y_sb[q, s, m, :],
                                   start=True, stop=True)
                            last = mm(ps[q, 4 * s, 256 + m * 64:256 + m * 64 + 64], y_sb[q, s, m, :],
                                      xx[q, s, 1, m, :], start=True, stop=True)
                        last.then_inc(S(f"x_mm{s}"), 1)
                for s in range(2):
                    hold(S("st_upd"), two[s + 1])
                    hold(S("ch_tok"), two[s + 1])
                    for m, q in H2:
                        o = ps[q, 6, m * 64:m * 64 + 64]
                        mm(o, ar[q, s, m, 0, :], st[q, s, m, :], start=True, stop=False)
                        last = mm(o, m2[q, s, m, 0:64], vk_tok[q, s, 0, m, :], start=False, stop=True)
                    last.then_inc(S("rhs_mm"), 1)
                    hold(S("rhs_cp"), two[s + 1])
                    hold(S(f"x_upd{s}"), five[5])
                    for m, q in H2:
                        last = mm(ps[q, 6, 256 + m * 64:256 + m * 64 + 64], xx[q, s, 1, m, :], rhs[q, m, :],
                                  start=True, stop=True)
                    last.then_inc(S("u_mm"), 1)
                    hold(S("u_cp"), two[s + 1])
                    for m, q in H2:
                        o = ps[q, 6, m * 64:m * 64 + 64]
                        mm(o, vk_tok[q, s, 1, m, :], vk_tok[q, s, 0, m, :], start=True, stop=False)
                        last = mm(o, b_tok[q, s, m, :], u_sb[q, m, :], start=False, stop=True)
                    last.then_inc(S("ds_mm"), 1)
                    hold(S("o_cp"), two[s + 1])
                    for m, q in H2:
                        o = ps[q, 7, m * 64:m * 64 + 64]
                        mm(o, st[q, s, m, :], ar[q, s, m, 1, :], start=True, stop=False)
                        mm(o, u_sb[q, m, :], m1[q, s, m, 64:], start=False, stop=False)
                        last = mm(o, vk_tok[q, s, 0, m, :], m2[q, s, m, 64:], start=False, stop=True)
                    last.then_inc(S("o_mm"), 1)

            pe.wait_ge(S("o_cp"), 17)
            for m in range(4):
                if m >= 2:
                    pe.wait_ge(S("oc_done"), m - 1)
                for h in range(2):
                    last = mm(ps[:, 2 * (m % 2) + h, :], par("center"), o1[:, m, h * 512:(h + 1) * 512],
                              start=True, stop=True)
                last.then_inc(S("cen_mm"), 1)
                pe.wait_ge(S("gn_sq"), m + 1)
                for t in range(NB):
                    last = mm(ps[:, 4, (m * NB + t) * 2:(m * NB + t) * 2 + 2], osq[:, m % 2, t * P:(t + 1) * P],
                              par("mean_half"), start=True, stop=True)
                last.then_inc(S("gn_mm"), 1)
            pe.wait_ge(S("gn_rstd"), 1)
            pe.wait_ge(S("oc_done"), 4)
            pe.wait_ge(S("rk_back"), 16)
            for m in range(4):
                if m:
                    pe.wait_ge(S("of_done"), m)
                spread(sm["kinv"], m, 0)
                for h in range(2):
                    t = slice(h * 512, (h + 1) * 512)
                    mm(ps[:, 2 + h, :], par("halves"), rk2[:, m, t], start=True, stop=True)
                    last = mm(ps[:, 5 + h, :], par("w_gate", m * P, P), proj[:, 19, t], start=True, stop=True)
                last.then_inc(S("fin_mm"), 1)
            if stop <= 3:
                return

            pe.wait_ge(S("x_lo_done"), 16)
            with pe.Fori(G_OUT // 2, G_FFN // 2) as i:
                for u in range(2):
                    gemm(2 * i + u, u, x_hi, x_lo)
            norm_sum(1)
            norm_sum(2)

            pe.wait_ge(S("x_lo_done"), 24)
            with pe.Fori(0, FFN_GROUPS) as gr:
                with pe.Fori(0, GROUP) as j:
                    g = pe.snap(G_FFN + 3 * GROUP * gr + 2 * j)
                    for u in range(2):
                        gemm(g + u, u, x_hi, x_lo)
                with pe.Fori(0, GROUP // 2) as j:
                    g = pe.snap(G_FFN + 3 * GROUP * gr + 2 * GROUP + 2 * j)
                    pe.wait_ge(S("f_lo_done"), 8 * gr + 8)
                    for u in range(2):
                        gemm(g + u, u, f_hi, f_lo)
            norm_sum(3)
            norm_sum(4)
            if stop <= 4:
                return

            pe.wait_ge(S("x_lo_done"), 32)
            with pe.Fori(G_IN2 // 2, (G_IN2 + N_GATE2 + N_CHAN2 - 1) // 2) as i:
                for u in range(2):
                    gemm(2 * i + u, u, x_hi, x_lo)
            g = G_IN2 + N_GATE2 + N_CHAN2 - 1
            gemm(g, g % 2, x_hi, x_lo)
            g0 = g + 1
            with pe.Fori(0, N_TOK2 // 2) as i:
                for u in range(2):
                    gemm(2 * i + (g0 + u), (g0 + u) % 2, x_hi, x_lo, by_token=True)
            pe.wait_ge(S("gemm_evac"), G_OUT2)
            for m in range(2):
                for h in range(2):
                    last = mm(ps[:, 2 * m + h, :], par("w_gla2", m * P, P, 0, 16), proj2[0:16, 8, h * 512:(h + 1) * 512],
                              start=True, stop=True)
                last.then_inc(S("gla_mm"), 1)

            pe.wait_ge(S("lsig"), 4)
            pe.sem_inc(S("lev_mm"), 2)
            pe.sem_inc(S("ds2_mm"), 1)

            def gla_block(b, s, last=False):
                if not last:
                    pe.wait_ge(S("kh_done"), b + 1)
                    pe.wait_ge(S("khT_cp"), b + 1)
                    for m in range(4):
                        i_ = nc.tensor.transpose(ps[:, 6, m * P:(m + 1) * P], kh[:, m, :], par("ident"))
                    i_.then_inc(S("khT_mm"), 1)
                for l in range(8):
                    if l < 7:
                        pe.wait_ge(S("z_done"), 7 * b + l + 1)
                    pe.wait_ge(S("lev_cp"), 8 * b + l + 1)
                    n = P // 2 if l < 7 else P
                    for h in range(8):
                        q = slice(64 * (h % 2), 64 * (h % 2) + 64)
                        if l < 7:
                            lh = zz[q, l % 2, h // 2, :]
                            rh = lh.rearrange("p (n w) -> p n w", w=P >> l)[:, :, 64 >> l:]
                        else:
                            lh, rh = k_b[q, s, h // 2, :], q_b[q, s, h // 2, :]
                        i_ = mm(ps[:, 2 * (l % 2) + h % 2, (h // 2) * n:(h // 2 + 1) * n], lh, rh, start=True, stop=True)
                    i_.then_inc(S("lev_mm"), 1)
                    if l == 4 and not last:
                        pe.wait_ge(S("khT_cp"), b + 2)
                        pe.wait_ge(S("st2_upd"), b + 1)
                        for h in range(4):
                            q = slice(64 * (h % 2), 64 * (h % 2) + 64)
                            mm(ps[q, 7, (h // 2) * P:(h // 2 + 1) * P], kh[:, h // 2, q], v_b[:, s, h, :],
                               start=True, stop=True)
                            i_ = mm(ps[q, 7, 256 + (h // 2) * 64:256 + (h // 2) * 64 + 64], kh[:, 2 + h // 2, q],
                                    v_b[:, s, 4 + h // 2, q], start=True, stop=True)
                        i_.then_inc(S("ds2_mm"), 1)
                pe.wait_ge(S("lev_cp"), 8 * b + 10)
                pe.wait_ge(S("st2_upd"), b + 1)
                pe.wait_ge(S("o2_cp"), b + 1)
                for h in range(4):
                    o = ps[:, 4 + h % 2, (h // 2) * P:(h // 2 + 1) * P]
                    q = slice(64 * (h % 2), 64 * (h % 2) + 64)
                    mm(o, v_b[:, s, h, :], s_m[:, s, 4 * (h % 2) + h // 2, :], start=True, stop=False)
                    mm(o, st2[q, (h // 2) * P:(h // 2 + 1) * P], qe[q, s, h // 2, :], start=False, stop=True)
                for h in range(4):
                    q = slice(64 * (h % 2), 64 * (h % 2) + 64)
                    o = ps[q, 4 + h % 2, 256 + (h // 2) * P:256 + (h // 2 + 1) * P]
                    mm(o, v_b[:, s, 4 + h // 2, q], s_m[:, s, 4 * (h % 2) + 2 + h // 2, :], start=True, stop=False)
                    i_ = mm(o, st2[q, 256 + (h // 2) * 64:256 + (h // 2) * 64 + 64], qe[q, s, 2 + h // 2, :],
                            start=False, stop=True)
                i_.then_inc(S("o2_mm"), 1)

            gla_block(0, 0)
            gla_block(1, 1)
            with pe.Fori(1, NB // 2 - 1) as i:
                for s in range(2):
                    gla_block(2 * i + s, s)
            gla_block(NB - 2, 0)
            gla_block(NB - 1, 1, last=True)

            pe.wait_ge(S("sbmask_in"), 16)
            pe.wait_ge(S("o2_cp"), 9)
            steps = [(h, b) for h in range(4) for b in range(NB - 1, -1, -1)]

            def halves_of(b):
                return [(x, max(b * P - 512 * x, 0), slice(max(b * P, 512 * x), 512 * (x + 1)))
                        for x in range(2) if b * P < 512 * (x + 1)]

            def z_scores(n):
                h, b = steps[n]
                q = slice(64 * (h % 2), 64 * (h % 2) + 64)
                if n >= 2:
                    pe.wait_ge(S("sb_w"), n - 1)
                for x, c, t in halves_of(b):
                    last = mm(ps[:, 2 * (n % 2) + x, c:], proj2[q, 11 + h // 2, b * P:(b + 1) * P],
                              proj2[q, 9 + h // 2, t], start=True, stop=True, skip_group_check=True)
                last.then_inc(S("sb_z"), 1)

            def weigh(n):
                h, b = steps[n]
                pe.wait_ge(S("sb_wm"), n + 1)
                q = slice(64 * (h % 2), 64 * (h % 2) + 64)
                for x, c, t in halves_of(b):
                    last = mm(ps[q, 4 + 2 * (h // 2) + x, c:], v2[:, 6 + h // 2, b, q], wts[:, n % 2, t],
                              start=(b == (NB - 1 if x else 3)), stop=(b == 0), skip_group_check=True)
                last.then_inc(S("sb_pv"), 1)

            z_scores(0)
            z_scores(1)
            for n, (h, b) in enumerate(steps):
                pe.wait_ge(S("sb_sp"), n + 1)
                for x, c, t in halves_of(b):
                    last = mm(ps[:, 2 * (n % 2) + x, c:], sbmask[:, 0, :], spl[:, n % 2, t], start=False, stop=True,
                              skip_group_check=True)
                if b < NB - 1:
                    pe.wait_ge(S("sb_acc"), n)
                    for x, c, t in halves_of(b + 1):
                        last = mm(ps[:, 2 * (n % 2) + x, c:], sbmask[:, 1, :], lacc[:, t], start=False, stop=True,
                                  skip_group_check=True)
                last.then_inc(S("sb_r"), 1)
                if n:
                    weigh(n - 1)
                if n + 2 < len(steps):
                    z_scores(n + 2)
            weigh(len(steps) - 1)

            for k in range(6):
                pe.wait_ge(S("hn_sq"), k + 1)
                for t in range(NB):
                    last = mm(ps[:, 0, (k * NB + t) * 2:(k * NB + t) * 2 + 2], sq_h[:, k % 2, t * P:(t + 1) * P],
                              par("mean2") if k < 4 else par("mean_half"), start=True, stop=True)
                last.then_inc(S("hn_mm"), 1)
            pe.wait_ge(S("hn_rstd"), 1)
            for k in range(6):
                if k >= 2:
                    pe.wait_ge(S("hn_out"), k - 1)
                spread(hn_r, k, 2 + 2 * (k % 2)).then_inc(S("hn_bc"), 1)
            if stop <= 5:
                return

            pe.wait_ge(S("x_lo_done"), 40)
            g0 = G_OUT2
            with pe.Fori(0, 4) as i:
                for u in range(2):
                    gemm(2 * i + (g0 + u), (g0 + u) % 2, x_hi, x_lo)
            norm_sum(5)

        @block.scalar
        def _(eng):
            act = InOrder(eng)
            fn = act.op(nc.scalar.activation)

            def copy(out, in_):
                return fn(out, in_, ACT.Copy)

            def take(sem, value):
                act.wait_ge(sem, value)
                copy(sm["took"], sm["one"])

            def norm(n, src, ready):
                for k in range(KT):
                    ready(k)
                    if n or k >= 2:
                        act.wait_ge(S("norm_mm"), max(8 * n + k - 1, 1))
                    fn(sq_of[n][:, k % 2, :], src(k), ACT.Square).then_inc(S("norm_sq"), 1)
                act.wait_ge(S("var_inv"), n + 1)
                fn(sm["rstd"], sm["var"], ACT.Sqrt).then_inc(S("rstd_tok"), 1)

            def high(n, src, sem):
                for k in range(KT):
                    if sem:
                        act.wait_ge(S(sem), 8 * n + k + 1)
                    copy(x_hi[:, k, :], src(k)).then_inc(S("x_hi_done"), 1)

            act.wait_ge(S("one"), 1)
            act.dma_start(x_in[:, 0:4, :], dr["xT"][:, 0:4 * T].rearrange("p (k t) -> p k t", t=T)).then_inc(S("x_in0"), 16)
            act.dma_start(x_in[:, 4:8, :], dr["xT"][:, 4 * T:].rearrange("p (k t) -> p k t", t=T)).then_inc(S("x_in1"), 16)
            act.dma_start(cst[:, :], dr["cst"]).then_inc(S("cst_in"), 16)

            def ada_load(n):
                if n >= ADA_RING:
                    act.wait_ge(S("ada_acc"), n - ADA_RING + 1)
                act.dma_start(ada_w[:, n % ADA_RING, :], dr["wada"][n]).then_inc(S(f"ada_in{n % ADA_RING}"), 16)

            for n in range(ADA_RING):
                ada_load(n)
            act.wait_ge(S("cst_in"), 16)
            fn(sm["silu_c"], par("c"), ACT.Silu).then_inc(S("c_silu"), 1)
            norm(0, lambda k: x_in[:, k, :], lambda k: act.wait_ge(S(f"x_in{k // 4}"), 16))
            for n in range(ADA_RING, 2 * ADA_RING):
                ada_load(n)
            act.wait_ge(S("bias_mm"), 1)
            copy(bias_row[0:8, :], ps[0:8, 0, 0:384]).then_inc(S("bias_cp"), 1)
            act.wait_ge(S("bias_cp"), 1)
            act.dma_start(bias_dram, bias_row[0:8, :].unsqueeze(1).to_broadcast([8, P, 384])).then_inc(S("bias_out"), 16)
            act.wait_ge(S("bias_out"), 16)
            act.dma_start(bias[:, :, :], bass.AP(bias_dram.tensor, 127, [[383, P], [P * 384, 8], [1, 2 * P]]))\
                .then_inc(S("bias_in"), 16)
            high(0, lambda k: nrm_a[:, k % 2, :], "h_done")

            for g in range(6):
                if g < 2:
                    for n in range((g + 2) * ADA_RING, (g + 3) * ADA_RING):
                        ada_load(n)
                act.wait_ge(S("gemm_mm"), g + 1)
                copy(proj[:, g, :], pair(2 * (g % 2))).then_inc(S("gemm_evac"), 1)
            for g in (6, 7):
                act.wait_ge(S("gemm_mm"), g + 1)
                copy(raw[:, g % 2, :], pair(2 * (g % 2))).then_inc(S("gemm_evac"), 1)
            with act.Fori(4, 10) as i:
                for u in range(2):
                    act.wait_ge(S("gemm_mm"), 2 * i + u + 1)
                    act.wait_ge(S("shift_done"), 2 * i + u - 7)
                    copy(raw[:, u, :], pair(2 * u)).then_inc(S("gemm_evac"), 1)
            if stop <= 1:
                return

            act.wait_ge(S("gemm_mm"), 20)
            act.dma_start(smask[:, :], dr["scan"][:, 0:T]).then_inc(S("smask_in"), 16)

            def stage(b, s, first=False):
                if first:
                    copy(q_st[:, s, :, :], proj[:, 0:4, 0:P])
                    copy(k_st[:, s, P:], proj[:, 4, 0:P])
                    copy(v_st[:, s, 1, :], proj[:, 5, 0:P]).then_inc(S("att_stage"), 1)
                else:
                    q0 = b * P
                    copy(q_st[:, s, :, :], proj[:, 0:4, bass.ds(q0, P)])
                    copy(k_st[:, s, :], proj[:, 4, bass.ds(q0 - P, 2 * P)])
                    copy(v_st[:, s, :, :].rearrange("p a c -> p (a c)"),
                         proj[:, 5, bass.ds(q0 - P, 2 * P)]).then_inc(S("att_stage"), 1)

            def attend(b, s, first=False, last=False):
                if not last:
                    stage(b + 1, 1 - s)
                k0 = P if first else 0
                for g in range(2):
                    act.wait_ge(S("att_max"), 2 * b + g + 1)
                    for m in range(4):
                        fn(sc[:, g, m, k0:], sc[:, g, m, k0:], ACT.Exp, bias=sm["nm"][:, 4 * g + m:4 * g + m + 1],
                           accum_out=sm["den"][:, 4 * g + m:4 * g + m + 1])
                    fn(sm["es"][:, 4 * g:4 * g + 4], sm["es"][:, 4 * g:4 * g + 4], ACT.Exp).then_inc(S("att_exp"), 1)
                for g in range(2):
                    act.wait_ge(S("attT_mm"), 2 * b + g + 1)
                    if first:
                        copy(pT[:, g, 1, :], ps[:, 5, :]).then_inc(S("attT_cp"), 1)
                    else:
                        copy(pT[:, g, :, :], ps[:, 4:6, :]).then_inc(S("attT_cp"), 1)
                for g in range(2):
                    take(S("av_mm"), 2 * b + g + 1)
                    q = slice(64 * g, 64 * g + 64)
                    dst = proj[q, 0:4, 0:P] if first else proj[q, 0:4, bass.ds(b * P, P)]
                    copy(dst, ps[q, 6 + s, :].rearrange("p (m t) -> p m t", t=P)).then_inc(S("att_out"), 1)

            act.wait_ge(S("gemm_evac"), 20)
            stage(0, 0, first=True)
            attend(0, 0, first=True)
            attend(1, 1)
            with act.Fori(1, NB // 2 - 1) as i:
                for s in range(2):
                    attend(2 * i + s, s)
            attend(NB - 2, 0)
            attend(NB - 1, 1, last=True)
            if stop <= 2:
                return

            act.wait_ge(S("shift_done"), 14)
            fn(proj[0:64, 18, :], proj[0:64, 18, :], ACT.Tanh)
            fn(proj[:, 19, :], proj[:, 19, :], ACT.Sigmoid).then_inc(S("lora_act"), 1)
            for m in range(4):
                act.wait_ge(S("lora_mm"), m + 1)
                if m >= 2:
                    act.wait_ge(S("cum_done"), m - 1)
                fn(ut[:, m % 2, :], pair(0), ACT.Sigmoid, bias=par("w0", m, 1))
                fn(kka[:, m, :], pair(2), ACT.Sigmoid, bias=par("a0", m, 1)).then_inc(S("lora_sig"), 1)
                act.wait_ge(S("kk_done"), m + 1)
                if m >= 2:
                    act.wait_ge(S("kn_mm"), m - 1)
                fn(tt_[:, m % 2, :], kkn[:, m, :], ACT.Square).then_inc(S("kn_sq"), 1)
            act.wait_ge(S("kn_mm"), 4)
            fn(sm["kn"], ps[:, 4, 0:64], ACT.Sqrt).then_inc(S("kn_sqrt"), 1)
            act.wait_ge(S("rk_done"), 4)
            act.dma_start(rk_dram, rk[:, :, :].rearrange("p m t -> p (m t)")).then_inc(S("rk_out"), 16)
            act.wait_ge(S("rk_out"), 16)
            act.dma_start(rmask[:, :], dr["rmask"]).then_inc(S("rmask_in"), 16)

            act.sem_inc(S("o_cp"), 1)

            def prepare(c, s):
                t = bass.ds(c * RC, RC)
                fn(e_neg[:, s, :, 1:], cum[:, :, t], ACT.Exp, scale=-DECAY)
                fn(e_pos[:, s, :, :], cum[:, :, t], ACT.Exp, scale=DECAY)
                copy(v_ch[:, s, :, :], proj[:, 14:18, t]).then_inc(S("ch_exp"), 1)

            def chunk_pair(i, last=False):
                for s in range(2):
                    act.wait_ge(S("ch_mm"), 2 * i + s + 1)
                    copy(vk_tok[:, s, :, :, :], ps[:, 4 * s + 3, :].rearrange("p (x m c) -> p x m c", x=2, m=4))\
                        .then_inc(S("ch_tok"), 1)
                for l in range(5):
                    for s in range(2):
                        act.wait_ge(S(f"y_mm{s}"), 5 * i + l + 1)
                        copy(y_sb[:, s, :, :], ps[:, 4 * s, 0:256]).then_inc(S(f"y_cp{s}"), 1)
                for s in range(2):
                    c = 2 * i + s
                    act.wait_ge(S("rhs_mm"), c + 1)
                    copy(rhs[:, :, :], ps[:, 6, 0:256]).then_inc(S("rhs_cp"), 1)
                    if s and not last:
                        act.wait_ge(S("st_upd"), 2 * i + 2)
                        prepare(c + 1, 0)
                    act.wait_ge(S("o_mm"), c + 1)
                    copy(o1[:, :, bass.ds(c * RC, RC)], ps[:, 7, 0:256].rearrange("p (m t) -> p m t", t=RC))\
                        .then_inc(S("o_cp"), 1)
                if not last:
                    act.wait_ge(S("st_upd"), 2 * i + 3)
                    prepare(2 * i + 3, 1)

            act.wait_ge(S("st_upd"), 1)
            for s in range(2):
                prepare(s, s)
            with act.Fori(0, 7) as i:
                chunk_pair(i)
            chunk_pair(7, last=True)

            act.wait_ge(S("st_upd"), 17)
            act.dma_start(rk2[:, :, :], rk_dram.rearrange("p (m t) -> p m t", t=T)).then_inc(S("rk_back"), 16)
            for m in range(4):
                act.wait_ge(S("cen_mm"), m + 1)
                if m >= 2:
                    act.wait_ge(S("gn_mm"), m - 1)
                fn(osq[:, m % 2, :], pair(2 * (m % 2)), ACT.Square).then_inc(S("gn_sq"), 1)
            act.wait_ge(S("gn_var"), 1)
            fn(sm["kinv"], sm["kn"], ACT.Sqrt).then_inc(S("gn_rstd"), 1)
            if stop <= 3:
                return

            act.wait_ge(S("of_done"), 4)
            for k in range(KT):
                copy(x_hi[:, k, :], mix_src[k]).then_inc(S("x_hi_done"), 1)
            act.wait_ge(S("x_lo_done"), 16)
            act.dma_start(x1[:, :, :], dr["xT"].rearrange("p (k t) -> p k t", t=T)).then_inc(S("x_again"), 16)
            for k in range(KT):
                g = G_OUT + k
                act.wait_ge(S("gemm_mm"), g + 1)
                copy(y1[:, k, :], pair(2 * (g % 2))).then_inc(S("gemm_evac"), 1)
            norm(1, lambda k: y1[:, k, :], lambda k: act.wait_ge(S("gemm_evac"), G_OUT + k + 1))
            norm(2, lambda k: x1[:, k, :], lambda k: act.wait_ge(S("x1_done"), k + 1))
            act.dma_start(x1_dram, x1[:, :, :].rearrange("p k t -> p (k t)")).then_inc(S("x1_out"), 16)
            high(1, lambda k: nrm_a[:, k % 2, :], "h_done")
            act.wait_ge(S("x1_out"), 16)

            eng.preload_act_table_set("gelu_apprx_tanh_and_others")
            with act.Fori(0, FFN_GROUPS) as gr:
                with act.Fori(0, GROUP) as j:
                    p = act.snap(GROUP * gr + j)
                    g = act.snap(G_FFN + 3 * GROUP * gr + 2 * j)
                    for u, dst in enumerate((cg, cv)):
                        col = act.snap(2 * p + u)
                        act.wait_ge(S("prod"), p + 1)
                        act.wait_ge(S("gemm_mm"), g + u + 1)
                        fn(dst[:, :], pair(2 * u), ACT.Identity, bias=par("conv_b")[:, bass.ds(col, 1)],
                           scale=par("conv_w")[:, bass.ds(128 + col, 1)]).then_inc(S("conv_a"), 1)
                    act.wait_ge(S("gemm_evac"), g + 1)
                    fn(cg[:, :], cg[:, :], ACT.Gelu_apprx_tanh).then_inc(S("gelu"), 1)
                    act.wait_ge(S("prod"), p + 2)
                    copy(f_hi[:, bass.ds(j, 1), :], gv[:, :].unsqueeze(1)).then_inc(S("f_hi_done"), 1)
            act.wait_ge(S("gemm_mm"), G_IN2)
            act.dma_start(x2[:, :, :], x1_dram.rearrange("p (k t) -> p k t", t=T)).then_inc(S("x1_back"), 16)
            act.wait_ge(S("gemm_evac"), G_IN2)
            norm(3, lambda k: f_acc[:, k, :], lambda k: None)
            norm(4, lambda k: x2[:, k, :], lambda k: act.wait_ge(S("x2_done"), k + 1))
            act.dma_start(x2_dram, x2[:, :, :].rearrange("p k t -> p (k t)")).then_inc(S("x2_out"), 16)
            high(2, lambda k: nrm_b[:, k % 2, :], "h_done")
            if stop <= 4:
                return

            act.wait_ge(S("x2_out"), 16)
            for k in range(N_GATE2):
                g = G_IN2 + k
                if k >= 2:
                    act.wait_ge(S(f"gate_out{k % 2}"), 16 * (k // 2))
                act.wait_ge(S("gemm_mm"), g + 1)
                fn(gate_st[:, k % 2, :], pair(2 * (g % 2)), ACT.Silu).then_inc(S("gemm_evac"), 1)
                act.wait_ge(S("gemm_evac"), g + 1)
                act.dma_start(gate_dram[k], gate_st[:, k % 2, :]).then_inc(S(f"gate_out{k % 2}"), 16)
            for k in range(N_CHAN2):
                g = G_IN2 + N_GATE2 + k
                act.wait_ge(S("gemm_mm"), g + 1)
                if k in (0, 1, 9, 10):
                    i_ = fn(proj2[:, k, :], pair(2 * (g % 2)), ACT.Copy, scale=SCALE)
                else:
                    i_ = fn(proj2[:, k, :], pair(2 * (g % 2)), ACT.Silu if k in (2, 3) else ACT.Copy)
                i_.then_inc(S("gemm_evac"), 1)
            for k in range(N_TOK2):
                g = G_IN2 + N_GATE2 + N_CHAN2 + k
                act.wait_ge(S("gemm_mm"), g + 1)
                copy(v2[:, k, :, :].rearrange("p t c -> p (t c)"), pair(2 * (g % 2))).then_inc(S("gemm_evac"), 1)
            act.wait_ge(S("x_lo_done"), 32)
            act.wait_ge(S("gemm_mm"), G_OUT2)
            act.dma_start(smask2[:, :], dr["scan"][:, T:2 * T]).then_inc(S("smask2_in"), 16)

            act.wait_ge(S("lb_d"), 1)
            eng.preload_act_table_set("natural_log_exp_and_others")
            fn(sm["lb_e"], sm["lb_d"], ACT.Exp).then_inc(S("lb_e"), 1)
            for m in range(4):
                if m < 2:
                    act.wait_ge(S("gla_mm"), 2)
                    src, b_ = pair(2 * m), par("b_gla", m, 1)
                else:
                    act.wait_ge(S("gemm_evac"), G_OUT2)
                    src, b_ = proj2[:, 4 + m, :], 0.0
                if m >= 2:
                    act.wait_ge(S("lsig"), m - 1)
                fn(g4[:, m % 2, :], src, ACT.Abs, bias=b_)
                fn(g4[:, m % 2, :], g4[:, m % 2, :], ACT.Exp, scale=-1.0)
                fn(g4[:, m % 2, :], g4[:, m % 2, :], ACT.Ln, bias=1.0).then_inc(S("ls_ln"), 1)
                if m >= 2:
                    fn(lbt[:, m % 2, :], src, ACT.Exp, scale=-1.0).then_inc(S("lbt_exp"), 1)
                    act.wait_ge(S("lbt_min"), m - 1)
                    fn(lbt[:, m % 2, :], lbt[:, m % 2, :], ACT.Ln, bias=1.0, scale=sm["lb"][:, m - 2:m - 1])\
                        .then_inc(S("lbt_ln"), 1)
                    act.wait_ge(S("fb_read"), m - 1)
                    fn(src, src, ACT.Sigmoid, scale=-1.0).then_inc(S("kb_sig"), 1)

            act.wait_ge(S("lsig"), 4)
            act.dma_start(gmask[:, :, :], dr["gmask"].rearrange("p (l t) -> p l t", t=P)).then_inc(S("gmask_in"), 16)
            act.sem_inc(S("khT_cp"), 1)
            act.sem_inc(S("o2_cp"), 1)
            act.wait_ge(S("kb_done"), 2)
            def stage(b, s):
                t = bass.ds(b * P, P)
                copy(c_b[:, s, :, :], c4[:, :, t])
                copy(k_b[:, s, :, :], proj2[:, 4:8, t])
                copy(q_b[:, s, :, :], proj2[:, 0:4, t])
                copy(v_b[:, s, :, :], v2[:, 0:6, :, :].rearrange("p j t c -> p j (t c)")[:, :, t]).then_inc(S("blk_stage"), 1)

            def exponentials(b, s, early=False):
                act.wait_ge(S("d_done"), 15 * b + 1)
                fn(e_end[:, :, :], e_end[:, :, :], ACT.Exp)
                fn(qe[:, s, :, :], c_b[:, s, :, :], ACT.Exp).then_inc(S("e_done"), 1)
                for l in range(7):
                    act.wait_ge(S("d_done"), 15 * b + 2 * l + 3)
                    fn(e7[:, s, l, :, :], e7[:, s, l, :, :], ACT.Exp).then_inc(S("e_done"), 1)
                if not early:
                    act.wait_ge(S("st2_upd"), b)
                fn(sm["ecl"][:, 4 * s:4 * s + 4].unsqueeze(2), c_b[:, s, :, P - 1:P], ACT.Exp).then_inc(S("ecl_done"), 1)

            def gla_block(b, s, first=False, last=False):
                if not last:
                    stage(b + 1, 1 - s)
                    act.wait_ge(S("khT_mm"), b + 1)
                    copy(kh[:, :, :], ps[:, 6, :].rearrange("p (m c) -> p m c", c=P)).then_inc(S("khT_cp"), 1)
                    exponentials(b + 1, 1 - s, early=first)
                t = bass.ds(b * P, P)
                take(S("o2_mm"), b + 1)
                for h in range(2):
                    q = slice(64 * h, 64 * h + 64)
                    copy(proj2[:, 0:4, :].rearrange("p (m h) t -> p m h t", h=2)[:, :, h, t],
                         ps[:, 4 + h, 0:256].rearrange("p (m t) -> p m t", t=P))
                    i_ = copy(proj2[q, 4:6, t], ps[q, 4 + h, 256:].rearrange("p (m t) -> p m t", t=P))
                i_.then_inc(S("o2_cp"), 1)

            stage(0, 0)
            exponentials(0, 0, early=True)
            gla_block(0, 0, first=True)
            gla_block(1, 1)
            with act.Fori(1, NB // 2 - 1) as i:
                for s in range(2):
                    gla_block(2 * i + s, s)
            gla_block(NB - 2, 0)
            gla_block(NB - 1, 1, last=True)

            eng.preload_act_table_set("natural_log_exp_and_others")
            act.dma_start(sbmask[:, :, :], dr["sbmask"].rearrange("p (l t) -> p l t", t=P)).then_inc(S("sbmask_in"), 16)
            steps = [(h, b) for h in range(4) for b in range(NB - 1, -1, -1)]

            def soft(n):
                h, b = steps[n]
                z = pair(2 * (n % 2))[:, b * P:]
                a = ab[:, n % 2, b * P:]
                act.wait_ge(S("sb_z"), n + 1)
                if n >= 2:
                    act.wait_ge(S("sb_sp"), n - 1)
                fn(a, z, ACT.Abs)
                fn(a, a, ACT.Exp, scale=-1.0)
                fn(a, a, ACT.Ln, bias=1.0).then_inc(S("sb_ln"), 1)

            def take_out(h):
                act.wait_ge(S("sb_pv"), NB * (h + 1))
                q = slice(64 * (h % 2), 64 * (h % 2) + 64)
                copy(proj2[q, 9 + h // 2, :], pair(4 + 2 * (h // 2))[q, :]).then_inc(S("oc2_cp"), 1)

            soft(0)
            soft(1)
            for n, (h, b) in enumerate(steps):
                act.wait_ge(S("sb_r"), n + 1)
                if n >= 2:
                    act.wait_ge(S("sb_pv"), n - 1)
                fn(wts[:, n % 2, b * P:], pair(2 * (n % 2))[:, b * P:], ACT.Exp).then_inc(S("sb_w"), 1)
                if n + 2 < len(steps):
                    soft(n + 2)
                if h and b == NB - 2:
                    take_out(h - 1)
            take_out(3)

            for k in range(6):
                if k >= 2:
                    act.wait_ge(S("hn_mm"), k - 1)
                else:
                    act.wait_ge(S("o2_cp"), 9)
                fn(sq_h[:, k % 2, :], proj2[:, k, :], ACT.Square).then_inc(S("hn_sq"), 1)
            act.wait_ge(S("hn_var"), 1)
            fn(hn_r[:, :], hn_v[:, :], ACT.Sqrt).then_inc(S("hn_rstd"), 1)
            act.wait_ge(S("oc2_cp"), 4)
            for k in range(KT):
                if k >= 2:
                    act.wait_ge(S("gate_used"), k - 1)
                act.dma_start(gate_in[:, k % 2, :], gate_dram[k]).then_inc(S(f"gate_back{k % 2}"), 16)
            for k in range(KT):
                act.wait_ge(S("gate_used"), k + 1)
                copy(x_hi[:, k, :], o_a[k]).then_inc(S("x_hi_done"), 1)
            if stop <= 5:
                return

            act.wait_ge(S("x_lo_done"), 40)
            act.dma_start(x3[:, :, :], x2_dram.rearrange("p (k t) -> p k t", t=T)).then_inc(S("x2_back"), 16)
            for k in range(KT):
                g = G_OUT2 + k
                act.wait_ge(S("gemm_mm"), g + 1)
                copy(y2[:, k, :], pair(2 * (g % 2))).then_inc(S("gemm_evac"), 1)
            norm(5, lambda k: x3[:, k, :], lambda k: act.wait_ge(S("x3_done"), k + 1))
            for k in range(KT):
                act.wait_ge(S("out_done"), k + 1)
                act.dma_start(dr["out"][:, k * T:(k + 1) * T], y2[:, k, :]).then_inc(S("out_dma"), 16)
            act.wait_ge(S("out_dma"), 16 * KT)

        @block.vector
        def _(eng):
            dve = InOrder(eng)
            tt, ts, stt = (dve.op(f) for f in (nc.vector.tensor_tensor, nc.vector.tensor_scalar,
                                               nc.vector.scalar_tensor_tensor))
            vcopy, memset, reciprocal, scan, reduce_max, copy_pred = (dve.op(f) for f in (
                nc.vector.tensor_copy, nc.vector.memset, nc.vector.reciprocal, nc.vector.tensor_tensor_scan,
                nc.vector.reduce_max, nc.vector.copy_predicated))
            dve.wait_ge(S("cst_in"), 16)
            memset(par("rel_bias", p0=N_BUCKETS, p1=N_BUCKETS + 1), NEG).then_inc(S("neg_row"), 1)
            ts(sm["omka"], par("k_a"), -1.0, 1.0, ALU.mult, ALU.add)

            def norm_var(n):
                dve.wait_ge(S("norm_mm"), 8 * n + 8)
                ts(sm["var"], ps[:, 4, 0:8], EPS, None, ALU.add)
                reciprocal(sm["var"], sm["var"]).then_inc(S("var_inv"), 1)

            def low(n, k, src):
                dve.wait_ge(S("x_hi_done"), 8 * n + k + 1)
                tt(x_lo[:, k, :], src, x_hi[:, k, :].bitcast(F32), ALU.subtract).then_inc(S("x_lo_done"), 1)

            def apply(k, buf, src, gain, shift=None):
                i_ = stt(buf[:, k % 2, :], src(k), gain(k), rs_bc, ALU.mult, ALU.mult)
                if shift is not None:
                    i_
                    i_ = ts(buf[:, k % 2, :], buf[:, k % 2, :], shift(k), None, ALU.add)
                i_.then_inc(S("h_done"), 1)

            def apply_all(n_set, buf, src, gain, shift=None):
                for k in range(KT):
                    apply(k, buf, src, gain, shift)
                    if k:
                        low(n_set, k - 1, buf[:, (k - 1) % 2, :])
                low(n_set, KT - 1, buf[:, (KT - 1) % 2, :])

            def modulation(n):
                k, part = n // 3, n % 3
                dve.wait_ge(S(f"ada_in{n % ADA_RING}"), 16 * (n // ADA_RING + 1))
                acc, w = ada_acc[:, part, :], ada_w[:, n % ADA_RING, :]
                if k == 0:
                    i_ = ts(acc, w, sm["silu_c"][:, 0:1], None, ALU.mult)
                else:
                    i_ = stt(acc, w, sm["silu_c"][:, k:k + 1], acc, ALU.mult, ALU.add)
                i_.then_inc(S("ada_acc"), 1)

            dve.wait_ge(S("c_silu"), 1)
            for n in range(ADA_RING):
                modulation(n)
            norm_var(0)
            dve.wait_ge(S("rs_bcast"), 1)
            apply_all(0, nrm_a, lambda k: x_in[:, k, :], lambda k: par("g_mix_pre", k, 1))
            for n in range(ADA_RING, ADA_N):
                modulation(n)
            dve.wait_ge(S("ada_mm"), 1)
            tt(sm["ada"], ps[:, 7, 0:24], par("b_ada"), ALU.add)
            ts(sm["ada"][:, 8:16], sm["ada"][:, 8:16], 1.0, None, ALU.add).then_inc(S("ada_done"), 1)

            def shift(g, j, s):
                dve.wait_ge(S("gemm_evac"), g + 1)
                tt(dif[:, s, 1:], raw[:, s, 0:T - 1], raw[:, s, 1:], ALU.subtract)
                ts(dif[:, s, 0:1], raw[:, s, 0:1], -1.0, None, ALU.mult)
                if isinstance(j, int):
                    out, mix = proj[:, 6 + j, :], par("shift_mix", j, 1)
                else:
                    out, mix = proj[:, 6:20, :][:, bass.ds(j, 1), :].rearrange("p o t -> p (o t)"), \
                        par("shift_mix")[:, bass.ds(j, 1)]
                stt(out, dif[:, s, :], mix, raw[:, s, :], ALU.mult, ALU.add).then_inc(S("shift_done"), 1)

            shift(6, 0, 0)
            shift(7, 1, 1)
            with dve.Fori(1, 7) as i:
                for s in range(2):
                    j = dve.snap(2 * i + s)
                    shift(j + 6, j, s)
            if stop <= 1:
                return

            def attend(b, s, first=False):
                k0 = P if first else 0
                n = 2 * P - k0
                for g in range(2):
                    h4 = slice(4 * g, 4 * g + 4)
                    dve.wait_ge(S("att_mm"), 2 * b + g + 1)
                    if not first:
                        dve.wait_ge(S("attT_mm"), 2 * b + g - 1)
                    for x in range(2):
                        i_ = stt(sc[:, g, 2 * x:2 * x + 2, k0:],
                                 ps[:, 2 * g + x, :].rearrange("p (m k) -> p m k", k=256)[:, :, k0:], SCALE,
                                 bias[:, 4 * g + 2 * x:4 * g + 2 * x + 2, k0:], ALU.mult, ALU.add)
                    i_.then_inc(S("att_sc"), 1)
                    dve.wait_ge(S("att_sc"), 2 * b + g + 1)
                    reduce_max(sm["mx"][:, h4], sc[:, g, :, k0:], AX_X)
                    tt(sm["mx"][:, h4], sm["mx"][:, h4], par("sinks")[:, h4], ALU.max)
                    ts(sm["nm"][:, h4], sm["mx"][:, h4], -1.0, None, ALU.mult)
                    tt(sm["es"][:, h4], par("sinks")[:, h4], sm["mx"][:, h4], ALU.subtract).then_inc(S("att_max"), 1)
                for g in range(2):
                    h4 = slice(4 * g, 4 * g + 4)
                    dve.wait_ge(S("att_exp"), 2 * b + g + 1)
                    tt(sm["rec"][:, h4], sm["den"][:, h4], sm["es"][:, h4], ALU.add)
                    reciprocal(sm["rec"][:, h4], sm["rec"][:, h4])
                    tt(sc[:, g, :, k0:], sc[:, g, :, k0:], sm["rec"][:, h4].unsqueeze(2).to_broadcast([P, 4, n]),
                       ALU.mult).then_inc(S("att_p"), 1)

            dve.wait_ge(S("bias_in"), 16)
            attend(0, 0, first=True)
            attend(1, 1)
            with dve.Fori(1, 4) as i:
                for s in range(2):
                    attend(2 * i + s, s)
            if stop <= 2:
                return

            dve.wait_ge(S("smask_in"), 16)
            for m in range(4):
                dve.wait_ge(S("lora_sig"), m + 1)
                scan(cum[:, m, :], smask[:, :], ut[:, m % 2, :], 0.0, ALU.mult, ALU.add)\
                    .then_inc(S("cum_done"), 1)
                ts(kkn[:, m, :], proj[:, 10 + m, :], par("k_k", m, 1), None, ALU.mult).then_inc(S("kk_done"), 1)
            dve.wait_ge(S("kn_sqrt"), 1)
            ts(sm["kn"], sm["kn"], 1e-12, None, ALU.max)
            reciprocal(sm["kinv"], sm["kn"]).then_inc(S("kinv"), 1)
            for m in range(4):
                ts(tt_[:, m % 2, :], kka[:, m, :], par("k_a", m, 1), sm["omka"][:, m:m + 1], ALU.mult, ALU.add)
                tt(proj[:, 10 + m, :], proj[:, 10 + m, :], tt_[:, m % 2, :], ALU.mult)
                dve.wait_ge(S("kinv_bc"), m + 1)
                tt(kkn[:, m, :], kkn[:, m, :], pair(2 * (m % 2)), ALU.mult).then_inc(S("kkn_done"), 1)
                dve.wait_ge(S("kkn_done"), m + 1)
                tt(kka[:, m, :], kka[:, m, :], kkn[:, m, :], ALU.mult)
                stt(rk[:, m, :], proj[:, 6 + m, :], par("r_k", m, 1), proj[:, 10 + m, :], ALU.mult, ALU.mult)\
                    .then_inc(S("rk_done"), 1)

            dve.wait_ge(S("rk_done"), 4)
            dve.wait_ge(S("rmask_in"), 16)
            memset(e_neg[:, :, :, 0:1], 1.0)
            memset(st[:, 0, :, :], 0.0).then_inc(S("st_upd"), 1)
            m_ar = rmask[:, 0:2 * RC].unsqueeze(1).to_broadcast([P, 4, 2 * RC])

            def rm(k):
                return rmask[:, 2 * RC + k * RC:3 * RC + k * RC].unsqueeze(1).to_broadcast([P, 4, RC])

            def prepare(c, s):
                t = bass.ds(c * RC, RC)
                dve.wait_ge(S("ch_exp"), c + 1)
                stt(ar[:, s, :, 0, :], kkn[:, :, t], -1.0, e_neg[:, s, :, 0:RC], ALU.mult, ALU.mult)
                tt(ar[:, s, :, 1, :], proj[:, 6:10, t], e_neg[:, s, :, 1:], ALU.mult)
                tt(b_ch[:, s, :, :], kka[:, :, t], e_pos[:, s, :, :], ALU.mult)
                tt(k_ch[:, s, :, :], proj[:, 10:14, t], e_pos[:, s, :, :], ALU.mult).then_inc(S("ch_prep"), 1)

            def level_part(s, l):
                tt(lvl[:, s, l, :, :], m1[:, s, :, 0:RC], rm(2 + l), ALU.mult)

            def mask_first(i, s):
                dve.wait_ge(S("ch_mm"), 2 * i + s + 1)
                tt(m1[:, s, :, :], ps[:, 4 * s, :].rearrange("p (m c) -> p m c", c=2 * RC), m_ar, ALU.mult)
                tt(xx[:, s, 0, :, :], ps[:, 4 * s + 2, 0:256].rearrange("p (m c) -> p m c", c=RC), rm(0), ALU.mult)
                tt(xx[:, s, 0, :, :], xx[:, s, 0, :, :], rm(7), ALU.add)
                tt(xx[:, s, 1, :, :], m1[:, s, :, 0:RC], rm(1), ALU.mult)
                tt(xx[:, s, 1, :, :], xx[:, s, 1, :, :], rm(7), ALU.add)
                level_part(s, 1)
                tt(lvl[:, s, 0, :, :], m1[:, s, :, 0:RC], rm(2), ALU.mult).then_inc(S("ch_masked"), 1)

            def mask_rest(s):
                for l in range(2, 5):
                    level_part(s, l)
                tt(m2[:, s, :, :], ps[:, 4 * s + 1, :].rearrange("p (m c) -> p m c", c=2 * RC), m_ar, ALU.mult)
                vcopy(b_tok[:, s, :, :], ps[:, 4 * s + 2, 256:].rearrange("p (m c) -> p m c", c=RC))

            def chunk_pair(i, last=False):
                mask_first(i, 0)
                mask_rest(0)
                mask_first(i, 1)
                for l in range(5):
                    for s in range(2):
                        dve.wait_ge(S(f"x_mm{s}"), 5 * i + l + 1)
                        lo = 0 if l < 4 else 1
                        tt(xx[:, s, lo:, :, :], xx[:, s, lo:, :, :],
                           ps[:, 4 * s, 256 * lo:].rearrange("p (x m c) -> p x m c", m=4, c=RC), ALU.add)\
                            .then_inc(S(f"x_upd{s}"), 1)
                    if l == 0:
                        mask_rest(1)
                for s in range(2):
                    c = 2 * i + s
                    dve.wait_ge(S("u_mm"), c + 1)
                    vcopy(u_sb[:, :, :], ps[:, 6, 256:].rearrange("p (m c) -> p m c", c=RC))\
                        .then_inc(S("u_cp"), 1)
                    if s and not last:
                        prepare(c + 1, 0)
                    dve.wait_ge(S("ds_mm"), c + 1)
                    tt(st[:, 1 - s, :, :], st[:, s, :, :], ps[:, 6, 0:256].rearrange("p (m c) -> p m c", c=RC),
                          ALU.add)
                    tt(st[:, 1 - s, :, :], st[:, 1 - s, :, :], e_neg[:, s, :, RC:].to_broadcast([P, 4, RC]),
                       ALU.mult).then_inc(S("st_upd"), 1)
                if not last:
                    prepare(2 * i + 3, 1)

            for s in range(2):
                prepare(s, s)
            with dve.Fori(0, 7) as i:
                chunk_pair(i)
            chunk_pair(7, last=True)

            for m in range(4):
                dve.wait_ge(S("gn_sq"), m + 1)
                vcopy(o1[:, m, :], pair(2 * (m % 2))).then_inc(S("oc_done"), 1)
            dve.wait_ge(S("gn_mm"), 4)
            ts(sm["kn"], ps[:, 4, 0:64], GN_EPS, None, ALU.add)
            reciprocal(sm["kn"], sm["kn"]).then_inc(S("gn_var"), 1)
            dve.wait_ge(S("oc_done"), 4)
            for m in range(4):
                dve.wait_ge(S("fin_mm"), m + 1)
                stt(o1[:, m, :], o1[:, m, :], par("ln_g", m, 1), pair(0), ALU.mult, ALU.mult)
                tt(oc[:, m % 2, :], pair(2), proj[:, 14 + m, :], ALU.mult)
                stt(o1[:, m, :], o1[:, m, :], par("ln_b", m, 1), oc[:, m % 2, :], ALU.add, ALU.add)
                tt(o1[:, m, :], o1[:, m, :], pair(5), ALU.mult).then_inc(S("of_done"), 1)
            if stop <= 3:
                return

            for k in range(KT):
                low(1, k, mix_src[k])
            norm_var(1)
            dve.wait_ge(S("rs_bcast"), 2)
            dve.wait_ge(S("x_again"), 16)
            for k in range(KT):
                stt(nrm_a[:, k % 2, :], y1[:, k, :], par("g_mix_post", k, 1), rs_bc, ALU.mult, ALU.mult)
                tt(x1[:, k, :], x1[:, k, :], nrm_a[:, k % 2, :], ALU.add).then_inc(S("x1_done"), 1)
            norm_var(2)
            dve.wait_ge(S("rs_bcast"), 3)
            apply_all(2, nrm_a, lambda k: x1[:, k, :], lambda k: par("g_ffn_pre", k, 1))
            memset(f_acc[:, 0:8, :], 0.0)
            dve.sem_inc(S("prod"), 1)

            with dve.Fori(0, FFN_GROUPS) as gr:
                with dve.Fori(0, GROUP) as j:
                    p = dve.snap(GROUP * gr + j)
                    g = dve.snap(G_FFN + 3 * GROUP * gr + 2 * j)
                    for u, dst in enumerate((cg, cv)):
                        col = dve.snap(2 * p + u)
                        dve.wait_ge(S("conv_a"), 2 * p + u + 1)
                        stt(dst[:, 1:], pair(2 * u)[:, 0:T - 1], par("conv_w")[:, bass.ds(64 + col, 1)], dst[:, 1:],
                            ALU.mult, ALU.add)
                        stt(dst[:, 2:], pair(2 * u)[:, 0:T - 2], par("conv_w")[:, bass.ds(col, 1)], dst[:, 2:],
                            ALU.mult, ALU.add).then_inc(S("gemm_evac"), 1)
                    dve.wait_ge(S("gelu"), p + 1)
                    dve.wait_ge(S("gemm_evac"), g + 2)
                    tt(gv[:, :], cg[:, :], cv[:, :], ALU.mult).then_inc(S("prod"), 1)
                    dve.wait_ge(S("f_hi_done"), p + 1)
                    tt(f_lo[:, bass.ds(j, 1), :], gv[:, :].unsqueeze(1), f_hi[:, bass.ds(j, 1), :].bitcast(F32),
                       ALU.subtract).then_inc(S("f_lo_done"), 1)
                with dve.Fori(0, GROUP // 2) as j:
                    g = dve.snap(G_FFN + 3 * GROUP * gr + 2 * GROUP + 2 * j)
                    for u in range(2):
                        dve.wait_ge(S("gemm_mm"), g + u + 1)
                        f = f_acc[:, :, :].rearrange("p (k u) t -> p k u t", u=2)[:, bass.ds(j, 1), u, :]\
                            .rearrange("p o t -> p (o t)")
                        tt(f, f, pair(2 * u), ALU.add).then_inc(S("gemm_evac"), 1)
            norm_var(3)
            dve.wait_ge(S("rs_bcast"), 4)
            dve.wait_ge(S("x1_back"), 16)
            for k in range(KT):
                stt(nrm_b[:, k % 2, :], f_acc[:, k, :], par("g_ffn_post", k, 1), rs_bc, ALU.mult, ALU.mult)
                tt(x2[:, k, :], x2[:, k, :], nrm_b[:, k % 2, :], ALU.add).then_inc(S("x2_done"), 1)
            norm_var(4)
            dve.wait_ge(S("rs_bcast"), 5)
            apply_all(3, nrm_b, lambda k: x2[:, k, :], lambda k: sm["ada"][:, 8 + k:9 + k],
                      lambda k: sm["ada"][:, k:k + 1])
            if stop <= 4:
                return

            tt(sm["lb_d"], par("lb"), par("lb"), ALU.subtract).then_inc(S("lb_d"), 1)
            dve.wait_ge(S("lb_e"), 1)
            reciprocal(sm["lb"], sm["lb_e"])
            tt(sm["lb_e"], sm["lb"], sm["lb_e"], ALU.mult)
            tt(sm["lb"], sm["lb_e"], sm["lb_e"], ALU.subtract)
            ts(sm["omlb"], sm["lb"], -1.0, 1.0, ALU.mult, ALU.add)
            dve.wait_ge(S("smask2_in"), 16)
            for m in range(4):
                dve.wait_ge(S("ls_ln"), m + 1)
                if m < 2:
                    src, b_ = pair(2 * m), par("b_gla", m, 1)
                else:
                    src, b_ = proj2[:, 4 + m, :], 0.0
                ts(g5[:, m % 2, :], src, b_, 0.0, ALU.add, ALU.min)
                if m < 2:
                    tt(g5[:, m % 2, :], g5[:, m % 2, :], g4[:, m % 2, :], ALU.subtract)
                    ts(g5[:, m % 2, :], g5[:, m % 2, :], 1.0 / 16.0, None, ALU.mult)
                else:
                    dve.wait_ge(S("lbt_exp"), m - 1)
                    ts(lbt[:, m % 2, :], lbt[:, m % 2, :], 1e18, None, ALU.min).then_inc(S("lbt_min"), 1)
                    tt(g5[:, m % 2, :], g5[:, m % 2, :], g4[:, m % 2, :], ALU.subtract).then_inc(S("fb_read"), 1)
                    dve.wait_ge(S("fb_read"), m - 1)
                    dve.wait_ge(S("lbt_ln"), m - 1)
                    tt(g5[:, m % 2, :], g5[:, m % 2, :], lbt[:, m % 2, :], ALU.add)
                scan(c4[:, m, :], smask2[:, :], g5[:, m % 2, :], 0.0, ALU.mult, ALU.add)\
                    .then_inc(S("lsig"), 1)
                if m >= 2:
                    dve.wait_ge(S("kb_sig"), m - 1)
                    ts(proj2[:, 4 + m, :], proj2[:, 4 + m, :], sm["omlb"][:, m - 2:m - 1], None, ALU.mult)\
                        .then_inc(S("kb_done"), 1)

            dve.wait_ge(S("lsig"), 4)
            dve.wait_ge(S("gmask_in"), 16)
            memset(s_m[:, :, :, :], 0.0)
            memset(st2[:, :], 0.0)
            dve.sem_inc(S("st2_upd"), 1)
            dve.sem_inc(S("lev_cp"), 2)

            def update_state(b, s):
                dve.wait_ge(S("ds2_mm"), b + 2)
                dve.wait_ge(S("ecl_done"), b + 1)
                dve.wait_ge(S("o2_mm"), b + 1)
                for m in range(4):
                    w, at0 = (P, m * P) if m < 2 else (64, 256 + (m - 2) * 64)
                    i_ = stt(st2[:, at0:at0 + w], st2[:, at0:at0 + w], sm["ecl"][:, 4 * s + m:4 * s + m + 1],
                             ps[:, 7, at0:at0 + w], ALU.mult, ALU.add)
                i_.then_inc(S("st2_upd"), 1)

            def gla_block(b, s, first=False, last=False):
                def level_into_scores(l):
                    dve.wait_ge(S("lev_mm"), 8 * b + l + 3)
                    ts(sm["took_v"], sm["one"], 1.0, None, ALU.mult)
                    for x in range(2):
                        out, mask = s_m[:, s, 4 * x:4 * x + 4, :], gmask[:, l:l + 1, :].bitcast(U32)
                        if l < 7:
                            w = P >> l
                            n = P // w
                            i_ = copy_pred(
                                out.rearrange("p h (n w) -> p h n w", w=w)[:, :, :, w // 2:],
                                mask.rearrange("p h (n w) -> p h n w", w=w)[:, :, :, w // 2:].to_broadcast([P, 4, n, w // 2]),
                                ps[:, 2 * (l % 2) + x, 0:256].rearrange("p (h n w) -> p h n w", h=4, n=n))
                        else:
                            i_ = copy_pred(out, mask.to_broadcast([P, 4, P]),
                                           ps[:, 2 * (l % 2) + x, :].rearrange("p (h t) -> p h t", t=P))
                    i_.then_inc(S("lev_cp"), 1)

                dve.wait_ge(S("e_done"), 8 * b + 1)
                dve.wait_ge(S("ds2_mm"), b + 1)
                tt(kh[:, :, :], e_end[:, :, :], k_b[:, s, :, :], ALU.mult).then_inc(S("kh_done"), 1)
                tt(qe[:, s, :, :], qe[:, s, :, :], q_b[:, s, :, :], ALU.mult)
                for l in range(7):
                    hw = 64 >> l
                    dve.wait_ge(S("e_done"), 8 * b + l + 2)
                    dve.wait_ge(S("lev_mm"), 8 * b + l + 1)
                    z, e = blocks(zz[:, l % 2, :, :], 2 * hw), blocks(e7[:, s, l, :, :], 2 * hw)
                    tt(z[:, :, 0:hw], blocks(k_b[:, s, :, :], 2 * hw)[:, :, 0:hw], e[:, :, 0:hw], ALU.mult)
                    tt(z[:, :, hw:], blocks(q_b[:, s, :, :], 2 * hw)[:, :, hw:], e[:, :, hw:], ALU.mult)\
                        .then_inc(S("z_done"), 1)
                    if l:
                        level_into_scores(l - 1)
                    if l == 3 and not first:
                        update_state(b - 1, 1 - s)
                level_into_scores(6)
                level_into_scores(7)

            gla_block(0, 0, first=True)
            gla_block(1, 1)
            with dve.Fori(1, NB // 2 - 1) as i:
                for s in range(2):
                    gla_block(2 * i + s, s)
            gla_block(NB - 2, 0)
            gla_block(NB - 1, 1, last=True)

            dve.wait_ge(S("sbmask_in"), 16)
            steps = [(h, b) for h in range(4) for b in range(NB - 1, -1, -1)]

            def soft(n):
                h, b = steps[n]
                dve.wait_ge(S("sb_ln"), n + 1)
                if n >= 2:
                    dve.wait_ge(S("sb_r"), n - 1)
                stt(spl[:, n % 2, b * P:], pair(2 * (n % 2))[:, b * P:], 0.0, ab[:, n % 2, b * P:], ALU.max, ALU.add)
                d = spl[:, n % 2, b * P:(b + 1) * P]
                tt(d, d, sbmask[:, 2, :], ALU.mult).then_inc(S("sb_sp"), 1)

            soft(0)
            soft(1)
            for n, (h, b) in enumerate(steps):
                dve.wait_ge(S("sb_r"), n + 1)
                dve.wait_ge(S("sb_sp"), n + 1)
                if b < NB - 1:
                    tt(lacc[:, (b + 1) * P:], lacc[:, (b + 1) * P:], spl[:, n % 2, (b + 1) * P:], ALU.add)
                vcopy(lacc[:, b * P:(b + 1) * P], spl[:, n % 2, b * P:(b + 1) * P])\
                    .then_inc(S("sb_acc"), 1)
                dve.wait_ge(S("sb_w"), n + 1)
                d = wts[:, n % 2, b * P:(b + 1) * P]
                tt(d, d, sbmask[:, 2, :], ALU.mult).then_inc(S("sb_wm"), 1)
                if n + 2 < len(steps):
                    soft(n + 2)

            dve.wait_ge(S("hn_mm"), 6)
            ts(hn_v[:, :], ps[:, 0, 0:96], EPS, None, ALU.add)
            reciprocal(hn_v[:, :], hn_v[:, :]).then_inc(S("hn_var"), 1)
            dve.wait_ge(S("oc2_cp"), 4)
            for k in range(KT):
                if k < 6:
                    dve.wait_ge(S("hn_bc"), k + 1)
                    w = par("gla_w") if k < 4 else par("hgrn_w")
                    stt(o_a[k], proj2[:, k, :], w, pair(2 + 2 * (k % 2)), ALU.mult, ALU.mult)\
                        .then_inc(S("hn_out"), 1)
                    dve.wait_ge(S("hn_out"), k + 1)
                    src = o_a[k]
                else:
                    src = proj2[:, 9 + k - 6, :]
                dve.wait_ge(S(f"gate_back{k % 2}"), 16 * (k // 2 + 1))
                tt(o_a[k], src, gate_in[:, k % 2, :], ALU.mult).then_inc(S("gate_used"), 1)
            for k in range(KT):
                low(4, k, o_a[k])
            if stop <= 5:
                return

            dve.wait_ge(S("x2_back"), 16)
            for k in range(KT):
                dve.wait_ge(S("gemm_evac"), G_OUT2 + k + 1)
                stt(x3[:, k, :], y2[:, k, :], sm["ada"][:, 16 + k:17 + k], x3[:, k, :], ALU.mult, ALU.add)\
                    .then_inc(S("x3_done"), 1)
            norm_var(5)
            dve.wait_ge(S("rs_bcast"), 6)
            for k in range(KT):
                stt(y2[:, k, :], x3[:, k, :], par("final_w", k, 1), rs_bc, ALU.mult, ALU.mult).then_inc(S("out_done"), 1)


def kernel(**inputs):
    import concourse.bacc as bacc
    from concourse.bass_utils import run_bass_kernel_spmd

    f = {k: np.asarray(v) for k, v in inputs.items()}

    def tiles(w):
        k, n = w.shape
        return w.reshape(KT, P, n // P, P).transpose(2, 1, 0, 3).reshape(n // P, P, KT * P)

    def cols(v):
        return v.reshape(-1, P).T

    pair_up = np.concatenate([np.arange(64) + 64 * h for m in range(4) for h in (m, m + 4)])
    w_in = f["w_in"][0]
    w_q, w_rest = w_in[:, :512][:, pair_up], w_in[:, 512:]
    w_out = np.concatenate([f["w_out"][0][:512][pair_up], f["w_out"][0][512:]], 0)
    up = tiles(f["w_ffn_up"][0])
    down = f["w_ffn_down"][0].reshape(FFN_GROUPS, GROUP * P, D)
    ffn = []
    for g in range(FFN_GROUPS):
        for j in range(GROUP):
            ffn += [up[GROUP * g + j], up[32 + GROUP * g + j]]
        ffn += list(tiles(down[g]))
    w2 = f["w_in_2"][0]
    widths = (256, 256, 512, 16, 512, 256, 256, 256, 256, 256, 256, 256, 256)
    part = dict(zip(("qa", "ka", "va", "lr", "ga", "qb", "fb", "ib", "gb", "qc", "kc", "vc", "gc"),
                    np.split(w2, np.cumsum(widths)[:-1], axis=1)))
    part["lr"] = np.concatenate([part["lr"], np.zeros((D, P - 16), np.float32)], 1)
    in2 = np.concatenate([part[n] for n in ("ga", "gb", "gc", "qa", "qb", "ka", "fb", "lr", "qc", "kc", "va", "ib", "vc")], 1)
    wall = np.concatenate([tiles(np.concatenate([w_q, w_rest], 1)), tiles(w_out), np.stack(ffn), tiles(in2),
                           tiles(f["w_out_2"][0])], 0)[:N_TILES]

    n = np.arange(P)
    half = (n[:, None] // 64 == n[None, :] // 64).astype(np.float32)
    rel = 255 - np.arange(384)
    nn = np.maximum(rel, 0)
    exact = N_BUCKETS // 2
    large = exact + (np.log(np.maximum(nn, 1).astype(np.float32) / np.float32(exact))
                     / np.float32(np.log(MAX_DISTANCE / exact)) * np.float32(N_BUCKETS - exact)).astype(np.int32)
    bucket = np.where(nn < exact, nn, np.minimum(large, N_BUCKETS - 1))
    bucket = np.where((rel >= 0) & (rel < P), bucket, N_BUCKETS)
    onehot = np.zeros((P, 384), np.float32)
    onehot[bucket, np.arange(384)] = 1
    rel_bias = np.zeros((P, 8), np.float32)
    rel_bias[:N_BUCKETS] = f["rel_bias"]
    w_gla2 = np.zeros((P, 256), np.float32)
    w_gla2[:16] = f["w_gla_gate2_2"][0]
    cw, cb = f["conv_w"][0], f["conv_b"][0]

    def gate_val(v):
        return np.stack([cols(v[:4096]), cols(v[4096:])], 2).reshape(P, 64)

    values = dict(
        g_mix_pre=cols(f["norm_mix_pre"][0]), g_mix_post=cols(f["norm_mix_post"][0]),
        g_ffn_pre=cols(f["norm_ffn_pre"][0]), g_ffn_post=cols(f["norm_ffn_post"][0]),
        shift_mix=cols(f["rwkv_shift_mix"][0]), w0=cols(f["w0"][0]), a0=cols(f["a0"][0]), k_k=cols(f["k_k"][0]),
        k_a=cols(f["k_a"][0]), r_k=cols(f["r_k"][0].reshape(-1)), ln_g=cols(f["ln_x_g"][0]), ln_b=cols(f["ln_x_b"][0]),
        conv_w=np.concatenate([gate_val(cw[j]) for j in range(3)], 1), conv_b=gate_val(cb),
        b_ada=cols(f["b_ada_2"][0]), c=cols(f["c_2"][0]), b_gla=cols(f["b_gla_gate_2"][0]),
        gla_w=f["gla_norm_w_2"][0][:, None], hgrn_w=np.tile(f["hgrn_norm_w_2"][0], 2)[:, None],
        lb=cols(f["hgrn_lb_logits_2"][0]), final_w=cols(f["final_norm_w_2"]),
        sinks=np.broadcast_to(f["sinks"][0][None, :], (P, 8)),
        ident=np.eye(P, dtype=np.float32), halves=half, center=np.eye(P, dtype=np.float32) - half / 64,
        mean_all=np.full((P, 1), 1 / D, np.float32), mean2=np.full((P, 2), 1 / P, np.float32),
        mean_half=half[:, ::64] / 64,
        w_lora=np.concatenate([f["w_decay_up"][0], f["w_iclr_up"][0]], 0), w_gate=f["w_gate_up"][0],
        w_gla2=w_gla2, onehot=onehot, rel_bias=rel_bias)
    cst = np.concatenate([values[name] for name, _ in PARAMS], 1).astype(np.float32)

    t = np.arange(RC)
    row, col = t[:, None], t[None, :]

    def level(h):
        m = np.arange(P)
        a, b = m[:, None], m[None, :]
        return (a // (2 * h) == b // (2 * h)) & (a // h % 2 == 0) & (b // h % 2 == 1)

    lv = {h: level(h) for h in (1, 2, 4, 8, 16, 32, 64)}
    rmask = np.concatenate([row < col, row <= col, lv[1][:RC, :RC].T] + [lv[h][:RC, :RC] for h in (1, 2, 4, 8, 16, 32)]
                           + [row == col], 1)
    rmask = np.tile(rmask, (2, 1)).astype(np.float32)
    gmask = np.concatenate([lv[64 >> i] for i in range(7)] + [np.eye(P, dtype=bool)], 1).astype(np.float32)
    sbmask = np.concatenate([-(n[:, None] >= n[None, :]).astype(np.float32), -np.ones((P, P), np.float32),
                             (n[:, None] < n[None, :]).astype(np.float32)], 1)
    scan = np.concatenate([np.tile((np.arange(T) % w != 0).astype(np.float32), (P, 1)) for w in (RC, P)], 1)

    arrays = dict(
        wall=wall, wada=f["w_ada_2"][0].reshape(KT, P, 3, D).transpose(0, 2, 1, 3).reshape(3 * KT, P, D), cst=cst, rmask=rmask, gmask=gmask, sbmask=sbmask, scan=scan,
        xT=f["x"][0].T.reshape(KT, P, T).transpose(1, 0, 2).reshape(P, KT * T))
    arrays = {k: np.ascontiguousarray(v) for k, v in arrays.items()}
    nc = bacc.Bacc("TRN2", target_bir_lowering=False, num_devices=1)
    dr = {k: nc.dram_tensor(k, v.shape, mybir.dt.from_np(v.dtype), kind="ExternalInput").ap() for k, v in arrays.items()}
    dr["out"] = nc.dram_tensor("out", (P, KT * T), F32, kind="ExternalOutput").ap()
    build(nc, dr)
    out = run_bass_kernel_spmd(nc, [arrays], core_ids=[0]).results[0]["out"]
    return np.ascontiguousarray(np.asarray(out).reshape(P, KT, T).transpose(2, 1, 0).reshape(1, T, D))
```

```python
from contextlib import ExitStack, contextmanager

import numpy as np

import concourse.bass as bass
from concourse import mybir

ACT = mybir.ActivationFunctionType
ALU = mybir.AluOpType
F32 = mybir.dt.float32
F32R = mybir.dt.float32r
U32 = mybir.dt.uint32
AX_X = mybir.AxisListType.X

P = 128
T = 1024
D = 1024
KT = D // P
NB = T // P
RC = 64
NEG = -1e30
EPS = 1e-6
GN_EPS = 64e-5
DECAY = float(np.exp(-0.5))
SCALE = 64 ** -0.5
N_BUCKETS, MAX_DISTANCE = 32, 128

G_IN, G_OUT, G_FFN = 0, 20, 28
FFN_GROUPS, GROUP = 4, 8
G_IN2 = G_FFN + FFN_GROUPS * 3 * GROUP
N_GATE2, N_CHAN2, N_TOK2 = 8, 13, 8
G_OUT2 = G_IN2 + N_GATE2 + N_CHAN2 + N_TOK2
N_TILES = G_OUT2 + 8

UNIT = 4096
BASE = 16640

PARAMS = [("g_mix_pre", 8), ("g_mix_post", 8), ("g_ffn_pre", 8), ("g_ffn_post", 8), ("shift_mix", 14),
          ("w0", 4), ("a0", 4), ("k_k", 4), ("k_a", 4), ("r_k", 4), ("ln_g", 4), ("ln_b", 4),
          ("conv_w", 3 * 64), ("conv_b", 64), ("b_ada", 24), ("c", 8), ("b_gla", 2), ("gla_w", 1),
          ("hgrn_w", 1), ("lb", 2), ("final_w", 8), ("sinks", 8),
          ("ident", 128), ("halves", 128), ("center", 128), ("mean_all", 1), ("mean2", 2), ("mean_half", 2),
          ("w_lora", 512), ("w_gate", 512), ("w_gla2", 256), ("onehot", 384), ("rel_bias", 8)]
COL = {}
for _n, _w in PARAMS:
    COL[_n] = (sum(w for _, w in COL.values()), _w)
N_COL = sum(w for _, w in COL.values())
N_RMASK = 2 * RC + RC + 6 * RC + RC


class InOrder:

    def __init__(self, eng):
        self.eng, self.busy = eng, False
        self.dma_start, self.snap, self.sem_inc = eng.dma_start, eng.snap, eng.sem_inc

    def settle(self):
        if self.busy:
            self.eng.drain()
            self.busy = False

    def wait_ge(self, sem, value):
        self.settle()
        self.eng.wait_ge(sem, value)

    def op(self, emit):
        def run(*args, **kw):
            self.settle()
            self.busy = True
            return emit(*args, **kw)
        return run

    @contextmanager
    def Fori(self, lo, hi):
        self.settle()
        with self.eng.Fori(lo, hi) as i:
            yield i
            self.settle()


def build(nc, dr, stop=99):
    with ExitStack() as ctx:
        sems = {}

        def S(name):
            if name not in sems:
                sems[name] = ctx.enter_context(nc.semaphore(name))
            return sems[name]

        def at(name, shape, unit, dt=F32, off=0):
            return nc.alloc_sbuf_tensor_at(name, shape, dt, offset=BASE + int(unit * UNIT) + off)

        w_raw = at("w_raw", [P, 2, KT, P], 0)
        w_hi = at("w_hi", [P, 2, KT, P], 2, F32R)
        w_lo = at("w_lo", [P, 2, KT, P], 4, F32R)
        x_hi = at("x_hi", [P, KT, T], 6, F32R)
        x_lo = at("x_lo", [P, KT, T], 14, F32R)
        f_hi = at("f_hi", [P, GROUP, T], 22, F32R)
        f_lo = at("f_lo", [P, GROUP, T], 30, F32R)
        cst = at("cst", [P, N_COL], 49)
        small = at("small", [P, 256], 49, off=-(-4 * N_COL // 32) * 32)
        assert 4 * (N_COL + 256) <= 229368 - BASE - 49 * UNIT

        def par(name, a=0, n=None, p0=0, p1=P):
            c, w = COL[name]
            return cst[p0:p1, c + a:c + a + (w - a if n is None else n)]


        class Places:

            def __init__(self, *runs):
                self.runs = [[BASE + a * UNIT, BASE + b * UNIT] for a, b in runs]

            def __call__(self, name, shape, dt=F32, size=4):
                need = -(-int(np.prod(shape[1:])) * size // 32) * 32
                run = next(r for r in self.runs if r[1] - r[0] >= need)
                run[0] += need
                return nc.alloc_sbuf_tensor_at(name, shape, dt, offset=run[0] - need)

        x_in = at("x_in", [P, KT, T], 22)
        sq_a = at("sq_a", [P, 2, T], 42)
        nrm_a = at("nrm_a", [P, 2, T], 44)
        sq_b = at("sq_b", [P, 2, T], 30)
        nrm_b = at("nrm_b", [P, 2, T], 32)
        proj = at("proj", [P, 20, T], 22)
        raw = at("raw", [P, 2, T], 42)
        dif = at("dif", [P, 2, T], 44)
        ADA_RING, ADA_N = 6, 3 * KT
        ada_w = at("ada_w", [P, ADA_RING, T], 33)
        ada_acc = at("ada_acc", [P, 3, T], 39)

        bias = at("bias", [P, 8, 256], 47)
        bias_row = at("bias_row", [P, 384], 46)
        pl = Places((6, 14))
        sc = pl("sc", [P, 2, 4, 256])
        pT = pl("pT", [P, 2, 2, 512])
        q_st = pl("q_st", [P, 2, 4, P])
        k_st = pl("k_st", [P, 2, 2 * P])
        v_st = pl("v_st", [P, 2, 2, P])

        kkn = at("kkn", [P, 4, T], 6)
        kka = at("kka", [P, 4, T], 10)
        cum = at("cum", [P, 4, T], 14)
        rk = at("rk", [P, 4, T], 18)
        smask = at("smask", [P, T], 46)
        ut = at("ut", [P, 2, T], 42)
        tt_ = at("tt_", [P, 2, T], 44)
        rmask = Places((40, 41))("rmask", [P, N_RMASK])
        pl = Places((18, 22), (26, 28), (42, 49))
        lvl = pl("lvl", [P, 2, 5, 4, RC])
        xx = pl("xx", [P, 2, 2, 4, RC])
        m1 = pl("m1", [P, 2, 4, 2 * RC])
        m2 = pl("m2", [P, 2, 4, 2 * RC])
        ar = pl("ar", [P, 2, 4, 2, RC])
        e_neg = pl("e_neg", [P, 2, 4, RC + 1])
        e_pos = pl("e_pos", [P, 2, 4, RC])
        b_ch = pl("b_ch", [P, 2, 4, RC])
        k_ch = pl("k_ch", [P, 2, 4, RC])
        v_ch = pl("v_ch", [P, 2, 4, RC])
        vk_tok = pl("vk_tok", [P, 2, 2, 4, RC])
        b_tok = pl("b_tok", [P, 2, 4, RC])
        y_sb = pl("y_sb", [P, 2, 4, RC])
        rhs = pl("rhs", [P, 4, RC])
        u_sb = pl("u_sb", [P, 4, RC])
        st = pl("st", [P, 2, 4, RC])
        o1 = proj[:, 6:10, :]
        rk2 = at("rk2", [P, 4, T], 18)
        oc = at("oc", [P, 2, T], 42)
        osq = at("osq", [P, 2, T], 44)

        y1 = at("y1", [P, KT, T], 22)
        x1 = at("x1", [P, KT, T], 30)
        f_acc = at("f_acc", [P, KT, T], 38)
        cg = at("cg", [P, T], 46)
        cv = at("cv", [P, T], 47)
        gv = at("gv", [P, T], 48)
        x2 = at("x2", [P, KT, T], 22)

        proj2 = at("proj2", [P, N_CHAN2, T], 22)
        v2 = at("v2", [P, 8, NB, P], 35)
        gate_st = at("gate_st", [P, 2, T], 43)
        to_turn = at("to_turn", [P, 2, T], 45)
        ls_t = at("ls_t", [P, 2, T], 43)
        la = at("la", [P, 2, T], 47)
        c4 = at("c4", [P, 4, T], 6)
        smask2 = at("smask2", [P, T], 10)
        g4 = at("g4", [P, 2, T], 12)
        g5 = at("g5", [P, 2, T], 14)
        lbt = at("lbt", [P, 2, T], 16)
        pl = Places((10, 22), (43, 49))
        e7 = pl("e7", [P, 2, 7, 4, P])
        s_m = pl("s_m", [P, 2, 8, P])
        zz = pl("zz", [P, 2, 4, P])
        v_b = pl("v_b", [P, 2, 6, P])
        st2 = pl("st2", [P, 384])
        c_b = pl("c_b", [P, 2, 4, P])
        q_b = pl("q_b", [P, 2, 4, P])
        k_b = pl("k_b", [P, 2, 4, P])
        qe = pl("qe", [P, 2, 4, P])
        gmask = pl("gmask", [P, 8, P])
        kh = pl("kh", [P, 4, P])
        e_end = pl("e_end", [P, 4, P])
        pl = Places((10, 22), (43, 49))
        sbmask = pl("sbmask", [P, 3, P])
        ab = pl("ab", [P, 2, T])
        spl = pl("spl", [P, 2, T])
        wts = pl("wts", [P, 2, T])
        lacc = pl("lacc", [P, T])
        sq_h = at("sq_h", [P, 2, T], 43)
        hn_v = at("hn_v", [P, 96], 45)
        hn_r = at("hn_r", [P, 96], 45, off=512)
        gate_in = at("gate_in", [P, 2, T], 46)
        y2 = at("y2", [P, KT, T], 22)
        x3 = at("x3", [P, KT, T], 30)

        ps = ctx.enter_context(nc.psum_tensor("ps", [P, 8, 512], F32))

        def pair(b):
            return ps[:, b:b + 2, :].rearrange("p a b -> p (a b)")

        def rs_of(n):
            return pair(4 + 2 * (n % 2))

        sm = {}
        for name, w in (("eps", 1), ("silu_c", 8), ("ada", 24), ("omka", 4), ("kn", 64), ("kinv", 64),
                        ("mx", 8), ("nm", 8), ("es", 8), ("den", 8), ("rec", 8), ("lb_d", 2), ("lb_e", 2), ("lb", 2), ("omlb", 2), ("ecl", 8), ("one", 1), ("took", 1), ("took_v", 1)):
            at0 = sum(v.shape[-1] for v in sm.values())
            sm[name] = small[:, at0:at0 + w]

        x1_dram = nc.dram_tensor("x1_spill", (P, KT * T), F32).ap()
        x2_dram = nc.dram_tensor("x2_spill", (P, KT * T), F32).ap()
        bias_dram = nc.dram_tensor("bias_table", (8, P, 384), F32).ap()
        rk_dram = nc.dram_tensor("rk_spill", (P, 4 * T), F32).ap()
        gate_dram = nc.dram_tensor("gate_spill", (8, P, T), F32).ap()

        sq_of = {0: sq_a, 1: sq_a, 2: sq_a, 3: sq_b, 4: sq_b, 5: sq_a}
        pairs_a, pairs_b, pairs_c = (at(f"pairs_{u}", [P, 2, T], u) for u in (30, 38, 34))
        pairs_of = {0: pairs_a, 1: pairs_b, 2: pairs_b, 3: pairs_c, 4: pairs_c, 5: pairs_b}

        mix_src = [proj[:, k, :] for k in range(4)] + [o1[:, k, :] for k in range(4)]
        o_a = [proj2[:, k, :] for k in range(6)] + [proj2[:, 9 + k, :] for k in range(2)]

        def reach(l):
            return (P // 2, 3 * P // 4)[l] if l < 2 else P

        def blocks(x, w):
            return x.rearrange("p a (n w) -> p (a n) w", w=w)

        block = ctx.enter_context(nc.Block())

        @block.sync
        def _(sp):
            def load(g, u):
                return sp.dma_start(w_raw[:, u, :, :], g.rearrange("o p (k c) -> p (o k) c", c=P))

            for u in range(2):
                load(dr["wall"][u:u + 1], u).then_inc(S(f"w_in{u}"), 16)
            with sp.Fori(1, N_TILES // 2) as i:
                for u in range(2):
                    g = sp.snap(2 * i + u)
                    src = dr["wall"][bass.ds(g, 1)]
                    sp.wait_ge(S("w_split"), 2 * i + u - 1)
                    load(src, u).then_inc(S(f"w_in{u}"), 16)
            if N_TILES % 2:
                sp.wait_ge(S("w_split"), N_TILES - 2)
                load(dr["wall"][N_TILES - 1:N_TILES], 0).then_inc(S("w_in0"), 16)

        @block.gpsimd
        def _(pool):
            def split(g, u, turn, first=False):
                pool.wait_ge(S(f"w_in{u}"), turn * 16)
                if not first:
                    pool.wait_ge(S("gemm_mm"), g - 1)
                nc.gpsimd.tensor_tensor(w_hi[:, u, :, :], w_raw[:, u, :, :],
                                        sm["one"].unsqueeze(2).to_broadcast([P, KT, P]), ALU.mult).then_inc(S("w_hi_done"), 1)
                pool.wait_ge(S("w_hi_done"), g + 1)
                nc.gpsimd.tensor_tensor(w_lo[:, u, :, :], w_raw[:, u, :, :], w_hi[:, u, :, :].bitcast(F32),
                                        ALU.subtract).then_inc(S("w_split"), 1)

            nc.gpsimd.memset(sm["eps"], EPS)
            nc.gpsimd.memset(sm["one"], 1.0).then_inc(S("one"), 1)
            pool.wait_ge(S("one"), 1)
            for u in range(2):
                split(u, u, 1, first=True)
            last = G_OUT2 + 1
            with pool.Fori(1, last // 2) as i:
                for u in range(2):
                    split(2 * i + u, u, i + 1)
            split(last, last % 2, last // 2 + 1)

            def exponents(b, s, first=False):
                pool.wait_ge(S("blk_stage"), b + 1)
                if not first:
                    pool.wait_ge(S("kh_done"), b)
                tt = nc.gpsimd.tensor_tensor
                tt(e_end[:, :, :], c_b[:, s, :, P - 1:P].to_broadcast([P, 4, P]), c_b[:, s, :, :], ALU.subtract)\
                    .then_inc(S("d_done"), 1)
                for l in range(7):
                    hw = 64 >> l
                    e, c_ = blocks(e7[:, s, l, :, :], 2 * hw), blocks(c_b[:, s, :, :], 2 * hw)
                    ref = c_[:, :, hw - 1:hw].to_broadcast([P, 4 * P // (2 * hw), hw])
                    tt(e[:, :, 0:hw], ref, c_[:, :, 0:hw], ALU.subtract).then_inc(S("d_done"), 1)
                    tt(e[:, :, hw:], c_[:, :, hw:], ref, ALU.subtract).then_inc(S("d_done"), 1)

            exponents(0, 0, first=True)
            exponents(1, 1)
            with pool.Fori(1, NB // 2) as i:
                for s in range(2):
                    exponents(2 * i + s, s)

            for g in range(last + 1, last + 2 + last % 2):
                split(g, g % 2, g // 2 + 1)
            with pool.Fori((last + 2 + last % 2) // 2, N_TILES // 2) as i:
                for u in range(2):
                    split(2 * i + u, u, i + 1)
            for g in range(N_TILES // 2 * 2, N_TILES):
                split(g, g % 2, g // 2 + 1)

        @block.tensor
        def _(pe):
            mm = nc.tensor.matmul

            def hold(sem, value):
                pe.wait_ge(S("cst_in"), 16)
                pe.wait_ge(sem, value)

            def gemm(g, u, hi, lo, first=False, parts=None):
                pe.wait_ge(S("w_split"), g + 1)
                if not first:
                    pe.wait_ge(S("gemm_evac"), g - 1)
                for k in range(KT):
                    if parts is not None:
                        pe.wait_ge(S(parts[0]), parts[1] + (k + 1))
                    for w, x in ((w_hi, hi), (w_hi, lo), (w_lo, hi)):
                        for h in range(2):
                            last = mm(ps[:, 2 * u + h, :], w[:, u, k, :], x[:, k, h * 512:(h + 1) * 512],
                                      start=(k == 0 and w is w_hi and x is hi),
                                      stop=(k == KT - 1 and w is w_lo))
                last.then_inc(S("gemm_mm"), 1)

            def turn(src, b0):
                for t in range(NB):
                    last = nc.tensor.transpose(ps[:, b0 + t // 4, (t % 4) * P:(t % 4 + 1) * P],
                                               src[:, t * P:(t + 1) * P], par("ident"))
                last.then_inc(S("turn_mm"), 1)

            def norm_sum(n):
                for j in range(KT // 2):
                    pe.wait_ge(S("norm_pair"), 4 * n + j + 1)
                    for h in range(2):
                        last = mm(rs_of(n)[:, h * 512:(h + 1) * 512], par("mean_all").to_broadcast([P, P]),
                                  pairs_of[n][:, j % 2, h * 512:(h + 1) * 512], start=(j == 0), stop=(j == 3),
                                  skip_group_check=True)
                    last.then_inc(S("norm_mm"), 1)

            pe.wait_ge(S("cst_in"), 16)
            pe.wait_ge(S("neg_row"), 1)
            mm(ps[0:8, 0, 0:384], par("rel_bias", p1=N_BUCKETS + 1), par("onehot", p1=N_BUCKETS + 1),
               start=True, stop=True).then_inc(S("bias_mm"), 1)
            norm_sum(0)

            pe.wait_ge(S("bias_cp"), 1)
            gemm(0, 0, x_hi, x_lo, first=True, parts=("x_lo_done", 0))
            gemm(1, 1, x_hi, x_lo, first=True)
            gemm(2, 0, x_hi, x_lo)
            gemm(3, 1, x_hi, x_lo)
            gemm(4, 0, x_hi, x_lo)
            gemm(5, 1, x_hi, x_lo)
            pe.wait_ge(S("one"), 1)
            pe.wait_ge(S("ada_acc"), ADA_N)
            for j in range(ADA_N):
                last = mm(ps[:, 7, j:j + 1], ada_acc[:, j // KT, (j % KT) * P:(j % KT + 1) * P], sm["one"],
                          start=True, stop=True)
            last.then_inc(S("ada_mm"), 1)
            pe.wait_ge(S("gemm_evac"), 6)
            turn(raw[:, 1, :], 4)
            with pe.Fori(3, 10) as i:
                for u in range(2):
                    gemm(2 * i + u, u, x_hi, x_lo)
            if stop <= 1:
                return

            pe.wait_ge(S("gemm_evac"), 20)

            def scores(b, s, first=False):
                kb0 = 1 if first else 0
                pe.wait_ge(S("att_stage"), b + 1)
                for g in range(2):
                    if not first:
                        pe.wait_ge(S("att_sc"), 2 * b + g - 1)
                    for m in range(4):
                        last = mm(ps[:, 2 * g + m // 2, (m % 2) * 256 + kb0 * P:(m % 2) * 256 + 256],
                                  q_st[64 * g:64 * g + 64, s, m, :], k_st[64 * g:64 * g + 64, s, kb0 * P:],
                                  start=True, stop=True)
                    last.then_inc(S("att_mm"), 1)

            def attend(b, s, first=False, second=False, last_one=False):
                kb0 = 1 if first else 0
                if not last_one:
                    scores(b + 1, 1 - s)
                for g in range(2):
                    pe.wait_ge(S("att_p"), 2 * b + g + 1)
                    if not (first and g == 0):
                        pe.wait_ge(S("attT_cp"), 2 * b + g)
                    for kb in range(kb0, 2):
                        for m in range(4):
                            last = nc.tensor.transpose(ps[:, 4 + kb, m * P:(m + 1) * P],
                                                       sc[:, g, m, kb * P:(kb + 1) * P], par("ident"))
                    last.then_inc(S("attT_mm"), 1)
                for g in range(2):
                    pe.wait_ge(S("attT_cp"), 2 * b + g + 1)
                    if first and g == 0:
                        pe.wait_ge(S("ada_done"), 1)
                    elif not (first or second) and g == 0:
                        pe.wait_ge(S("att_out"), 2 * b - 2)
                    for kb in range(kb0, 2):
                        last = mm(ps[64 * g:64 * g + 64, 6 + s, :], v_st[:, s, kb, 64 * g:64 * g + 64],
                                  pT[:, g, kb, :], start=(kb == kb0), stop=(kb == 1))
                    last.then_inc(S("av_mm"), 1)

            scores(0, 0, first=True)
            attend(0, 0, first=True)
            attend(1, 1, second=True)
            with pe.Fori(1, NB // 2 - 1) as i:
                for s in range(2):
                    attend(2 * i + s, s)
            attend(NB - 2, 0)
            attend(NB - 1, 1, last_one=True)
            if stop <= 2:
                return

            def low_rank(m):
                if m:
                    pe.wait_ge(S("lora_sig"), m)
                for h in range(2):
                    t = slice(h * 512, (h + 1) * 512)
                    mm(ps[:, h, :], par("w_lora", m * P, P, 0, 64), proj[0:64, 18, t], start=True, stop=True)
                    last = mm(ps[:, 2 + h, :], par("w_lora", m * P, P, 64, P), proj[64:P, 18, t], start=True, stop=True)
                last.then_inc(S("lora_mm"), 1)

            pe.wait_ge(S("att_out"), 16)
            for m in range(4):
                pe.wait_ge(S("kn_sq"), m + 1)
                for t in range(NB):
                    last = mm(ps[:, 4, (m * NB + t) * 2:(m * NB + t) * 2 + 2], tt_[:, m % 2, t * P:(t + 1) * P],
                              par("halves")[:, 0:P:64], start=True, stop=True)
                last.then_inc(S("kn_mm"), 1)
                if m == 1:
                    pe.wait_ge(S("lora_act"), 1)
                    low_rank(0)

            def spread(src, m, b0):
                for t in range(NB):
                    for h in range(2):
                        c = (m * NB + t) * 2 + h
                        last = mm(ps[64 * h:64 * h + 64, b0 + t // 4, (t % 4) * P:(t % 4 + 1) * P],
                                  src[:, c:c + 1].to_broadcast([P, 64]), par("ident"), start=True, stop=True)
                return last

            low_rank(1)
            pe.wait_ge(S("kinv"), 1)
            for m in range(4):
                if m:
                    pe.wait_ge(S("kkn_done"), m)
                spread(sm["kinv"], m, 5).then_inc(S("kinv_bc"), 1)
                if m < 2:
                    low_rank(m + 2)

            pe.wait_ge(S("kkn_done"), 4)
            H2 = [(m, slice(64 * h, 64 * h + 64)) for m in range(4) for h in range(2)]

            two = {n: pe.alloc_register(f"two{n}") for n in (1, 2, 3)}
            five = {n: pe.alloc_register(f"five{n}") for n in range(1, 6)}
            with pe.Fori(0, 8) as i:
                for n, r in two.items():
                    pe.reg_mov(r, 2 * i + n)
                for n, r in five.items():
                    pe.reg_mov(r, 5 * i + n)
                pe.nop()
                for s in range(2):
                    hold(S("ch_prep"), two[s + 1])
                    z = 4 * s
                    for m, q in H2:
                        mm(ps[q, z + 0, m * P:(m + 1) * P], b_ch[q, s, m, :], ar[q, s, m, :, :], start=True, stop=True)
                        mm(ps[q, z + 1, m * P:(m + 1) * P], k_ch[q, s, m, :], ar[q, s, m, :, :], start=True, stop=True)
                        mm(ps[q, z + 2, m * 64:m * 64 + 64], ar[q, s, m, 0, :], b_ch[q, s, m, :], start=True, stop=True)
                        mm(ps[q, z + 2, 256 + m * 64:256 + m * 64 + 64], b_ch[q, s, m, :], par("ident")[q, q],
                           start=True, stop=True)
                        mm(ps[q, z + 3, m * 64:m * 64 + 64], v_ch[q, s, m, :], par("ident")[q, q], start=True, stop=True)
                        last = mm(ps[q, z + 3, 256 + m * 64:256 + m * 64 + 64], k_ch[q, s, m, :], par("ident")[q, q],
                                  start=True, stop=True)
                    last.then_inc(S("ch_mm"), 1)
                for l in range(5):
                    for s in range(2):
                        if l == 0:
                            hold(S("ch_masked"), two[s + 1])
                        else:
                            hold(S(f"x_upd{s}"), five[l])
                        for m, q in H2:
                            last = mm(ps[q, 4 * s, m * 64:m * 64 + 64], lvl[q, s, l, m, :], xx[q, s, 0, m, :],
                                      start=True, stop=True)
                        last.then_inc(S(f"y_mm{s}"), 1)
                    for s in range(2):
                        hold(S(f"y_cp{s}"), five[l + 1])
                        for m, q in H2:
                            if l < 4:
                                mm(ps[q, 4 * s, m * 64:m * 64 + 64], xx[q, s, 1, m, :], y_sb[q, s, m, :],
                                   start=True, stop=True)
                            last = mm(ps[q, 4 * s, 256 + m * 64:256 + m * 64 + 64], y_sb[q, s, m, :],
                                      xx[q, s, 1, m, :], start=True, stop=True)
                        last.then_inc(S(f"x_mm{s}"), 1)
                for s in range(2):
                    hold(S("st_upd"), two[s + 1])
                    hold(S("ch_tok"), two[s + 1])
                    for m, q in H2:
                        o = ps[q, 6, m * 64:m * 64 + 64]
                        mm(o, ar[q, s, m, 0, :], st[q, s, m, :], start=True, stop=False)
                        last = mm(o, m2[q, s, m, 0:64], vk_tok[q, s, 0, m, :], start=False, stop=True)
                    last.then_inc(S("rhs_mm"), 1)
                    hold(S("rhs_cp"), two[s + 1])
                    hold(S(f"x_upd{s}"), five[5])
                    for m, q in H2:
                        last = mm(ps[q, 6, 256 + m * 64:256 + m * 64 + 64], xx[q, s, 1, m, :], rhs[q, m, :],
                                  start=True, stop=True)
                    last.then_inc(S("u_mm"), 1)
                    hold(S("u_cp"), two[s + 1])
                    for m, q in H2:
                        o = ps[q, 6, m * 64:m * 64 + 64]
                        mm(o, vk_tok[q, s, 1, m, :], vk_tok[q, s, 0, m, :], start=True, stop=False)
                        last = mm(o, b_tok[q, s, m, :], u_sb[q, m, :], start=False, stop=True)
                    last.then_inc(S("ds_mm"), 1)
                    hold(S("o_cp"), two[s + 1])
                    for m, q in H2:
                        o = ps[q, 7, m * 64:m * 64 + 64]
                        mm(o, st[q, s, m, :], ar[q, s, m, 1, :], start=True, stop=False)
                        mm(o, u_sb[q, m, :], m1[q, s, m, 64:], start=False, stop=False)
                        last = mm(o, vk_tok[q, s, 0, m, :], m2[q, s, m, 64:], start=False, stop=True)
                    last.then_inc(S("o_mm"), 1)

            pe.wait_ge(S("o_cp"), 17)

            def centered(m):
                if m >= 2:
                    pe.wait_ge(S("oc_done"), m - 1)
                for h in range(2):
                    last = mm(ps[:, 2 * (m % 2) + h, :], par("center"), o1[:, m, h * 512:(h + 1) * 512],
                              start=True, stop=True)
                last.then_inc(S("cen_mm"), 1)

            centered(0)
            for m in range(4):
                if m < 3:
                    centered(m + 1)
                pe.wait_ge(S("gn_sq"), m + 1)
                for t in range(NB):
                    last = mm(ps[:, 4, (m * NB + t) * 2:(m * NB + t) * 2 + 2], osq[:, m % 2, t * P:(t + 1) * P],
                              par("mean_half"), start=True, stop=True)
                last.then_inc(S("gn_mm"), 1)
            pe.wait_ge(S("gn_rstd"), 1)
            pe.wait_ge(S("oc_done"), 4)
            pe.wait_ge(S("rk_back"), 16)
            for m in range(4):
                if m:
                    pe.wait_ge(S("inv_used"), m)
                spread(sm["kinv"], m, 0)
                if m:
                    pe.wait_ge(S("bonus_used"), m)
                for h in range(2):
                    mm(ps[:, 2 + h, :], par("halves"), rk2[:, m, h * 512:(h + 1) * 512], start=True, stop=True)
                if m:
                    pe.wait_ge(S("of_done"), m)
                for h in range(2):
                    last = mm(ps[:, 5 + h, :], par("w_gate", m * P, P), proj[:, 19, h * 512:(h + 1) * 512],
                              start=True, stop=True)
                last.then_inc(S("fin_mm"), 1)
            if stop <= 3:
                return

            pe.wait_ge(S("inv_used"), 4)
            gemm(G_OUT, 0, x_hi, x_lo, parts=("x_lo_done", 8))
            pe.wait_ge(S("bonus_used"), 4)
            gemm(G_OUT + 1, 1, x_hi, x_lo)
            with pe.Fori(G_OUT // 2 + 1, G_FFN // 2) as i:
                for u in range(2):
                    gemm(2 * i + u, u, x_hi, x_lo)
            norm_sum(1)
            norm_sum(2)

            with pe.Fori(0, FFN_GROUPS) as gr:
                with pe.Fori(0, GROUP) as j:
                    g = pe.snap(G_FFN + 3 * GROUP * gr + 2 * j)
                    for u in range(2):
                        gemm(g + u, u, x_hi, x_lo, parts=None if u else ("x_lo_done", 16))
                with pe.Fori(0, GROUP // 2) as j:
                    g = pe.snap(G_FFN + 3 * GROUP * gr + 2 * GROUP + 2 * j)
                    for u in range(2):
                        gemm(g + u, u, f_hi, f_lo, parts=None if u else ("f_lo_done", 8 * gr))
            norm_sum(3)
            norm_sum(4)
            if stop <= 4:
                return

            gemm(G_IN2, 0, x_hi, x_lo, parts=("x_lo_done", 24))
            gemm(G_IN2 + 1, 1, x_hi, x_lo)
            with pe.Fori(G_IN2 // 2 + 1, (G_IN2 + N_GATE2 + N_CHAN2 - 1) // 2) as i:
                for u in range(2):
                    gemm(2 * i + u, u, x_hi, x_lo)
            g = G_IN2 + N_GATE2 + N_CHAN2 - 1
            gemm(g, g % 2, x_hi, x_lo)
            g0 = g + 1
            pe.wait_ge(S("gemm_evac"), G_IN2 + N_GATE2 + 9)
            for m in range(2):
                for h in range(2):
                    last = mm(ps[:, 4 + 2 * m + h, :], par("w_gla2", m * P, P, 0, 16), proj2[0:16, 8, h * 512:(h + 1) * 512],
                              start=True, stop=True)
                last.then_inc(S("gla_mm"), 1)
            def turn2(n, u, first=False):
                pe.wait_ge(S("gemm_evac"), n + (g0 + 1))
                if not first:
                    pe.wait_ge(S("turn_cp"), n)
                turn(to_turn[:, u, :], 4 + 2 * u)

            gemm(g0, g0 % 2, x_hi, x_lo)
            gemm(g0 + 1, (g0 + 1) % 2, x_hi, x_lo)
            pe.wait_ge(S("gla_cp"), 2)
            turn2(0, 0, first=True)
            gemm(g0 + 2, g0 % 2, x_hi, x_lo)
            turn2(1, 1, first=True)
            with pe.Fori(1, N_TOK2 // 2 - 1) as i:
                for u in range(2):
                    gemm(2 * i + (g0 + 1 + u), (g0 + 1 + u) % 2, x_hi, x_lo)
                    turn2(2 * i + u, u)
            gemm(g0 + N_TOK2 - 1, (g0 + 1) % 2, x_hi, x_lo)
            for n in (N_TOK2 - 2, N_TOK2 - 1):
                turn2(n, n % 2)
            pe.wait_ge(S("lsig"), 4)
            pe.sem_inc(S("lev_mm"), 2)
            pe.sem_inc(S("ds2_mm"), 1)

            def gla_block(b, s, last=False):
                if not last:
                    pe.wait_ge(S("kh_done"), b + 1)
                    pe.wait_ge(S("khT_cp"), b + 1)
                    for m in range(4):
                        i_ = nc.tensor.transpose(ps[:, 6, m * P:(m + 1) * P], kh[:, m, :], par("ident"))
                    i_.then_inc(S("khT_mm"), 1)
                for l in range(8):
                    if l < 7:
                        pe.wait_ge(S("z_done"), 7 * b + l + 1)
                    pe.wait_ge(S("lev_cp"), 8 * b + l + 1)
                    n = P // 2 if l < 7 else P
                    for h in range(8):
                        q = slice(64 * (h % 2), 64 * (h % 2) + 64)
                        r = reach(l) if h else P
                        if l < 7:
                            lh = zz[q, l % 2, h // 2, 0:r]
                            rh = zz[q, l % 2, h // 2, :].rearrange("p (n w) -> p n w", w=P >> l)[:, :, 64 >> l:]
                        else:
                            lh, rh = k_b[q, s, h // 2, :], q_b[q, s, h // 2, :]
                        i_ = mm(ps[0:r, 2 * (l % 2) + h % 2, (h // 2) * n:(h // 2 + 1) * n], lh, rh, start=True, stop=True)
                    i_.then_inc(S("lev_mm"), 1)
                    if l == 4 and not last:
                        pe.wait_ge(S("khT_cp"), b + 2)
                        pe.wait_ge(S("st2_upd"), b + 1)
                        for h in range(4):
                            q = slice(64 * (h % 2), 64 * (h % 2) + 64)
                            mm(ps[q, 7, (h // 2) * P:(h // 2 + 1) * P], kh[:, h // 2, q], v_b[:, s, h, :],
                               start=True, stop=True)
                            i_ = mm(ps[q, 7, 256 + (h // 2) * 64:256 + (h // 2) * 64 + 64], kh[:, 2 + h // 2, q],
                                    v_b[:, s, 4 + h // 2, q], start=True, stop=True)
                        i_.then_inc(S("ds2_mm"), 1)
                pe.wait_ge(S("lev_cp"), 8 * b + 10)
                pe.wait_ge(S("st2_upd"), b + 1)
                pe.wait_ge(S("o2_cp"), b + 1)
                for h in range(4):
                    o = ps[:, 4 + h % 2, (h // 2) * P:(h // 2 + 1) * P]
                    q = slice(64 * (h % 2), 64 * (h % 2) + 64)
                    mm(o, v_b[:, s, h, :], s_m[:, s, 4 * (h % 2) + h // 2, :], start=True, stop=False)
                    mm(o, st2[q, (h // 2) * P:(h // 2 + 1) * P], qe[q, s, h // 2, :], start=False, stop=True)
                for h in range(4):
                    q = slice(64 * (h % 2), 64 * (h % 2) + 64)
                    o = ps[q, 4 + h % 2, 256 + (h // 2) * P:256 + (h // 2 + 1) * P]
                    mm(o, v_b[:, s, 4 + h // 2, q], s_m[:, s, 4 * (h % 2) + 2 + h // 2, :], start=True, stop=False)
                    i_ = mm(o, st2[q, 256 + (h // 2) * 64:256 + (h // 2) * 64 + 64], qe[q, s, 2 + h // 2, :],
                            start=False, stop=True)
                i_.then_inc(S("o2_mm"), 1)

            gla_block(0, 0)
            gla_block(1, 1)
            with pe.Fori(1, NB // 2 - 1) as i:
                for s in range(2):
                    gla_block(2 * i + s, s)
            gla_block(NB - 2, 0)
            gla_block(NB - 1, 1, last=True)

            pe.wait_ge(S("sbmask_in"), 16)
            pe.wait_ge(S("o2_cp"), 9)
            steps = [(h, b) for h in range(4) for b in range(NB - 1, -1, -1)]

            def halves_of(b):
                return [(x, max(b * P - 512 * x, 0), slice(max(b * P, 512 * x), 512 * (x + 1)))
                        for x in range(2) if b * P < 512 * (x + 1)]

            def z_scores(n):
                h, b = steps[n]
                q = slice(64 * (h % 2), 64 * (h % 2) + 64)
                if n >= 2:
                    pe.wait_ge(S("sb_w"), n - 1)
                for x, c, t in halves_of(b):
                    last = mm(ps[:, 2 * (n % 2) + x, c:], proj2[q, 11 + h // 2, b * P:(b + 1) * P],
                              proj2[q, 9 + h // 2, t], start=True, stop=True, skip_group_check=True)
                last.then_inc(S("sb_z"), 1)

            def weigh(n):
                h, b = steps[n]
                pe.wait_ge(S("sb_wm"), n + 1)
                q = slice(64 * (h % 2), 64 * (h % 2) + 64)
                for x, c, t in halves_of(b):
                    last = mm(ps[q, 4 + 2 * (h // 2) + x, c:], v2[:, 6 + h // 2, b, q], wts[:, n % 2, t],
                              start=(b == (NB - 1 if x else 3)), stop=(b == 0), skip_group_check=True)
                last.then_inc(S("sb_pv"), 1)

            z_scores(0)
            z_scores(1)
            for n, (h, b) in enumerate(steps):
                pe.wait_ge(S("sb_sp"), n + 1)
                for x, c, t in halves_of(b):
                    last = mm(ps[:, 2 * (n % 2) + x, c:], sbmask[:, 0, :], spl[:, n % 2, t], start=False, stop=True,
                              skip_group_check=True)
                if b < NB - 1:
                    pe.wait_ge(S("sb_acc"), n)
                    for x, c, t in halves_of(b + 1):
                        last = mm(ps[:, 2 * (n % 2) + x, c:], sbmask[:, 1, :], lacc[:, t], start=False, stop=True,
                                  skip_group_check=True)
                last.then_inc(S("sb_r"), 1)
                if n:
                    weigh(n - 1)
                if n + 2 < len(steps):
                    z_scores(n + 2)
            weigh(len(steps) - 1)

            for k in range(6):
                pe.wait_ge(S("hn_sq"), k + 1)
                for t in range(NB):
                    last = mm(ps[:, 0, (k * NB + t) * 2:(k * NB + t) * 2 + 2], sq_h[:, k % 2, t * P:(t + 1) * P],
                              par("mean2") if k < 4 else par("mean_half"), start=True, stop=True)
                last.then_inc(S("hn_mm"), 1)
            pe.wait_ge(S("hn_rstd"), 1)
            pe.wait_ge(S("oc2_cp"), 4)
            for k in range(6):
                if k >= 2:
                    pe.wait_ge(S("hn_out"), k - 1)
                spread(hn_r, k, 4 + 2 * (k % 2)).then_inc(S("hn_bc"), 1)
            if stop <= 5:
                return

            g0 = G_OUT2
            gemm(g0, g0 % 2, x_hi, x_lo, parts=("x_lo_done", 32))
            gemm(g0 + 1, (g0 + 1) % 2, x_hi, x_lo)
            with pe.Fori(1, 4) as i:
                for u in range(2):
                    gemm(2 * i + (g0 + u), (g0 + u) % 2, x_hi, x_lo)
            norm_sum(5)

        @block.scalar
        def _(eng):
            act = InOrder(eng)
            fn = act.op(nc.scalar.activation)

            def copy(out, in_):
                return fn(out, in_, ACT.Copy)

            def take(sem, value):
                act.wait_ge(sem, value)
                copy(sm["took"], sm["one"])

            def norm(n, src, ready):
                for k in range(KT):
                    ready(k)
                    if n or k >= 2:
                        act.wait_ge(S("norm_pair"), 4 * n + k // 2)
                    fn(sq_of[n][:, k % 2, :], src(k), ACT.Square).then_inc(S("norm_sq"), 1)
                act.wait_ge(S("norm_mm"), 4 * n + 4)
                fn(rs_of(n), rs_of(n), ACT.Sqrt, bias=sm["eps"]).then_inc(S("norm_root"), 1)

            def high(n, src, sem):
                for k in range(KT):
                    if sem:
                        act.wait_ge(S(sem), 8 * n + k + 1)
                    copy(x_hi[:, k, :], src(k)).then_inc(S("x_hi_done"), 1)

            act.wait_ge(S("one"), 1)
            act.dma_start(x_in[:, 0:4, :], dr["xT"][:, 0:4 * T].rearrange("p (k t) -> p k t", t=T)).then_inc(S("x_in0"), 16)
            act.dma_start(x_in[:, 4:8, :], dr["xT"][:, 4 * T:].rearrange("p (k t) -> p k t", t=T)).then_inc(S("x_in1"), 16)
            act.dma_start(cst[:, :], dr["cst"]).then_inc(S("cst_in"), 16)

            def ada_load(n):
                if n >= ADA_RING:
                    act.wait_ge(S("ada_acc"), n - ADA_RING + 1)
                act.dma_start(ada_w[:, n % ADA_RING, :], dr["wada"][n]).then_inc(S(f"ada_in{n % ADA_RING}"), 16)

            for n in range(ADA_RING):
                ada_load(n)
            act.wait_ge(S("cst_in"), 16)
            fn(sm["silu_c"], par("c"), ACT.Silu).then_inc(S("c_silu"), 1)
            norm(0, lambda k: x_in[:, k, :], lambda k: act.wait_ge(S(f"x_in{k // 4}"), 16))
            act.wait_ge(S("bias_mm"), 1)
            copy(bias_row[0:8, :], ps[0:8, 0, 0:384]).then_inc(S("bias_cp"), 1)
            act.wait_ge(S("bias_cp"), 1)
            act.dma_start(bias_dram, bias_row[0:8, :].unsqueeze(1).to_broadcast([8, P, 384])).then_inc(S("bias_out"), 16)
            act.wait_ge(S("bias_out"), 16)
            act.dma_start(bias[:, :, :], bass.AP(bias_dram.tensor, 127, [[383, P], [P * 384, 8], [1, 2 * P]]))\
                .then_inc(S("bias_in"), 16)
            high(0, lambda k: nrm_a[:, k % 2, :], "h_done")
            for n in range(ADA_RING, 2 * ADA_RING):
                ada_load(n)

            for g in range(6):
                for n in range(2 * ADA_RING + 3 * g, min(2 * ADA_RING + 3 * g + 3, ADA_N)):
                    ada_load(n)
                act.wait_ge(S("gemm_mm"), g + 1)
                copy(proj[:, g, :] if g < 5 else raw[:, 1, :], pair(2 * (g % 2))).then_inc(S("gemm_evac"), 1)
            act.wait_ge(S("turn_mm"), 1)
            copy(proj[:, 5, :], pair(4)).then_inc(S("turn_cp"), 1)
            for g in (6, 7):
                act.wait_ge(S("gemm_mm"), g + 1)
                copy(raw[:, g % 2, :], pair(2 * (g % 2))).then_inc(S("gemm_evac"), 1)
            with act.Fori(4, 10) as i:
                for u in range(2):
                    act.wait_ge(S("gemm_mm"), 2 * i + u + 1)
                    act.wait_ge(S("shift_done"), 2 * i + u - 7)
                    copy(raw[:, u, :], pair(2 * u)).then_inc(S("gemm_evac"), 1)
            if stop <= 1:
                return

            act.wait_ge(S("gemm_mm"), 20)
            act.dma_start(smask[:, :], dr["scan"][:, 0:T]).then_inc(S("smask_in"), 16)

            def stage(b, s, first=False):
                if first:
                    copy(q_st[:, s, :, :], proj[:, 0:4, 0:P])
                    copy(k_st[:, s, P:], proj[:, 4, 0:P])
                    copy(v_st[:, s, 1, :], proj[:, 5, 0:P]).then_inc(S("att_stage"), 1)
                else:
                    q0 = b * P
                    copy(q_st[:, s, :, :], proj[:, 0:4, bass.ds(q0, P)])
                    copy(k_st[:, s, :], proj[:, 4, bass.ds(q0 - P, 2 * P)])
                    copy(v_st[:, s, :, :].rearrange("p a c -> p (a c)"),
                         proj[:, 5, bass.ds(q0 - P, 2 * P)]).then_inc(S("att_stage"), 1)

            def attend(b, s, first=False, last=False):
                if not last:
                    stage(b + 1, 1 - s)
                k0 = P if first else 0
                for g in range(2):
                    act.wait_ge(S("att_max"), 2 * b + g + 1)
                    for m in range(4):
                        fn(sc[:, g, m, k0:], sc[:, g, m, k0:], ACT.Exp, bias=sm["nm"][:, 4 * g + m:4 * g + m + 1],
                           accum_out=sm["den"][:, 4 * g + m:4 * g + m + 1])
                    fn(sm["es"][:, 4 * g:4 * g + 4], sm["es"][:, 4 * g:4 * g + 4], ACT.Exp).then_inc(S("att_exp"), 1)
                for g in range(2):
                    act.wait_ge(S("attT_mm"), 2 * b + g + 1)
                    if first:
                        copy(pT[:, g, 1, :], ps[:, 5, :]).then_inc(S("attT_cp"), 1)
                    else:
                        copy(pT[:, g, :, :], ps[:, 4:6, :]).then_inc(S("attT_cp"), 1)
                for g in range(2):
                    take(S("av_mm"), 2 * b + g + 1)
                    q = slice(64 * g, 64 * g + 64)
                    dst = proj[q, 0:4, 0:P] if first else proj[q, 0:4, bass.ds(b * P, P)]
                    copy(dst, ps[q, 6 + s, :].rearrange("p (m t) -> p m t", t=P)).then_inc(S("att_out"), 1)

            act.wait_ge(S("gemm_evac"), 20)
            stage(0, 0, first=True)
            attend(0, 0, first=True)
            attend(1, 1)
            with act.Fori(1, NB // 2 - 1) as i:
                for s in range(2):
                    attend(2 * i + s, s)
            attend(NB - 2, 0)
            attend(NB - 1, 1, last=True)
            if stop <= 2:
                return

            act.wait_ge(S("shift_done"), 14)

            def key_squares(m):
                act.wait_ge(S("kk_done"), m + 1)
                if m >= 2:
                    act.wait_ge(S("kn_mm"), m - 1)
                fn(tt_[:, m % 2, :], kkn[:, m, :], ACT.Square).then_inc(S("kn_sq"), 1)

            def rates(m):
                act.wait_ge(S("lora_mm"), m + 1)
                if m >= 2:
                    act.wait_ge(S("cum_done"), m - 1)
                fn(ut[:, m % 2, :], pair(0), ACT.Sigmoid, bias=par("w0", m, 1))
                fn(kka[:, m, :], pair(2), ACT.Sigmoid, bias=par("a0", m, 1)).then_inc(S("lora_sig"), 1)

            key_squares(0)
            key_squares(1)
            fn(proj[0:64, 18, :], proj[0:64, 18, :], ACT.Tanh)
            fn(proj[:, 19, :], proj[:, 19, :], ACT.Sigmoid).then_inc(S("lora_act"), 1)
            key_squares(2)
            key_squares(3)
            rates(0)
            act.wait_ge(S("kn_mm"), 4)
            fn(sm["kn"], ps[:, 4, 0:64], ACT.Sqrt).then_inc(S("kn_sqrt"), 1)
            for m in range(1, 4):
                rates(m)
            act.dma_start(rmask[:, :], dr["rmask"]).then_inc(S("rmask_in"), 16)
            for m in range(4):
                act.wait_ge(S("rk_done"), m + 1)
                act.dma_start(rk_dram[:, m * T:(m + 1) * T], rk[:, m, :]).then_inc(S("rk_out"), 16)
            act.wait_ge(S("rk_out"), 64)

            act.sem_inc(S("o_cp"), 1)

            def prepare(c, s):
                t = bass.ds(c * RC, RC)
                fn(e_neg[:, s, :, 1:], cum[:, :, t], ACT.Exp, scale=-DECAY)
                fn(e_pos[:, s, :, :], cum[:, :, t], ACT.Exp, scale=DECAY)
                copy(v_ch[:, s, :, :], proj[:, 14:18, t]).then_inc(S("ch_exp"), 1)

            def chunk_pair(i, last=False):
                for s in range(2):
                    act.wait_ge(S("ch_mm"), 2 * i + s + 1)
                    copy(vk_tok[:, s, :, :, :], ps[:, 4 * s + 3, :].rearrange("p (x m c) -> p x m c", x=2, m=4))\
                        .then_inc(S("ch_tok"), 1)
                for l in range(5):
                    for s in range(2):
                        act.wait_ge(S(f"y_mm{s}"), 5 * i + l + 1)
                        copy(y_sb[:, s, :, :], ps[:, 4 * s, 0:256]).then_inc(S(f"y_cp{s}"), 1)
                for s in range(2):
                    c = 2 * i + s
                    act.wait_ge(S("rhs_mm"), c + 1)
                    copy(rhs[:, :, :], ps[:, 6, 0:256]).then_inc(S("rhs_cp"), 1)
                    if s and not last:
                        act.wait_ge(S("st_upd"), 2 * i + 2)
                        prepare(c + 1, 0)
                    act.wait_ge(S("o_mm"), c + 1)
                    copy(o1[:, :, bass.ds(c * RC, RC)], ps[:, 7, 0:256].rearrange("p (m t) -> p m t", t=RC))\
                        .then_inc(S("o_cp"), 1)
                if not last:
                    act.wait_ge(S("st_upd"), 2 * i + 3)
                    prepare(2 * i + 3, 1)

            act.wait_ge(S("st_upd"), 1)
            for s in range(2):
                prepare(s, s)
            with act.Fori(0, 7) as i:
                chunk_pair(i)
            chunk_pair(7, last=True)

            act.wait_ge(S("st_upd"), 17)
            act.dma_start(rk2[:, :, :], rk_dram.rearrange("p (m t) -> p m t", t=T)).then_inc(S("rk_back"), 16)
            for k in range(4):
                copy(x_hi[:, k, :], mix_src[k]).then_inc(S("x_hi_done"), 1)
            for m in range(4):
                act.wait_ge(S("cen_mm"), m + 1)
                if m >= 2:
                    act.wait_ge(S("gn_mm"), m - 1)
                fn(osq[:, m % 2, :], pair(2 * (m % 2)), ACT.Square).then_inc(S("gn_sq"), 1)
            act.wait_ge(S("gn_var"), 1)
            fn(sm["kinv"], sm["kn"], ACT.Sqrt).then_inc(S("gn_rstd"), 1)
            if stop <= 3:
                return

            for k in range(4, KT):
                act.wait_ge(S("of_done"), k - 3)
                copy(x_hi[:, k, :], mix_src[k]).then_inc(S("x_hi_done"), 1)
            act.wait_ge(S("x_lo_done"), 16)
            act.dma_start(x1[:, :, :], dr["xT"].rearrange("p (k t) -> p k t", t=T)).then_inc(S("x_again"), 16)

            def y1_tile(k):
                g = G_OUT + k
                act.wait_ge(S("gemm_mm"), g + 1)
                copy(y1[:, k, :], pair(2 * (g % 2))).then_inc(S("gemm_evac"), 1)

            norm(1, lambda k: y1[:, k, :], y1_tile)
            norm(2, lambda k: x1[:, k, :], lambda k: act.wait_ge(S("x1_done"), k + 1))
            act.dma_start(x1_dram, x1[:, :, :].rearrange("p k t -> p (k t)")).then_inc(S("x1_out"), 16)
            high(1, lambda k: nrm_a[:, k % 2, :], "h_done")
            act.wait_ge(S("x1_out"), 16)

            eng.preload_act_table_set("gelu_apprx_tanh_and_others")
            with act.Fori(0, FFN_GROUPS) as gr:
                with act.Fori(0, GROUP) as j:
                    p = act.snap(GROUP * gr + j)
                    g = act.snap(G_FFN + 3 * GROUP * gr + 2 * j)
                    for u, dst in enumerate((cg, cv)):
                        col = act.snap(2 * p + u)
                        act.wait_ge(S("prod"), p + 1)
                        act.wait_ge(S("gemm_mm"), g + u + 1)
                        fn(dst[:, :], pair(2 * u), ACT.Identity, bias=par("conv_b")[:, bass.ds(col, 1)],
                           scale=par("conv_w")[:, bass.ds(128 + col, 1)]).then_inc(S("conv_a"), 1)
                    act.wait_ge(S("gemm_evac"), g + 1)
                    fn(cg[:, :], cg[:, :], ACT.Gelu_apprx_tanh).then_inc(S("gelu"), 1)
                    act.wait_ge(S("prod"), p + 2)
                    copy(f_hi[:, bass.ds(j, 1), :], gv[:, :].unsqueeze(1)).then_inc(S("f_hi_done"), 1)
            act.wait_ge(S("gemm_mm"), G_IN2)
            act.dma_start(x2[:, :, :], x1_dram.rearrange("p (k t) -> p k t", t=T)).then_inc(S("x1_back"), 16)
            act.wait_ge(S("gemm_evac"), G_IN2)
            norm(3, lambda k: f_acc[:, k, :], lambda k: None)
            norm(4, lambda k: x2[:, k, :], lambda k: act.wait_ge(S("x2_done"), k + 1))
            act.dma_start(x2_dram, x2[:, :, :].rearrange("p k t -> p (k t)")).then_inc(S("x2_out"), 16)
            high(2, lambda k: nrm_b[:, k % 2, :], "h_done")
            if stop <= 4:
                return

            act.wait_ge(S("x2_out"), 16)
            for k in range(N_GATE2):
                g = G_IN2 + k
                if k >= 2:
                    act.wait_ge(S(f"gate_out{k % 2}"), 16 * (k // 2))
                act.wait_ge(S("gemm_mm"), g + 1)
                fn(gate_st[:, k % 2, :], pair(2 * (g % 2)), ACT.Silu).then_inc(S("gemm_evac"), 1)
                act.wait_ge(S("gemm_evac"), g + 1)
                act.dma_start(gate_dram[k], gate_st[:, k % 2, :]).then_inc(S(f"gate_out{k % 2}"), 16)
            for k in range(N_CHAN2):
                g = G_IN2 + N_GATE2 + k
                act.wait_ge(S("gemm_mm"), g + 1)
                if k in (0, 1, 9, 10):
                    i_ = fn(proj2[:, k, :], pair(2 * (g % 2)), ACT.Copy, scale=SCALE)
                else:
                    i_ = fn(proj2[:, k, :], pair(2 * (g % 2)), ACT.Silu if k in (2, 3) else ACT.Copy)
                i_.then_inc(S("gemm_evac"), 1)

            for m in range(2):
                act.wait_ge(S("gla_mm"), m + 1)
                fn(la[:, m, :], pair(4 + 2 * m), ACT.Identity, bias=par("b_gla", m, 1)).then_inc(S("gla_cp"), 1)
            act.wait_ge(S("lb_d"), 1)
            eng.preload_act_table_set("natural_log_exp_and_others")
            fn(sm["lb_e"], sm["lb_d"], ACT.Exp).then_inc(S("lb_e"), 1)

            def softplus_part(out, src):
                fn(out, src, ACT.Abs)
                fn(out, out, ACT.Exp, scale=-1.0)
                fn(out, out, ACT.Ln, bias=1.0).then_inc(S("ls_ln"), 1)

            for u in range(2):
                act.wait_ge(S(f"gate_out{u}"), 16 * N_GATE2 // 2)

            def turned(n):
                act.wait_ge(S("turn_mm"), n + 2)
                copy(v2[:, n, :, :].rearrange("p t c -> p (t c)"), pair(4 + 2 * (n % 2))).then_inc(S("turn_cp"), 1)

            for k in range(N_TOK2):
                g = G_IN2 + N_GATE2 + N_CHAN2 + k
                act.wait_ge(S("gemm_mm"), g + 1)
                copy(to_turn[:, k % 2, :], pair(2 * (g % 2))).then_inc(S("gemm_evac"), 1)
                if k:
                    turned(k - 1)
                if k < 2:
                    softplus_part(ls_t[:, k, :], la[:, k, :])
            turned(N_TOK2 - 1)
            act.wait_ge(S("x_lo_done"), 32)
            act.wait_ge(S("gemm_mm"), G_OUT2)
            act.dma_start(smask2[:, :], dr["scan"][:, T:2 * T]).then_inc(S("smask2_in"), 16)

            act.wait_ge(S("gemm_evac"), G_OUT2)
            for m in range(2, 4):
                src = proj2[:, 4 + m, :]
                softplus_part(g4[:, m % 2, :], src)
                fn(lbt[:, m % 2, :], src, ACT.Exp, scale=-1.0).then_inc(S("lbt_exp"), 1)
                act.wait_ge(S("lbt_min"), m - 1)
                fn(lbt[:, m % 2, :], lbt[:, m % 2, :], ACT.Ln, bias=1.0, scale=sm["lb"][:, m - 2:m - 1])\
                    .then_inc(S("lbt_ln"), 1)
                act.wait_ge(S("fb_read"), m - 1)
                fn(src, src, ACT.Sigmoid, scale=-1.0).then_inc(S("kb_sig"), 1)

            act.wait_ge(S("lsig"), 4)
            act.dma_start(gmask[:, :, :], dr["gmask"].rearrange("p (l t) -> p l t", t=P)).then_inc(S("gmask_in"), 16)
            act.sem_inc(S("khT_cp"), 1)
            act.sem_inc(S("o2_cp"), 1)
            act.wait_ge(S("kb_done"), 2)
            def stage(b, s):
                t = bass.ds(b * P, P)
                copy(c_b[:, s, :, :], c4[:, :, t])
                copy(k_b[:, s, :, :], proj2[:, 4:8, t])
                copy(q_b[:, s, :, :], proj2[:, 0:4, t])
                copy(v_b[:, s, :, :], v2[:, 0:6, :, :].rearrange("p j t c -> p j (t c)")[:, :, t]).then_inc(S("blk_stage"), 1)

            def exponentials(b, s, early=False):
                act.wait_ge(S("d_done"), 15 * b + 1)
                fn(e_end[:, :, :], e_end[:, :, :], ACT.Exp)
                fn(qe[:, s, :, :], c_b[:, s, :, :], ACT.Exp).then_inc(S("e_done"), 1)
                for l in range(7):
                    act.wait_ge(S("d_done"), 15 * b + 2 * l + 3)
                    fn(e7[:, s, l, :, :], e7[:, s, l, :, :], ACT.Exp).then_inc(S("e_done"), 1)
                if not early:
                    act.wait_ge(S("st2_upd"), b)
                fn(sm["ecl"][:, 4 * s:4 * s + 4].unsqueeze(2), c_b[:, s, :, P - 1:P], ACT.Exp).then_inc(S("ecl_done"), 1)

            def gla_block(b, s, first=False, last=False):
                if not last:
                    stage(b + 1, 1 - s)
                    act.wait_ge(S("khT_mm"), b + 1)
                    copy(kh[:, :, :], ps[:, 6, :].rearrange("p (m c) -> p m c", c=P)).then_inc(S("khT_cp"), 1)
                    exponentials(b + 1, 1 - s, early=first)
                t = bass.ds(b * P, P)
                take(S("o2_mm"), b + 1)
                for h in range(2):
                    q = slice(64 * h, 64 * h + 64)
                    copy(proj2[:, 0:4, :].rearrange("p (m h) t -> p m h t", h=2)[:, :, h, t],
                         ps[:, 4 + h, 0:256].rearrange("p (m t) -> p m t", t=P))
                    i_ = copy(proj2[q, 4:6, t], ps[q, 4 + h, 256:].rearrange("p (m t) -> p m t", t=P))
                i_.then_inc(S("o2_cp"), 1)

            stage(0, 0)
            exponentials(0, 0, early=True)
            gla_block(0, 0, first=True)
            gla_block(1, 1)
            with act.Fori(1, NB // 2 - 1) as i:
                for s in range(2):
                    gla_block(2 * i + s, s)
            gla_block(NB - 2, 0)
            gla_block(NB - 1, 1, last=True)

            eng.preload_act_table_set("natural_log_exp_and_others")
            act.dma_start(sbmask[:, :, :], dr["sbmask"].rearrange("p (l t) -> p l t", t=P)).then_inc(S("sbmask_in"), 16)
            steps = [(h, b) for h in range(4) for b in range(NB - 1, -1, -1)]

            def soft(n):
                h, b = steps[n]
                z = pair(2 * (n % 2))[:, b * P:]
                a = ab[:, n % 2, b * P:]
                act.wait_ge(S("sb_z"), n + 1)
                if n >= 2:
                    act.wait_ge(S("sb_sp"), n - 1)
                fn(a, z, ACT.Abs)
                fn(a, a, ACT.Exp, scale=-1.0)
                fn(a, a, ACT.Ln, bias=1.0).then_inc(S("sb_ln"), 1)

            def take_out(h):
                act.wait_ge(S("sb_pv"), NB * (h + 1))
                q = slice(64 * (h % 2), 64 * (h % 2) + 64)
                copy(proj2[q, 9 + h // 2, :], pair(4 + 2 * (h // 2))[q, :]).then_inc(S("oc2_cp"), 1)

            soft(0)
            soft(1)
            for n, (h, b) in enumerate(steps):
                act.wait_ge(S("sb_r"), n + 1)
                if n >= 2:
                    act.wait_ge(S("sb_pv"), n - 1)
                fn(wts[:, n % 2, b * P:], pair(2 * (n % 2))[:, b * P:], ACT.Exp).then_inc(S("sb_w"), 1)
                if n + 2 < len(steps):
                    soft(n + 2)
                if h and b == NB - 2:
                    take_out(h - 1)
            take_out(3)

            for k in range(6):
                if k >= 2:
                    act.wait_ge(S("hn_mm"), k - 1)
                else:
                    act.wait_ge(S("o2_cp"), 9)
                fn(sq_h[:, k % 2, :], proj2[:, k, :], ACT.Square).then_inc(S("hn_sq"), 1)
            act.wait_ge(S("hn_var"), 1)
            fn(hn_r[:, :], hn_v[:, :], ACT.Sqrt).then_inc(S("hn_rstd"), 1)
            act.wait_ge(S("oc2_cp"), 4)
            for k in range(KT + 2):
                if k >= 2:
                    act.wait_ge(S("gate_used"), k - 1)
                if k < KT:
                    act.dma_start(gate_in[:, k % 2, :], gate_dram[k]).then_inc(S(f"gate_back{k % 2}"), 16)
                if k >= 2:
                    copy(x_hi[:, k - 2, :], o_a[k - 2]).then_inc(S("x_hi_done"), 1)
            if stop <= 5:
                return

            act.wait_ge(S("x_lo_done"), 40)
            act.dma_start(x3[:, :, :], x2_dram.rearrange("p (k t) -> p k t", t=T)).then_inc(S("x2_back"), 16)

            def y2_tile(k):
                g = G_OUT2 + k
                act.wait_ge(S("gemm_mm"), g + 1)
                copy(y2[:, k, :], pair(2 * (g % 2))).then_inc(S("gemm_evac"), 1)
                act.wait_ge(S("x3_done"), k + 1)

            norm(5, lambda k: x3[:, k, :], y2_tile)
            for k in range(KT):
                act.wait_ge(S("out_done"), k + 1)
                act.dma_start(dr["out"][:, k * T:(k + 1) * T], y2[:, k, :]).then_inc(S("out_dma"), 16)
            act.wait_ge(S("out_dma"), 16 * KT)

        @block.vector
        def _(eng):
            dve = InOrder(eng)
            tt, ts, stt = (dve.op(f) for f in (nc.vector.tensor_tensor, nc.vector.tensor_scalar,
                                               nc.vector.scalar_tensor_tensor))
            vcopy, memset, reciprocal, scan, reduce_max, copy_pred = (dve.op(f) for f in (
                nc.vector.tensor_copy, nc.vector.memset, nc.vector.reciprocal, nc.vector.tensor_tensor_scan,
                nc.vector.reduce_max, nc.vector.copy_predicated))
            dve.wait_ge(S("cst_in"), 16)
            memset(par("rel_bias", p0=N_BUCKETS, p1=N_BUCKETS + 1), NEG).then_inc(S("neg_row"), 1)
            ts(sm["omka"], par("k_a"), -1.0, 1.0, ALU.mult, ALU.add)

            def norm_pair(n, j):
                dve.wait_ge(S("norm_sq"), 8 * n + 2 * j + 2)
                if j >= 2:
                    dve.wait_ge(S("norm_mm"), 4 * n + j - 1)
                tt(pairs_of[n][:, j % 2, :], sq_of[n][:, 0, :], sq_of[n][:, 1, :], ALU.add).then_inc(S("norm_pair"), 1)

            def norm_inverse(n):
                dve.wait_ge(S("norm_root"), n + 1)
                reciprocal(rs_of(n), rs_of(n))

            def low(n, k, src):
                dve.wait_ge(S("x_hi_done"), 8 * n + k + 1)
                tt(x_lo[:, k, :], src, x_hi[:, k, :].bitcast(F32), ALU.subtract).then_inc(S("x_lo_done"), 1)

            def apply(n, k, buf, src, gain, shift=None):
                i_ = stt(buf[:, k % 2, :], src(k), gain(k), rs_of(n), ALU.mult, ALU.mult)
                if shift is not None:
                    i_ = ts(buf[:, k % 2, :], buf[:, k % 2, :], shift(k), None, ALU.add)
                i_.then_inc(S("h_done"), 1)

            def apply_all(n, n_set, buf, src, gain, shift=None):
                norm_inverse(n)
                for k in range(KT):
                    apply(n, k, buf, src, gain, shift)
                    if k:
                        low(n_set, k - 1, buf[:, (k - 1) % 2, :])
                low(n_set, KT - 1, buf[:, (KT - 1) % 2, :])

            def modulation(n):
                k, part = n // 3, n % 3
                dve.wait_ge(S(f"ada_in{n % ADA_RING}"), 16 * (n // ADA_RING + 1))
                acc, w = ada_acc[:, part, :], ada_w[:, n % ADA_RING, :]
                if k == 0:
                    i_ = ts(acc, w, sm["silu_c"][:, 0:1], None, ALU.mult)
                else:
                    i_ = stt(acc, w, sm["silu_c"][:, k:k + 1], acc, ALU.mult, ALU.add)
                i_.then_inc(S("ada_acc"), 1)

            dve.wait_ge(S("c_silu"), 1)
            for j in range(4):
                norm_pair(0, j)
            apply_all(0, 0, nrm_a, lambda k: x_in[:, k, :], lambda k: par("g_mix_pre", k, 1))
            for n in range(ADA_N):
                modulation(n)
            dve.wait_ge(S("ada_mm"), 1)
            tt(sm["ada"], ps[:, 7, 0:24], par("b_ada"), ALU.add)
            ts(sm["ada"][:, 8:16], sm["ada"][:, 8:16], 1.0, None, ALU.add).then_inc(S("ada_done"), 1)

            def shift(g, j, s):
                dve.wait_ge(S("gemm_evac"), g + 1)
                tt(dif[:, s, 1:], raw[:, s, 0:T - 1], raw[:, s, 1:], ALU.subtract)
                ts(dif[:, s, 0:1], raw[:, s, 0:1], -1.0, None, ALU.mult)
                if isinstance(j, int):
                    out, mix = proj[:, 6 + j, :], par("shift_mix", j, 1)
                else:
                    out, mix = proj[:, 6:20, :][:, bass.ds(j, 1), :].rearrange("p o t -> p (o t)"), \
                        par("shift_mix")[:, bass.ds(j, 1)]
                stt(out, dif[:, s, :], mix, raw[:, s, :], ALU.mult, ALU.add).then_inc(S("shift_done"), 1)

            shift(6, 0, 0)
            shift(7, 1, 1)
            with dve.Fori(1, 7) as i:
                for s in range(2):
                    j = dve.snap(2 * i + s)
                    shift(j + 6, j, s)
            if stop <= 1:
                return

            def attend(b, s, first=False):
                k0 = P if first else 0
                n = 2 * P - k0
                for g in range(2):
                    h4 = slice(4 * g, 4 * g + 4)
                    dve.wait_ge(S("att_mm"), 2 * b + g + 1)
                    if not first:
                        dve.wait_ge(S("attT_mm"), 2 * b + g - 1)
                    for x in range(2):
                        i_ = stt(sc[:, g, 2 * x:2 * x + 2, k0:],
                                 ps[:, 2 * g + x, :].rearrange("p (m k) -> p m k", k=256)[:, :, k0:], SCALE,
                                 bias[:, 4 * g + 2 * x:4 * g + 2 * x + 2, k0:], ALU.mult, ALU.add)
                    i_.then_inc(S("att_sc"), 1)
                    dve.wait_ge(S("att_sc"), 2 * b + g + 1)
                    reduce_max(sm["mx"][:, h4], sc[:, g, :, k0:], AX_X)
                    tt(sm["mx"][:, h4], sm["mx"][:, h4], par("sinks")[:, h4], ALU.max)
                    ts(sm["nm"][:, h4], sm["mx"][:, h4], -1.0, None, ALU.mult)
                    tt(sm["es"][:, h4], par("sinks")[:, h4], sm["mx"][:, h4], ALU.subtract).then_inc(S("att_max"), 1)
                for g in range(2):
                    h4 = slice(4 * g, 4 * g + 4)
                    dve.wait_ge(S("att_exp"), 2 * b + g + 1)
                    tt(sm["rec"][:, h4], sm["den"][:, h4], sm["es"][:, h4], ALU.add)
                    reciprocal(sm["rec"][:, h4], sm["rec"][:, h4])
                    tt(sc[:, g, :, k0:], sc[:, g, :, k0:], sm["rec"][:, h4].unsqueeze(2).to_broadcast([P, 4, n]),
                       ALU.mult).then_inc(S("att_p"), 1)

            dve.wait_ge(S("bias_in"), 16)
            attend(0, 0, first=True)
            attend(1, 1)
            with dve.Fori(1, 4) as i:
                for s in range(2):
                    attend(2 * i + s, s)
            if stop <= 2:
                return

            dve.wait_ge(S("smask_in"), 16)
            dve.wait_ge(S("att_out"), 16)
            for m in range(4):
                ts(kkn[:, m, :], proj[:, 10 + m, :], par("k_k", m, 1), None, ALU.mult).then_inc(S("kk_done"), 1)
            dve.wait_ge(S("kn_sqrt"), 1)
            ts(sm["kn"], sm["kn"], 1e-12, None, ALU.max)
            reciprocal(sm["kinv"], sm["kn"]).then_inc(S("kinv"), 1)
            for m in range(4):
                dve.wait_ge(S("lora_sig"), m + 1)
                scan(cum[:, m, :], smask[:, :], ut[:, m % 2, :], 0.0, ALU.mult, ALU.add).then_inc(S("cum_done"), 1)
                ts(tt_[:, m % 2, :], kka[:, m, :], par("k_a", m, 1), sm["omka"][:, m:m + 1], ALU.mult, ALU.add)
                tt(proj[:, 10 + m, :], proj[:, 10 + m, :], tt_[:, m % 2, :], ALU.mult)
                dve.wait_ge(S("kinv_bc"), m + 1)
                tt(kkn[:, m, :], kkn[:, m, :], pair(5), ALU.mult).then_inc(S("kkn_done"), 1)
                dve.wait_ge(S("kkn_done"), m + 1)
                tt(kka[:, m, :], kka[:, m, :], kkn[:, m, :], ALU.mult)
                stt(rk[:, m, :], proj[:, 6 + m, :], par("r_k", m, 1), proj[:, 10 + m, :], ALU.mult, ALU.mult)\
                    .then_inc(S("rk_done"), 1)

            dve.wait_ge(S("rk_out"), 64)
            dve.wait_ge(S("rmask_in"), 16)
            memset(e_neg[:, :, :, 0:1], 1.0)
            memset(st[:, 0, :, :], 0.0).then_inc(S("st_upd"), 1)
            m_ar = rmask[:, 0:2 * RC].unsqueeze(1).to_broadcast([P, 4, 2 * RC])

            def rm(k):
                return rmask[:, 2 * RC + k * RC:3 * RC + k * RC].unsqueeze(1).to_broadcast([P, 4, RC])

            def prepare(c, s):
                t = bass.ds(c * RC, RC)
                dve.wait_ge(S("ch_exp"), c + 1)
                stt(ar[:, s, :, 0, :], kkn[:, :, t], -1.0, e_neg[:, s, :, 0:RC], ALU.mult, ALU.mult)
                tt(ar[:, s, :, 1, :], proj[:, 6:10, t], e_neg[:, s, :, 1:], ALU.mult)
                tt(b_ch[:, s, :, :], kka[:, :, t], e_pos[:, s, :, :], ALU.mult)
                tt(k_ch[:, s, :, :], proj[:, 10:14, t], e_pos[:, s, :, :], ALU.mult).then_inc(S("ch_prep"), 1)

            def level_part(s, l):
                tt(lvl[:, s, l, :, :], m1[:, s, :, 0:RC], rm(2 + l), ALU.mult)

            def mask_first(i, s):
                dve.wait_ge(S("ch_mm"), 2 * i + s + 1)
                tt(m1[:, s, :, :], ps[:, 4 * s, :].rearrange("p (m c) -> p m c", c=2 * RC), m_ar, ALU.mult)
                tt(xx[:, s, 0, :, :], ps[:, 4 * s + 2, 0:256].rearrange("p (m c) -> p m c", c=RC), rm(0), ALU.mult)
                tt(xx[:, s, 0, :, :], xx[:, s, 0, :, :], rm(7), ALU.add)
                tt(xx[:, s, 1, :, :], m1[:, s, :, 0:RC], rm(1), ALU.mult)
                tt(xx[:, s, 1, :, :], xx[:, s, 1, :, :], rm(7), ALU.add)
                level_part(s, 1)
                tt(lvl[:, s, 0, :, :], m1[:, s, :, 0:RC], rm(2), ALU.mult).then_inc(S("ch_masked"), 1)

            def mask_rest(s):
                for l in range(2, 5):
                    level_part(s, l)
                tt(m2[:, s, :, :], ps[:, 4 * s + 1, :].rearrange("p (m c) -> p m c", c=2 * RC), m_ar, ALU.mult)
                vcopy(b_tok[:, s, :, :], ps[:, 4 * s + 2, 256:].rearrange("p (m c) -> p m c", c=RC))

            def chunk_pair(i, last=False):
                mask_first(i, 0)
                mask_rest(0)
                mask_first(i, 1)
                for l in range(5):
                    for s in range(2):
                        dve.wait_ge(S(f"x_mm{s}"), 5 * i + l + 1)
                        lo = 0 if l < 4 else 1
                        tt(xx[:, s, lo:, :, :], xx[:, s, lo:, :, :],
                           ps[:, 4 * s, 256 * lo:].rearrange("p (x m c) -> p x m c", m=4, c=RC), ALU.add)\
                            .then_inc(S(f"x_upd{s}"), 1)
                    if l == 0:
                        mask_rest(1)
                for s in range(2):
                    c = 2 * i + s
                    dve.wait_ge(S("u_mm"), c + 1)
                    vcopy(u_sb[:, :, :], ps[:, 6, 256:].rearrange("p (m c) -> p m c", c=RC))\
                        .then_inc(S("u_cp"), 1)
                    if s and not last:
                        prepare(c + 1, 0)
                    dve.wait_ge(S("ds_mm"), c + 1)
                    tt(st[:, 1 - s, :, :], st[:, s, :, :], ps[:, 6, 0:256].rearrange("p (m c) -> p m c", c=RC),
                          ALU.add)
                    tt(st[:, 1 - s, :, :], st[:, 1 - s, :, :], e_neg[:, s, :, RC:].to_broadcast([P, 4, RC]),
                       ALU.mult).then_inc(S("st_upd"), 1)
                if not last:
                    prepare(2 * i + 3, 1)

            for s in range(2):
                prepare(s, s)
            with dve.Fori(0, 7) as i:
                chunk_pair(i)
            chunk_pair(7, last=True)

            for k in range(4):
                low(1, k, mix_src[k])
            for m in range(4):
                dve.wait_ge(S("gn_sq"), m + 1)
                vcopy(o1[:, m, :], pair(2 * (m % 2))).then_inc(S("oc_done"), 1)
            dve.wait_ge(S("gn_mm"), 4)
            ts(sm["kn"], ps[:, 4, 0:64], GN_EPS, None, ALU.add)
            reciprocal(sm["kn"], sm["kn"]).then_inc(S("gn_var"), 1)
            dve.wait_ge(S("oc_done"), 4)
            for m in range(4):
                dve.wait_ge(S("fin_mm"), m + 1)
                stt(o1[:, m, :], o1[:, m, :], par("ln_g", m, 1), pair(0), ALU.mult, ALU.mult).then_inc(S("inv_used"), 1)
                tt(oc[:, m % 2, :], pair(2), proj[:, 14 + m, :], ALU.mult).then_inc(S("bonus_used"), 1)
                stt(o1[:, m, :], o1[:, m, :], par("ln_b", m, 1), oc[:, m % 2, :], ALU.add, ALU.add)
                tt(o1[:, m, :], o1[:, m, :], pair(5), ALU.mult).then_inc(S("of_done"), 1)
                if m:
                    low(1, 3 + m, mix_src[3 + m])
            low(1, 7, mix_src[7])
            for j in range(4):
                norm_pair(1, j)
            norm_inverse(1)
            dve.wait_ge(S("x_again"), 16)
            for k in range(KT):
                stt(nrm_a[:, k % 2, :], y1[:, k, :], par("g_mix_post", k, 1), rs_of(1), ALU.mult, ALU.mult)
                tt(x1[:, k, :], x1[:, k, :], nrm_a[:, k % 2, :], ALU.add).then_inc(S("x1_done"), 1)
                if k >= 2 and k % 2 == 0:
                    norm_pair(2, k // 2 - 1)
            norm_pair(2, 3)
            apply_all(2, 2, nrm_a, lambda k: x1[:, k, :], lambda k: par("g_ffn_pre", k, 1))
            memset(f_acc[:, 0:8, :], 0.0)
            dve.sem_inc(S("prod"), 1)

            with dve.Fori(0, FFN_GROUPS) as gr:
                with dve.Fori(0, GROUP) as j:
                    p = dve.snap(GROUP * gr + j)
                    g = dve.snap(G_FFN + 3 * GROUP * gr + 2 * j)
                    for u, dst in enumerate((cg, cv)):
                        col = dve.snap(2 * p + u)
                        dve.wait_ge(S("conv_a"), 2 * p + u + 1)
                        stt(dst[:, 1:], pair(2 * u)[:, 0:T - 1], par("conv_w")[:, bass.ds(64 + col, 1)], dst[:, 1:],
                            ALU.mult, ALU.add)
                        stt(dst[:, 2:], pair(2 * u)[:, 0:T - 2], par("conv_w")[:, bass.ds(col, 1)], dst[:, 2:],
                            ALU.mult, ALU.add).then_inc(S("gemm_evac"), 1)
                    dve.wait_ge(S("gelu"), p + 1)
                    dve.wait_ge(S("gemm_evac"), g + 2)
                    tt(gv[:, :], cg[:, :], cv[:, :], ALU.mult).then_inc(S("prod"), 1)
                    dve.wait_ge(S("f_hi_done"), p + 1)
                    tt(f_lo[:, bass.ds(j, 1), :], gv[:, :].unsqueeze(1), f_hi[:, bass.ds(j, 1), :].bitcast(F32),
                       ALU.subtract).then_inc(S("f_lo_done"), 1)
                with dve.Fori(0, GROUP // 2) as j:
                    g = dve.snap(G_FFN + 3 * GROUP * gr + 2 * GROUP + 2 * j)
                    for u in range(2):
                        dve.wait_ge(S("gemm_mm"), g + u + 1)
                        f = f_acc[:, :, :].rearrange("p (k u) t -> p k u t", u=2)[:, bass.ds(j, 1), u, :]\
                            .rearrange("p o t -> p (o t)")
                        tt(f, f, pair(2 * u), ALU.add).then_inc(S("gemm_evac"), 1)
            for j in range(4):
                norm_pair(3, j)
            norm_inverse(3)
            dve.wait_ge(S("x1_back"), 16)
            for k in range(KT):
                stt(nrm_b[:, k % 2, :], f_acc[:, k, :], par("g_ffn_post", k, 1), rs_of(3), ALU.mult, ALU.mult)
                tt(x2[:, k, :], x2[:, k, :], nrm_b[:, k % 2, :], ALU.add).then_inc(S("x2_done"), 1)
                if k >= 2 and k % 2 == 0:
                    norm_pair(4, k // 2 - 1)
            norm_pair(4, 3)
            apply_all(4, 3, nrm_b, lambda k: x2[:, k, :], lambda k: sm["ada"][:, 8 + k:9 + k],
                      lambda k: sm["ada"][:, k:k + 1])
            if stop <= 4:
                return

            tt(sm["lb_d"], par("lb"), par("lb"), ALU.subtract).then_inc(S("lb_d"), 1)
            dve.wait_ge(S("lb_e"), 1)
            reciprocal(sm["lb"], sm["lb_e"])
            tt(sm["lb_e"], sm["lb"], sm["lb_e"], ALU.mult)
            tt(sm["lb"], sm["lb_e"], sm["lb_e"], ALU.subtract)
            ts(sm["omlb"], sm["lb"], -1.0, 1.0, ALU.mult, ALU.add)
            for m in range(2):
                dve.wait_ge(S("ls_ln"), m + 1)
                ts(la[:, m, :], la[:, m, :], 0.0, None, ALU.min)
                tt(la[:, m, :], la[:, m, :], ls_t[:, m, :], ALU.subtract)
                ts(la[:, m, :], la[:, m, :], 1.0 / 16.0, None, ALU.mult)
            dve.wait_ge(S("smask2_in"), 16)
            for m in range(4):
                if m < 2:
                    decay = la[:, m, :]
                else:
                    decay, src = g5[:, m % 2, :], proj2[:, 4 + m, :]
                    dve.wait_ge(S("ls_ln"), m + 1)
                    stt(decay, src, 0.0, g4[:, m % 2, :], ALU.min, ALU.subtract).then_inc(S("fb_read"), 1)
                    dve.wait_ge(S("lbt_exp"), m - 1)
                    ts(lbt[:, m % 2, :], lbt[:, m % 2, :], 1e18, None, ALU.min).then_inc(S("lbt_min"), 1)
                    dve.wait_ge(S("lbt_ln"), m - 1)
                    tt(decay, decay, lbt[:, m % 2, :], ALU.add)
                scan(c4[:, m, :], smask2[:, :], decay, 0.0, ALU.mult, ALU.add).then_inc(S("lsig"), 1)
                if m >= 2:
                    dve.wait_ge(S("kb_sig"), m - 1)
                    ts(proj2[:, 4 + m, :], proj2[:, 4 + m, :], sm["omlb"][:, m - 2:m - 1], None, ALU.mult)\
                        .then_inc(S("kb_done"), 1)

            dve.wait_ge(S("lsig"), 4)
            dve.wait_ge(S("gmask_in"), 16)
            memset(s_m[:, :, :, :], 0.0)
            memset(st2[:, :], 0.0)
            dve.sem_inc(S("st2_upd"), 1)
            dve.sem_inc(S("lev_cp"), 2)

            def update_state(b, s):
                dve.wait_ge(S("ds2_mm"), b + 2)
                dve.wait_ge(S("ecl_done"), b + 1)
                dve.wait_ge(S("o2_mm"), b + 1)
                for m in range(4):
                    w, at0 = (P, m * P) if m < 2 else (64, 256 + (m - 2) * 64)
                    i_ = stt(st2[:, at0:at0 + w], st2[:, at0:at0 + w], sm["ecl"][:, 4 * s + m:4 * s + m + 1],
                             ps[:, 7, at0:at0 + w], ALU.mult, ALU.add)
                i_.then_inc(S("st2_upd"), 1)

            def gla_block(b, s, first=False, last=False):
                def level_into_scores(l):
                    dve.wait_ge(S("lev_mm"), 8 * b + l + 3)
                    ts(sm["took_v"], sm["one"], 1.0, None, ALU.mult)
                    for x in range(2):
                        r = slice(0, reach(l))
                        out, mask = s_m[r, s, 4 * x:4 * x + 4, :], gmask[r, l:l + 1, :].bitcast(U32)
                        if l < 7:
                            w = P >> l
                            n = P // w
                            i_ = copy_pred(
                                out.rearrange("p h (n w) -> p h n w", w=w)[:, :, :, w // 2:],
                                mask.rearrange("p h (n w) -> p h n w", w=w)[:, :, :, w // 2:].to_broadcast([reach(l), 4, n, w // 2]),
                                ps[r, 2 * (l % 2) + x, 0:256].rearrange("p (h n w) -> p h n w", h=4, n=n))
                        else:
                            i_ = copy_pred(out, mask.to_broadcast([P, 4, P]),
                                           ps[:, 2 * (l % 2) + x, :].rearrange("p (h t) -> p h t", t=P))
                    i_.then_inc(S("lev_cp"), 1)

                dve.wait_ge(S("e_done"), 8 * b + 1)
                dve.wait_ge(S("ds2_mm"), b + 1)
                tt(kh[:, :, :], e_end[:, :, :], k_b[:, s, :, :], ALU.mult).then_inc(S("kh_done"), 1)
                tt(qe[:, s, :, :], qe[:, s, :, :], q_b[:, s, :, :], ALU.mult)
                for l in range(7):
                    hw = 64 >> l
                    dve.wait_ge(S("e_done"), 8 * b + l + 2)
                    dve.wait_ge(S("lev_mm"), 8 * b + l + 1)
                    z, e = blocks(zz[:, l % 2, :, :], 2 * hw), blocks(e7[:, s, l, :, :], 2 * hw)
                    tt(z[:, :, 0:hw], blocks(k_b[:, s, :, :], 2 * hw)[:, :, 0:hw], e[:, :, 0:hw], ALU.mult)
                    tt(z[:, :, hw:], blocks(q_b[:, s, :, :], 2 * hw)[:, :, hw:], e[:, :, hw:], ALU.mult)\
                        .then_inc(S("z_done"), 1)
                    if l:
                        level_into_scores(l - 1)
                    if l == 3 and not first:
                        update_state(b - 1, 1 - s)
                level_into_scores(6)
                level_into_scores(7)

            gla_block(0, 0, first=True)
            gla_block(1, 1)
            with dve.Fori(1, NB // 2 - 1) as i:
                for s in range(2):
                    gla_block(2 * i + s, s)
            gla_block(NB - 2, 0)
            gla_block(NB - 1, 1, last=True)

            dve.wait_ge(S("sbmask_in"), 16)
            steps = [(h, b) for h in range(4) for b in range(NB - 1, -1, -1)]

            def soft(n):
                h, b = steps[n]
                dve.wait_ge(S("sb_ln"), n + 1)
                if n >= 2:
                    dve.wait_ge(S("sb_r"), n - 1)
                stt(spl[:, n % 2, b * P:], pair(2 * (n % 2))[:, b * P:], 0.0, ab[:, n % 2, b * P:], ALU.max, ALU.add)
                d = spl[:, n % 2, b * P:(b + 1) * P]
                tt(d, d, sbmask[:, 2, :], ALU.mult).then_inc(S("sb_sp"), 1)

            soft(0)
            soft(1)
            for n, (h, b) in enumerate(steps):
                dve.wait_ge(S("sb_r"), n + 1)
                dve.wait_ge(S("sb_sp"), n + 1)
                if b < NB - 1:
                    tt(lacc[:, (b + 1) * P:], lacc[:, (b + 1) * P:], spl[:, n % 2, (b + 1) * P:], ALU.add)
                vcopy(lacc[:, b * P:(b + 1) * P], spl[:, n % 2, b * P:(b + 1) * P])\
                    .then_inc(S("sb_acc"), 1)
                dve.wait_ge(S("sb_w"), n + 1)
                d = wts[:, n % 2, b * P:(b + 1) * P]
                tt(d, d, sbmask[:, 2, :], ALU.mult).then_inc(S("sb_wm"), 1)
                if n + 2 < len(steps):
                    soft(n + 2)

            dve.wait_ge(S("hn_mm"), 6)
            ts(hn_v[:, :], ps[:, 0, 0:96], EPS, None, ALU.add)
            reciprocal(hn_v[:, :], hn_v[:, :]).then_inc(S("hn_var"), 1)
            dve.wait_ge(S("oc2_cp"), 4)
            for k in range(KT):
                if k < 6:
                    dve.wait_ge(S("hn_bc"), k + 1)
                    w = par("gla_w") if k < 4 else par("hgrn_w")
                    stt(o_a[k], proj2[:, k, :], w, pair(4 + 2 * (k % 2)), ALU.mult, ALU.mult)\
                        .then_inc(S("hn_out"), 1)
                    dve.wait_ge(S("hn_out"), k + 1)
                    src = o_a[k]
                else:
                    src = proj2[:, 9 + k - 6, :]
                dve.wait_ge(S(f"gate_back{k % 2}"), 16 * (k // 2 + 1))
                tt(o_a[k], src, gate_in[:, k % 2, :], ALU.mult).then_inc(S("gate_used"), 1)
                if k:
                    low(4, k - 1, o_a[k - 1])
            low(4, KT - 1, o_a[KT - 1])
            if stop <= 5:
                return

            dve.wait_ge(S("x2_back"), 16)
            for k in range(KT):
                dve.wait_ge(S("gemm_evac"), G_OUT2 + k + 1)
                stt(x3[:, k, :], y2[:, k, :], sm["ada"][:, 16 + k:17 + k], x3[:, k, :], ALU.mult, ALU.add)\
                    .then_inc(S("x3_done"), 1)
                if k % 2:
                    norm_pair(5, k // 2)
            norm_inverse(5)
            for k in range(KT):
                stt(y2[:, k, :], x3[:, k, :], par("final_w", k, 1), rs_of(5), ALU.mult, ALU.mult).then_inc(S("out_done"), 1)


def kernel(**inputs):
    import concourse.bacc as bacc
    from concourse.bass_utils import run_bass_kernel_spmd

    f = {k: np.asarray(v) for k, v in inputs.items()}

    def tiles(w):
        k, n = w.shape
        return w.reshape(KT, P, n // P, P).transpose(2, 1, 0, 3).reshape(n // P, P, KT * P)

    def cols(v):
        return v.reshape(-1, P).T

    pair_up = np.concatenate([np.arange(64) + 64 * h for m in range(4) for h in (m, m + 4)])
    w_in = f["w_in"][0]
    w_q, w_rest = w_in[:, :512][:, pair_up], w_in[:, 512:]
    w_out = np.concatenate([f["w_out"][0][:512][pair_up], f["w_out"][0][512:]], 0)
    up = tiles(f["w_ffn_up"][0])
    down = f["w_ffn_down"][0].reshape(FFN_GROUPS, GROUP * P, D)
    ffn = []
    for g in range(FFN_GROUPS):
        for j in range(GROUP):
            ffn += [up[GROUP * g + j], up[32 + GROUP * g + j]]
        ffn += list(tiles(down[g]))
    w2 = f["w_in_2"][0]
    widths = (256, 256, 512, 16, 512, 256, 256, 256, 256, 256, 256, 256, 256)
    part = dict(zip(("qa", "ka", "va", "lr", "ga", "qb", "fb", "ib", "gb", "qc", "kc", "vc", "gc"),
                    np.split(w2, np.cumsum(widths)[:-1], axis=1)))
    part["lr"] = np.concatenate([part["lr"], np.zeros((D, P - 16), np.float32)], 1)
    in2 = np.concatenate([part[n] for n in ("ga", "gb", "gc", "qa", "qb", "ka", "fb", "lr", "qc", "kc", "va", "ib", "vc")], 1)
    wall = np.concatenate([tiles(np.concatenate([w_q, w_rest], 1)), tiles(w_out), np.stack(ffn), tiles(in2),
                           tiles(f["w_out_2"][0])], 0)[:N_TILES]

    n = np.arange(P)
    half = (n[:, None] // 64 == n[None, :] // 64).astype(np.float32)
    rel = 255 - np.arange(384)
    nn = np.maximum(rel, 0)
    exact = N_BUCKETS // 2
    large = exact + (np.log(np.maximum(nn, 1).astype(np.float32) / np.float32(exact))
                     / np.float32(np.log(MAX_DISTANCE / exact)) * np.float32(N_BUCKETS - exact)).astype(np.int32)
    bucket = np.where(nn < exact, nn, np.minimum(large, N_BUCKETS - 1))
    bucket = np.where((rel >= 0) & (rel < P), bucket, N_BUCKETS)
    onehot = np.zeros((P, 384), np.float32)
    onehot[bucket, np.arange(384)] = 1
    rel_bias = np.zeros((P, 8), np.float32)
    rel_bias[:N_BUCKETS] = f["rel_bias"]
    w_gla2 = np.zeros((P, 256), np.float32)
    w_gla2[:16] = f["w_gla_gate2_2"][0]
    cw, cb = f["conv_w"][0], f["conv_b"][0]

    def gate_val(v):
        return np.stack([cols(v[:4096]), cols(v[4096:])], 2).reshape(P, 64)

    values = dict(
        g_mix_pre=cols(f["norm_mix_pre"][0]), g_mix_post=cols(f["norm_mix_post"][0]),
        g_ffn_pre=cols(f["norm_ffn_pre"][0]), g_ffn_post=cols(f["norm_ffn_post"][0]),
        shift_mix=cols(f["rwkv_shift_mix"][0]), w0=cols(f["w0"][0]), a0=cols(f["a0"][0]), k_k=cols(f["k_k"][0]),
        k_a=cols(f["k_a"][0]), r_k=cols(f["r_k"][0].reshape(-1)), ln_g=cols(f["ln_x_g"][0]), ln_b=cols(f["ln_x_b"][0]),
        conv_w=np.concatenate([gate_val(cw[j]) for j in range(3)], 1), conv_b=gate_val(cb),
        b_ada=cols(f["b_ada_2"][0]), c=cols(f["c_2"][0]), b_gla=cols(f["b_gla_gate_2"][0]),
        gla_w=f["gla_norm_w_2"][0][:, None], hgrn_w=np.tile(f["hgrn_norm_w_2"][0], 2)[:, None],
        lb=cols(f["hgrn_lb_logits_2"][0]), final_w=cols(f["final_norm_w_2"]),
        sinks=np.broadcast_to(f["sinks"][0][None, :], (P, 8)),
        ident=np.eye(P, dtype=np.float32), halves=half, center=np.eye(P, dtype=np.float32) - half / 64,
        mean_all=np.full((P, 1), 1 / D, np.float32), mean2=np.full((P, 2), 1 / P, np.float32),
        mean_half=half[:, ::64] / 64,
        w_lora=np.concatenate([f["w_decay_up"][0], f["w_iclr_up"][0]], 0), w_gate=f["w_gate_up"][0],
        w_gla2=w_gla2, onehot=onehot, rel_bias=rel_bias)
    cst = np.concatenate([values[name] for name, _ in PARAMS], 1).astype(np.float32)

    t = np.arange(RC)
    row, col = t[:, None], t[None, :]

    def level(h):
        m = np.arange(P)
        a, b = m[:, None], m[None, :]
        return (a // (2 * h) == b // (2 * h)) & (a // h % 2 == 0) & (b // h % 2 == 1)

    lv = {h: level(h) for h in (1, 2, 4, 8, 16, 32, 64)}
    rmask = np.concatenate([row < col, row <= col, lv[1][:RC, :RC].T] + [lv[h][:RC, :RC] for h in (1, 2, 4, 8, 16, 32)]
                           + [row == col], 1)
    rmask = np.tile(rmask, (2, 1)).astype(np.float32)
    gmask = np.concatenate([lv[64 >> i] for i in range(7)] + [np.eye(P, dtype=bool)], 1).astype(np.float32)
    sbmask = np.concatenate([-(n[:, None] >= n[None, :]).astype(np.float32), -np.ones((P, P), np.float32),
                             (n[:, None] < n[None, :]).astype(np.float32)], 1)
    scan = np.concatenate([np.tile((np.arange(T) % w != 0).astype(np.float32), (P, 1)) for w in (RC, P)], 1)

    arrays = dict(
        wall=wall, wada=f["w_ada_2"][0].reshape(KT, P, 3, D).transpose(0, 2, 1, 3).reshape(3 * KT, P, D), cst=cst, rmask=rmask, gmask=gmask, sbmask=sbmask, scan=scan,
        xT=f["x"][0].T.reshape(KT, P, T).transpose(1, 0, 2).reshape(P, KT * T))
    arrays = {k: np.ascontiguousarray(v) for k, v in arrays.items()}
    nc = bacc.Bacc("TRN2", target_bir_lowering=False, num_devices=1)
    dr = {k: nc.dram_tensor(k, v.shape, mybir.dt.from_np(v.dtype), kind="ExternalInput").ap() for k, v in arrays.items()}
    dr["out"] = nc.dram_tensor("out", (P, KT * T), F32, kind="ExternalOutput").ap()
    build(nc, dr)
    out = run_bass_kernel_spmd(nc, [arrays], core_ids=[0]).results[0]["out"]
    return np.ascontiguousarray(np.asarray(out).reshape(P, KT, T).transpose(2, 1, 0).reshape(1, T, D))
```
